# Optimizing a Trainium2 kernel written in Bass

```python
import jax, jax.numpy as jnp
from jax import lax
import numpy as np

D_MODEL = 1024
BATCH = 1
SEQ = 512
DEPTH = 1

HEAD_DIM = 64
RWKV_HEADS = D_MODEL // HEAD_DIM
RWKV_WIDTH = RWKV_HEADS * HEAD_DIM
DECAY_LORA = 64
AAA_LORA = 64
GATE_LORA = 160
RWKV_COLS = 3 * RWKV_WIDTH + DECAY_LORA + AAA_LORA + GATE_LORA
GN_EPS = 64e-5
ATTN_PAIRS = ((128, 1), (512, 4), (2048, 16))
ATTN_GROUPS = 3
ATTN_HEADS_PER_GROUP = 4
ATTN_HEADS = ATTN_GROUPS * ATTN_HEADS_PER_GROUP
ATTN_WIDTH = ATTN_HEADS * HEAD_DIM
N_BRANCHES = 2
IN_COLS = RWKV_COLS + 3 * ATTN_WIDTH + N_BRANCHES * D_MODEL
D_FF = 2816
RMS_EPS = 1e-6
NEG_INF = -1e30


def _split_last(t, sizes):
    out, start = [], 0
    for n in sizes:
        out.append(t[..., start:start + n])
        start += n
    return out

def rms_norm(x, g):
    xf = x.astype(jnp.float32)
    y = xf * lax.rsqrt(jnp.mean(xf * xf, axis=-1, keepdims=True) + RMS_EPS)
    return y.astype(x.dtype) * g

def swiglu(h, w_in, w_out):
    gate, up = _split_last(h @ w_in, (D_FF, D_FF))
    return (jax.nn.silu(gate) * up) @ w_out

def token_shift(p, mu):
    prev = jnp.pad(p, ((0, 0), (1, 0), (0, 0)))[:, :-1]
    return p + (prev - p) * mu

def wkv7_scan(r, w, k, v, a, b):
    B, S, H, N = r.shape
    to_time = lambda t: jnp.moveaxis(t, 1, 0)

    def step(state, inp):
        r_t, w_t, k_t, v_t, a_t, b_t = inp
        sa = jnp.einsum('bhvk,bhk->bhv', state, a_t)
        state = (state * w_t[:, :, None, :] + sa[..., None] * b_t[:, :, None, :]
                 + v_t[..., None] * k_t[:, :, None, :])
        return state, jnp.einsum('bhvk,bhk->bhv', state, r_t)

    state0 = jnp.zeros((B, H, N, N), jnp.float32)
    _, out = lax.scan(step, state0, (to_time(r), to_time(w), to_time(k),
                                      to_time(v), to_time(a), to_time(b)))
    return jnp.moveaxis(out, 0, 1)

def rwkv7_time_mix(p, mu, w0, w2, a0, a2, g2, k_k, k_a, r_k, ln_w, ln_b):
    B, S, _ = p.shape
    H, N = RWKV_HEADS, HEAD_DIM
    p = token_shift(p.astype(jnp.float32), mu)
    r, k, v, wd, ad, gd = _split_last(
        p, (RWKV_WIDTH, RWKV_WIDTH, RWKV_WIDTH, DECAY_LORA, AAA_LORA, GATE_LORA))
    w = -jax.nn.softplus(-(w0 + jnp.tanh(wd) @ w2)) - 0.5
    decay = jnp.exp(-jnp.exp(w))
    a = jax.nn.sigmoid(a0 + ad @ a2)
    g = jax.nn.sigmoid(gd) @ g2
    heads = lambda t: t.reshape(B, S, H, N)
    kk = heads(k * k_k)
    kk = kk / jnp.maximum(jnp.sqrt(jnp.sum(kk * kk, axis=-1, keepdims=True)), 1e-12)
    k = k * (1.0 + (a - 1.0) * k_a)
    rh, kh, vh, ah = heads(r), heads(k), heads(v), heads(a)
    wkv = wkv7_scan(rh, heads(decay), kh, vh, -kk, kk * ah)
    mean = jnp.mean(wkv, axis=-1, keepdims=True)
    var = jnp.mean(jnp.square(wkv - mean), axis=-1, keepdims=True)
    y = ((wkv - mean) * lax.rsqrt(var + GN_EPS)).reshape(B, S, RWKV_WIDTH) * ln_w + ln_b
    bonus = jnp.sum(rh * kh * r_k, axis=-1, keepdims=True) * vh
    return (y + bonus.reshape(B, S, RWKV_WIDTH)) * g

def dilated_group_attention(q, k, v, window, dilation):
    B, S, Hg, E = q.shape
    span = window // dilation
    blk = span
    sub = S // dilation
    nb = -(-sub // blk)
    pad = nb * blk - sub

    def to_sub(t):
        t = t.reshape(B, sub, dilation, Hg, E).transpose(0, 2, 1, 3, 4)
        t = jnp.pad(t, ((0, 0), (0, 0), (0, pad), (0, 0), (0, 0)))
        return t.reshape(B, dilation, nb, blk, Hg, E)

    def with_prev(t):
        tp = jnp.pad(t, ((0, 0), (0, 0), (1, 0), (0, 0), (0, 0), (0, 0)))
        return jnp.concatenate([tp[:, :, :-1], tp[:, :, 1:]], axis=3)

    qb = to_sub(q)
    kw, vw = with_prev(to_sub(k)), with_prev(to_sub(v))
    s = jnp.einsum('bdnqhe,bdnkhe->bdnhqk', qb, kw)
    qi = jnp.arange(blk)[:, None]
    kj = jnp.arange(2 * blk)[None, :]
    dist = qi + blk - kj
    bidx = jnp.arange(nb)[:, None, None]
    valid = (dist >= 0) & (dist <= span) & (bidx * blk + kj - blk >= 0)
    s = jnp.where(valid[None, None, :, None], s, NEG_INF)
    m = jnp.max(s, axis=-1, keepdims=True)
    pexp = jnp.exp(s - m)
    den = jnp.sum(pexp, axis=-1, keepdims=True)
    o = jnp.einsum('bdnhqk,bdnkhe->bdnqhe', pexp / den, vw)
    lse = (m + jnp.log(den))[..., 0].transpose(0, 1, 2, 4, 3)
    o = o.reshape(B, dilation, nb * blk, Hg, E)[:, :, :sub]
    o = o.transpose(0, 2, 1, 3, 4).reshape(B, S, Hg, E)
    lse = lse.reshape(B, dilation, nb * blk, Hg)[:, :, :sub]
    lse = lse.transpose(0, 2, 1, 3).reshape(B, S, Hg)
    return o, lse

def dilated_attention(pq, pk, pv, q_gain, k_gain):
    B, S, _ = pq.shape
    heads = lambda t: t.astype(jnp.float32).reshape(B, S, ATTN_HEADS, HEAD_DIM)
    q = rms_norm(heads(pq), q_gain) * (HEAD_DIM ** -0.5)
    k = rms_norm(heads(pk), k_gain)
    v = heads(pv)
    outs, lses = [], []
    for gi, (window, dilation) in enumerate(ATTN_PAIRS):
        sl = slice(gi * ATTN_HEADS_PER_GROUP, (gi + 1) * ATTN_HEADS_PER_GROUP)
        o, lse = dilated_group_attention(q[:, :, sl], k[:, :, sl], v[:, :, sl], window, dilation)
        outs.append(o)
        lses.append(lse)
    o = jnp.stack(outs, axis=2)
    alpha = jax.nn.softmax(jnp.stack(lses, axis=2), axis=2)
    return (o * alpha[..., None]).reshape(B, S, ATTN_WIDTH)

def first_inputs(seed: int = 0) -> dict:
    key = jax.random.key(seed)
    ks = jax.random.split(key, 27)
    f32 = jnp.float32
    L, D = DEPTH, D_MODEL

    def nrm(k, shape, scale):
        return scale * jax.random.normal(k, shape, f32)

    def gain(k, shape):
        return 1.0 + 0.1 * jax.random.normal(k, shape, f32)

    return {
        'x': jax.random.normal(ks[0], (BATCH, SEQ, D), f32),
        'ffn1_norm': gain(ks[1], (L, D)),
        'ffn1_w_in': nrm(ks[2], (L, D, 2 * D_FF), D ** -0.5),
        'ffn1_w_out': nrm(ks[3], (L, D_FF, D), D_FF ** -0.5),
        'mix_norm': gain(ks[4], (L, D)),
        'w_in': nrm(ks[5], (L, D, IN_COLS), D ** -0.5),
        'b_gate': nrm(ks[6], (L, N_BRANCHES * D), 0.1),
        'rwkv_mu': jax.random.uniform(ks[7], (L, RWKV_COLS), f32),
        'rwkv_w0': jax.random.uniform(ks[8], (L, RWKV_WIDTH), f32, -6.0, 0.0),
        'rwkv_w2': nrm(ks[9], (L, DECAY_LORA, RWKV_WIDTH), 0.1 * DECAY_LORA ** -0.5),
        'rwkv_a0': nrm(ks[10], (L, RWKV_WIDTH), 0.1),
        'rwkv_a2': nrm(ks[11], (L, AAA_LORA, RWKV_WIDTH), AAA_LORA ** -0.5),
        'rwkv_g2': nrm(ks[12], (L, GATE_LORA, RWKV_WIDTH), GATE_LORA ** -0.5),
        'rwkv_k_k': gain(ks[13], (L, RWKV_WIDTH)),
        'rwkv_k_a': gain(ks[14], (L, RWKV_WIDTH)),
        'rwkv_r_k': nrm(ks[15], (L, RWKV_HEADS, HEAD_DIM), 0.1),
        'rwkv_ln_w': gain(ks[16], (L, RWKV_WIDTH)),
        'rwkv_ln_b': nrm(ks[17], (L, RWKV_WIDTH), 0.01),
        'attn_q_norm': gain(ks[18], (L, HEAD_DIM)),
        'attn_k_norm': gain(ks[19], (L, HEAD_DIM)),
        'w_proj_rwkv': nrm(ks[20], (L, RWKV_WIDTH, D), RWKV_WIDTH ** -0.5),
        'w_proj_attn': nrm(ks[21], (L, ATTN_WIDTH, D), ATTN_WIDTH ** -0.5),
        'w_out': nrm(ks[22], (L, D, D), D ** -0.5),
        'ffn2_norm': gain(ks[23], (L, D)),
        'ffn2_w_in': nrm(ks[24], (L, D, 2 * D_FF), D ** -0.5),
        'ffn2_w_out': nrm(ks[25], (L, D_FF, D), D_FF ** -0.5),
    }

def first_block(x, ffn1_norm, ffn1_w_in, ffn1_w_out, mix_norm, w_in, b_gate, rwkv_mu,
              rwkv_w0, rwkv_w2, rwkv_a0, rwkv_a2, rwkv_g2, rwkv_k_k, rwkv_k_a, rwkv_r_k,
              rwkv_ln_w, rwkv_ln_b, attn_q_norm, attn_k_norm, w_proj_rwkv, w_proj_attn,
              w_out, ffn2_norm, ffn2_w_in, ffn2_w_out):
    for l in range(DEPTH):
        x = x + 0.5 * swiglu(rms_norm(x, ffn1_norm[l]), ffn1_w_in[l], ffn1_w_out[l])
        h = rms_norm(x, mix_norm[l])
        p_rwkv, p_q, p_k, p_v, p_gate = _split_last(
            h @ w_in[l], (RWKV_COLS, ATTN_WIDTH, ATTN_WIDTH, ATTN_WIDTH, N_BRANCHES * D_MODEL))
        y_a = rwkv7_time_mix(p_rwkv, rwkv_mu[l], rwkv_w0[l], rwkv_w2[l], rwkv_a0[l],
                             rwkv_a2[l], rwkv_g2[l], rwkv_k_k[l], rwkv_k_a[l], rwkv_r_k[l],
                             rwkv_ln_w[l], rwkv_ln_b[l]).astype(x.dtype)
        y_b = dilated_attention(p_q, p_k, p_v, attn_q_norm[l], attn_k_norm[l]).astype(x.dtype)
        g_a, g_b = _split_last(jax.nn.sigmoid(p_gate + b_gate[l]), (D_MODEL, D_MODEL))
        merged = g_a * (y_a @ w_proj_rwkv[l]) + g_b * (y_b @ w_proj_attn[l])
        x = x + merged @ w_out[l]
        x = x + 0.5 * swiglu(rms_norm(x, ffn2_norm[l]), ffn2_w_in[l], ffn2_w_out[l])
    return x


DEPTH_2 = 2

CTX_LEN = 256
GRID_W = 64
Q_BLOCK = 128
ROPE_THETA = 10000.0
EPS = 1e-6

MLA_HEADS = 6
MLA_Q_RANK = 256
MLA_KV_RANK = 128
MLA_NOPE = 64
MLA_ROPE = 32
MLA_V = 64
MLA_WIDTH = MLA_HEADS * MLA_V
GQA_HEADS = 6
GQA_KV_HEADS = 2
GQA_HEAD_DIM = 64
GQA_WIDTH = GQA_HEADS * GQA_HEAD_DIM
CONV_CH = 256
CONV_K = 31
MIX_WIDTH = MLA_WIDTH + GQA_WIDTH + CONV_CH

L_MLA_KV = 0
L_MLA_KR = L_MLA_KV + MLA_KV_RANK
L_GQA_K = L_MLA_KR + MLA_ROPE
L_GQA_V = L_GQA_K + GQA_KV_HEADS * GQA_HEAD_DIM
KV_COLS = L_GQA_V + GQA_KV_HEADS * GQA_HEAD_DIM
OFF_MLA_Q = 0
OFF_KV = OFF_MLA_Q + MLA_Q_RANK
OFF_GQA_Q = OFF_KV + KV_COLS
OFF_CONV = OFF_GQA_Q + GQA_WIDTH
OFF_GATE = OFF_CONV + 2 * CONV_CH
IN_COLS_2 = OFF_GATE + MIX_WIDTH


def rms_norm_2(x, g):
    xf = x.astype(jnp.float32)
    y = xf * lax.rsqrt(jnp.mean(xf * xf, axis=-1, keepdims=True) + EPS)
    return (y * g.astype(jnp.float32)).astype(x.dtype)

def layer_norm(x, g, b):
    xf = x.astype(jnp.float32)
    mu = jnp.mean(xf, axis=-1, keepdims=True)
    var = jnp.mean(jnp.square(xf - mu), axis=-1, keepdims=True)
    y = (xf - mu) * lax.rsqrt(var + EPS) * g.astype(jnp.float32) + b.astype(jnp.float32)
    return y.astype(x.dtype)

def rope_1d(x, pos):
    half = x.shape[-1] // 2
    freqs = ROPE_THETA ** (-jnp.arange(half, dtype=jnp.float32) / half)
    ang = pos.astype(jnp.float32)[:, None] * freqs[None, :]
    cos = jnp.cos(ang)[None, :, None, :]
    sin = jnp.sin(ang)[None, :, None, :]
    xf = x.astype(jnp.float32)
    x1, x2 = xf[..., :half], xf[..., half:]
    return jnp.concatenate([x1 * cos - x2 * sin, x1 * sin + x2 * cos], axis=-1).astype(x.dtype)

def axial_rope(x, row, col):
    r = x.shape[-1] // 2
    return jnp.concatenate([rope_1d(x[..., :r], row), rope_1d(x[..., r:], col)], axis=-1)

def block_attention(q, k, v):
    B, S, H, D = q.shape
    G = k.shape[2]
    R = H // G
    Dv = v.shape[-1]
    scale = D ** -0.5
    nblk = S // Q_BLOCK
    qb = q.reshape(B, nblk, Q_BLOCK, G, R, D).transpose(1, 0, 2, 3, 4, 5)

    def one_block(qi):
        s = jnp.einsum('bqgrd,bkgd->bgrqk', qi, k).astype(jnp.float32) * scale
        p = jax.nn.softmax(s, axis=-1).astype(v.dtype)
        return jnp.einsum('bgrqk,bkgv->bqgrv', p, v)

    o = lax.map(one_block, qb)
    return o.transpose(1, 0, 2, 3, 4, 5).reshape(B, S, H * Dv)

def mla_query(p, q_norm, w_uq, row, col):
    B, T = p.shape[:2]
    cq = rms_norm_2(p[..., OFF_MLA_Q:OFF_MLA_Q + MLA_Q_RANK], q_norm)
    q = (cq @ w_uq).reshape(B, T, MLA_HEADS, MLA_NOPE + MLA_ROPE)
    if row is not None:
        q = jnp.concatenate([q[..., :MLA_NOPE], axial_rope(q[..., MLA_NOPE:], row, col)], axis=-1)
    return q

def mla_keys_values(pkv, kv_norm, w_ukv, row, col):
    B, T = pkv.shape[:2]
    ckv = rms_norm_2(pkv[..., L_MLA_KV:L_MLA_KR], kv_norm)
    kv = (ckv @ w_ukv).reshape(B, T, MLA_HEADS, MLA_NOPE + MLA_V)
    k_nope, v = kv[..., :MLA_NOPE], kv[..., MLA_NOPE:]
    k_rope = pkv[..., L_MLA_KR:L_GQA_K][:, :, None, :]
    if row is not None:
        k_rope = axial_rope(k_rope, row, col)
    k_rope = jnp.broadcast_to(k_rope, (B, T, MLA_HEADS, MLA_ROPE))
    return jnp.concatenate([k_nope, k_rope], axis=-1), v

def gqa_query(p, q_norm, row, col):
    B, T = p.shape[:2]
    q = rms_norm_2(p[..., OFF_GQA_Q:OFF_CONV].reshape(B, T, GQA_HEADS, GQA_HEAD_DIM), q_norm)
    if row is not None:
        q = axial_rope(q, row, col)
    return q

def gqa_keys_values(pkv, k_norm, row, col):
    B, T = pkv.shape[:2]
    k = rms_norm_2(pkv[..., L_GQA_K:L_GQA_V].reshape(B, T, GQA_KV_HEADS, GQA_HEAD_DIM), k_norm)
    if row is not None:
        k = axial_rope(k, row, col)
    v = pkv[..., L_GQA_V:KV_COLS].reshape(B, T, GQA_KV_HEADS, GQA_HEAD_DIM)
    return k, v

def conformer_conv(u, dw_w, dw_b, ln_w, ln_b, pw_w, pw_b):
    a, g = jnp.split(u, 2, axis=-1)
    y = a * jax.nn.sigmoid(g)
    y = lax.conv_general_dilated(
        y, dw_w[:, None, :], window_strides=(1,),
        padding=((CONV_K // 2, CONV_K // 2),),
        dimension_numbers=('NWC', 'WIO', 'NWC'),
        feature_group_count=CONV_CH) + dw_b
    y = jax.nn.silu(layer_norm(y, ln_w, ln_b))
    return y @ pw_w + pw_b

def hybrid_layer(x, ctx, c, c_ctx, row, col, last,
                 norm_w, w_mod, b_mod, w_in, mla_q_norm, mla_w_uq, mla_kv_norm, mla_w_ukv,
                 gqa_q_norm, gqa_k_norm, conv_dw_w, conv_dw_b, conv_ln_w, conv_ln_b,
                 conv_pw_w, conv_pw_b, w_out):
    shift, scale, gate = jnp.split(jax.nn.silu(c) @ w_mod + b_mod, 3, axis=-1)
    shift_c, scale_c, gate_c = jnp.split(jax.nn.silu(c_ctx) @ w_mod + b_mod, 3, axis=-1)
    h = rms_norm_2(x, norm_w) * (1.0 + scale[:, None, :]) + shift[:, None, :]
    hc = rms_norm_2(ctx, norm_w) * (1.0 + scale_c) + shift_c

    p = h @ w_in
    if last:
        pc_kv = hc @ w_in[:, OFF_KV:OFF_GQA_Q]
    else:
        pc = hc @ w_in
        pc_kv = pc[..., OFF_KV:OFF_GQA_Q]
    p_kv = p[..., OFF_KV:OFF_GQA_Q]

    k_mla_c, v_mla_c = mla_keys_values(pc_kv, mla_kv_norm, mla_w_ukv, None, None)
    k_gqa_c, v_gqa_c = gqa_keys_values(pc_kv, gqa_k_norm, None, None)

    k_mla, v_mla = mla_keys_values(p_kv, mla_kv_norm, mla_w_ukv, row, col)
    q_mla = mla_query(p, mla_q_norm, mla_w_uq, row, col)
    o_mla = block_attention(q_mla, jnp.concatenate([k_mla, k_mla_c], axis=1),
                            jnp.concatenate([v_mla, v_mla_c], axis=1))
    k_gqa, v_gqa = gqa_keys_values(p_kv, gqa_k_norm, row, col)
    q_gqa = gqa_query(p, gqa_q_norm, row, col)
    o_gqa = block_attention(q_gqa, jnp.concatenate([k_gqa, k_gqa_c], axis=1),
                            jnp.concatenate([v_gqa, v_gqa_c], axis=1))
    o_conv = conformer_conv(p[..., OFF_CONV:OFF_GATE], conv_dw_w, conv_dw_b,
                            conv_ln_w, conv_ln_b, conv_pw_w, conv_pw_b)
    y = jnp.concatenate([o_mla, o_gqa, o_conv], axis=-1) * jax.nn.silu(p[..., OFF_GATE:])
    x_new = x + gate[:, None, :] * (y @ w_out)

    if last:
        return x_new, ctx

    oc_mla = block_attention(mla_query(pc, mla_q_norm, mla_w_uq, None, None), k_mla_c, v_mla_c)
    oc_gqa = block_attention(gqa_query(pc, gqa_q_norm, None, None), k_gqa_c, v_gqa_c)
    oc_conv = conformer_conv(pc[..., OFF_CONV:OFF_GATE], conv_dw_w, conv_dw_b,
                             conv_ln_w, conv_ln_b, conv_pw_w, conv_pw_b)
    yc = jnp.concatenate([oc_mla, oc_gqa, oc_conv], axis=-1) * jax.nn.silu(pc[..., OFF_GATE:])
    ctx_new = ctx + gate_c * (yc @ w_out)
    return x_new, ctx_new

def second_inputs(seed: int = 0) -> dict:
    key = jax.random.key(seed)
    ks = jax.random.split(key, 24)
    f32 = jnp.float32
    nrm = lambda k, shape, s: jax.random.normal(k, shape, f32) * s
    L, D = DEPTH_2, D_MODEL
    return {
        'x': nrm(ks[0], (BATCH, SEQ, D), 1.0),
        'c': nrm(ks[1], (BATCH, D), 1.0),
        'ctx': nrm(ks[2], (BATCH, CTX_LEN, D), 1.0),
        'c_ctx': nrm(ks[3], (D,), 1.0),
        'norm_w': 1.0 + nrm(ks[4], (L, D), 0.05),
        'w_mod': nrm(ks[5], (L, D, 3 * D), 0.5 * D ** -0.5),
        'b_mod': nrm(ks[6], (L, 3 * D), 0.02),
        'w_in': nrm(ks[7], (L, D, IN_COLS_2), D ** -0.5),
        'mla_q_norm': 1.0 + nrm(ks[8], (L, MLA_Q_RANK), 0.05),
        'mla_w_uq': nrm(ks[9], (L, MLA_Q_RANK, MLA_HEADS * (MLA_NOPE + MLA_ROPE)), MLA_Q_RANK ** -0.5),
        'mla_kv_norm': 1.0 + nrm(ks[10], (L, MLA_KV_RANK), 0.05),
        'mla_w_ukv': nrm(ks[11], (L, MLA_KV_RANK, MLA_HEADS * (MLA_NOPE + MLA_V)), MLA_KV_RANK ** -0.5),
        'gqa_q_norm': 1.0 + nrm(ks[12], (L, GQA_HEAD_DIM), 0.05),
        'gqa_k_norm': 1.0 + nrm(ks[13], (L, GQA_HEAD_DIM), 0.05),
        'conv_dw_w': nrm(ks[14], (L, CONV_K, CONV_CH), CONV_K ** -0.5),
        'conv_dw_b': nrm(ks[15], (L, CONV_CH), 0.02),
        'conv_ln_w': 1.0 + nrm(ks[16], (L, CONV_CH), 0.05),
        'conv_ln_b': nrm(ks[17], (L, CONV_CH), 0.02),
        'conv_pw_w': nrm(ks[18], (L, CONV_CH, CONV_CH), CONV_CH ** -0.5),
        'conv_pw_b': nrm(ks[19], (L, CONV_CH), 0.02),
        'w_out': nrm(ks[20], (L, MIX_WIDTH, D), MIX_WIDTH ** -0.5),
        'final_norm_w': 1.0 + nrm(ks[21], (D,), 0.05),
    }

def second_block(x, c, ctx, c_ctx, norm_w, w_mod, b_mod, w_in, mla_q_norm, mla_w_uq, mla_kv_norm,
              mla_w_ukv, gqa_q_norm, gqa_k_norm, conv_dw_w, conv_dw_b, conv_ln_w, conv_ln_b,
              conv_pw_w, conv_pw_b, w_out, final_norm_w):
    S = x.shape[1]
    rows = S // GRID_W
    row = jnp.repeat(jnp.arange(rows, dtype=jnp.int32), GRID_W)
    col = jnp.tile(jnp.arange(GRID_W, dtype=jnp.int32), rows)
    for l in range(DEPTH_2):
        x, ctx = hybrid_layer(
            x, ctx, c, c_ctx, row, col, l == DEPTH_2 - 1,
            norm_w[l], w_mod[l], b_mod[l], w_in[l], mla_q_norm[l], mla_w_uq[l],
            mla_kv_norm[l], mla_w_ukv[l], gqa_q_norm[l], gqa_k_norm[l],
            conv_dw_w[l], conv_dw_b[l], conv_ln_w[l], conv_ln_b[l],
            conv_pw_w[l], conv_pw_b[l], w_out[l])
    return rms_norm_2(x, final_norm_w)


def setup_inputs(seed=0):
    out = dict(first_inputs(seed))
    for name, value in second_inputs(seed + 1).items():
        if name != "x":
            out[name + "_2"] = value
    return out


def reference(
    x, ffn1_norm, ffn1_w_in, ffn1_w_out, mix_norm, w_in, b_gate, rwkv_mu, rwkv_w0, rwkv_w2,
    rwkv_a0, rwkv_a2, rwkv_g2, rwkv_k_k, rwkv_k_a, rwkv_r_k, rwkv_ln_w, rwkv_ln_b, attn_q_norm,
    attn_k_norm, w_proj_rwkv, w_proj_attn, w_out, ffn2_norm, ffn2_w_in, ffn2_w_out, c_2, ctx_2,
    c_ctx_2, norm_w_2, w_mod_2, b_mod_2, w_in_2, mla_q_norm_2, mla_w_uq_2, mla_kv_norm_2,
    mla_w_ukv_2, gqa_q_norm_2, gqa_k_norm_2, conv_dw_w_2, conv_dw_b_2, conv_ln_w_2, conv_ln_b_2,
    conv_pw_w_2, conv_pw_b_2, w_out_2, final_norm_w_2,
):
    x = first_block(
        x, ffn1_norm, ffn1_w_in, ffn1_w_out, mix_norm, w_in, b_gate, rwkv_mu, rwkv_w0, rwkv_w2,
        rwkv_a0, rwkv_a2, rwkv_g2, rwkv_k_k, rwkv_k_a, rwkv_r_k, rwkv_ln_w, rwkv_ln_b,
        attn_q_norm, attn_k_norm, w_proj_rwkv, w_proj_attn, w_out, ffn2_norm, ffn2_w_in,
        ffn2_w_out,
    )
    return second_block(
        x, c_2, ctx_2, c_ctx_2, norm_w_2, w_mod_2, b_mod_2, w_in_2, mla_q_norm_2, mla_w_uq_2,
        mla_kv_norm_2, mla_w_ukv_2, gqa_q_norm_2, gqa_k_norm_2, conv_dw_w_2, conv_dw_b_2,
        conv_ln_w_2, conv_ln_b_2, conv_pw_w_2, conv_pw_b_2, w_out_2, final_norm_w_2,
    )


_drawn_inputs = setup_inputs


def setup_inputs(seed=0):
    import zlib

    import numpy as np

    out = dict(_drawn_inputs(seed))
    spreads = {}
    factors = {'b_gate': 4.732,
     'rwkv_w2': 8.0,
     'rwkv_a0': 5.392,
     'rwkv_ln_b': 8.0,
     'attn_q_norm': 8.0,
     'attn_k_norm': 8.0,
     'ctx_2': 7.542,
     'c_ctx_2': 2.899,
     'norm_w_2': 8.0,
     'b_mod_2': 6.935,
     'mla_q_norm_2': 8.0,
     'mla_w_uq_2': 3.855,
     'mla_kv_norm_2': 8.0,
     'gqa_q_norm_2': 8.0,
     'gqa_k_norm_2': 8.0,
     'conv_dw_b_2': 8.0,
     'conv_ln_w_2': 8.0,
     'conv_ln_b_2': 8.0,
     'conv_pw_b_2': 8.0}
    for name, (base, spread) in spreads.items():
        noise = np.random.default_rng([zlib.crc32(name.encode()), seed]).standard_normal(out[name].shape)
        drawn = base * np.exp(spread * noise) if base else spread * noise
        out[name] = __import__('jax').numpy.asarray(drawn.astype(out[name].dtype))
    for name, factor in factors.items():
        out[name] = (out[name] * factor).astype(out[name].dtype)
    return out
```

```python
from contextlib import ExitStack

import numpy as np

import concourse.bass as bass
from concourse import mybir

F32 = mybir.dt.float32
F32R = mybir.dt.float32r
I32 = mybir.dt.int32
ACT = mybir.ActivationFunctionType
ALU = mybir.AluOpType
AX = mybir.AxisListType.X

P = 128
D = 1024
T = 512
TC = 256
TT = T + TC
KT = D // P
HD = 64
D_FF = 2816
FT = D_FF // P
UNITS = 8
RMS_EPS = 1e-6
GN_EPS = 64e-5
NEG_INF = -1e30

RW_HEADS = D // HD
PAIRS = RW_HEADS // 2
W_LORA, A_LORA, G_LORA = 64, 64, 160
RW_COLS = 3 * D + W_LORA + A_LORA + G_LORA
CHUNK = 64
CHUNKS = T // CHUNK
LEVELS = 6
DECAY = float(np.exp(-0.5))

AT_TILES = 6
AT_WIDTH = AT_TILES * P
BLOCKS = T // P

LAYERS = 2
GRID_W = 64
ROPE_THETA = 10000.0
MLA_HEADS, MLA_NOPE, MLA_ROPE, MLA_V = 6, 64, 32, 64
MLA_Q_RANK, MLA_KV_RANK = 256, 128
GQA_HEADS, GQA_KV = 6, 2
CONV_CH, CONV_K = 256, 31
HALO = CONV_K // 2
Y_TILES = 8
KB = TT // P

MOD_TILES = 3 * D // P
MOD_PER_PAIR = MOD_TILES // PAIRS
FFN_IN_BLOCKS = 2 * FT
FFN_OUT_PER_TILE = -(-FT // UNITS)
FFN_OUT_BLOCKS = KT * FFN_OUT_PER_TILE
FFN_OUT_LOOPS = KT // 2
MOD_PER_OUT = MOD_TILES // FFN_OUT_LOOPS
LORA_BLOCKS = 3
PAIR_BLOCKS = 3 + MOD_PER_PAIR
ATT_BLOCKS = 3 * AT_TILES
MERGE_BLOCKS = 4 * KT
OUT_BLOCKS = KT
WIN2 = ["mq0", "mq1", "mkv", "kr", "gk", "gv", "gq0", "gq1", "gq2", "ca0", "cg0", "ca1", "cg1"]
GATE2_BLOCKS = Y_TILES
UQ0, KN0, V0 = 0, 2 * MLA_HEADS, 3 * MLA_HEADS
PW0 = -(-(V0 + 3) // UNITS) * UNITS
SMALL2_BLOCKS = PW0 // UNITS + 1


def columns():
    out, at = {}, 0
    def put(name, n):
        nonlocal at
        out[name] = at
        at += n
    for name, n in (("ffn1_norm", KT), ("mix_norm", KT), ("ffn2_norm", KT), ("b_gate", 2 * KT), ("mu_lora", 3),
                    ("mu_rkv", 3 * PAIRS), ("w0", KT), ("a0", KT), ("k_k", KT), ("k_a", KT), ("r_k", KT), ("ln_w", KT),
                    ("ln_b", KT), ("q_norm", 1), ("k_norm", 1), ("final_norm", KT), ("cond", 2 * KT)):
        put(name, n)
    for l in range(LAYERS):
        for name, n in (("norm", KT), ("b_mod", MOD_TILES), ("mla_q", 2), ("mla_kv", 1), ("gqa_q", 1), ("gqa_k", 1),
                        ("dw_w", 2 * CONV_K), ("dw_b", 2), ("cln_w", 2), ("cln_b", 2), ("pw_b", 2)):
            put(f"{name}{l}", n)
    out["total"] = at
    return out


COL = columns()


def rope_tables(dim):
    r = dim // 2
    half = r // 2
    freqs = (np.float32(ROPE_THETA) ** (-np.arange(half, dtype=np.float32) / np.float32(half))).astype(np.float32)
    t = np.arange(T)
    cos, sin, partner = np.zeros((dim, T), np.float32), np.zeros((dim, T), np.float32), np.zeros(dim, int)
    for d in range(dim):
        pos = (t // GRID_W if d < r else t % GRID_W).astype(np.float32)
        ang = pos * freqs[d % half]
        first = d % r < half
        cos[d] = np.cos(ang)
        sin[d] = np.sin(ang) * (-1 if first else 1)
        partner[d] = d + half if first else d - half
    return cos, sin, partner


def constant_arrays():
    p = np.arange(P)[:, None]
    f = np.arange(P)[None, :]
    eye = np.eye(P, dtype=np.float32)
    ones = np.ones((P, P), np.float32)
    heads = (p // HD == f // HD).astype(np.float32)
    s = p % HD
    c = np.arange(CHUNK)[None, :]
    before = (s < c).astype(np.float32)
    upto = (s <= c).astype(np.float32)
    after = (s > c).astype(np.float32)
    eye2 = (s == c).astype(np.float32)
    square = np.concatenate([eye, ones, heads, before, upto, after, eye2], 1)
    lower, upper = [], []
    for l in range(LEVELS):
        w = 1 << l
        low = (s // (2 * w) == c // (2 * w)) & (s % (2 * w) >= w) & (c % (2 * w) < w)
        up = (s // (2 * w) == c // (2 * w)) & (s % (2 * w) < w) & (c % (2 * w) >= w)
        lower.append(low)
        upper.append(up)
    levels = np.concatenate(lower + upper, 1).astype(np.int32)
    scan = np.ones((P, T), np.float32)
    scan[:, ::CHUNK] = 0
    cur = np.where(f <= p, 0, NEG_INF)
    prev = np.where(f >= p, 0, NEG_INF)
    dil = np.where((f <= p) & (f // 32 == p // 32), 0, NEG_INF)
    masks = np.concatenate([prev, cur, dil], 1).astype(np.float32)
    first = np.concatenate([square[:, 3 * P:], scan, masks], 1)
    cos, sin, partner = rope_tables(MLA_ROPE)
    mla = np.ones((P, TT), np.float32)
    mla[MLA_NOPE:MLA_NOPE + MLA_ROPE, :T] = cos
    mla[MLA_NOPE + MLA_ROPE:, :T] = sin
    mla[MLA_NOPE + MLA_ROPE:, T:] = 0
    kr = np.concatenate([sin, sin, cos, cos], 0)
    cos, sin, partner = rope_tables(HD)
    swap = np.zeros((P, P), np.float32)
    for h in range(2):
        for d in range(HD):
            swap[h * HD + partner[d], h * HD + d] = 1
    second = np.concatenate([mla, kr, np.concatenate([cos, cos], 0), swap, np.concatenate([sin, sin], 0)], 1)
    return square[:, :3 * P], first, levels, second


FC = {"before": 0, "after": 2 * CHUNK, "eye2": 3 * CHUNK, "scan": 4 * CHUNK, "masks": 4 * CHUNK + T,
      "total": 4 * CHUNK + T + 3 * P}
SC = {"mla": 0, "kr": TT, "cos": TT + T, "swap": TT + 2 * T, "total": TT + 2 * T + P}


class Counter:
    def __init__(self, sem):
        self.sem, self.total = sem, 0


class Steps:
    def __init__(self, counter, names, times=1):
        self.sem, self.base, self.names, self.times, self.next = counter.sem, counter.total, list(names), times, 0
        self.index = {n: k for k, n in enumerate(self.names)}
        assert len(self.index) == len(self.names)
        counter.total += len(self.names) * times

    def at(self, name, i=0):
        return self.sem, self.base + self.index[name] + 1 + i * len(self.names)

    def before(self, name, i):
        assert self.base + self.index[name] + 1 > len(self.names), "a wait below one"
        return self.sem, self.base + self.index[name] + 1 - len(self.names) + i * len(self.names)

    def last(self):
        return self.sem, self.base + len(self.names) * self.times

    def inc(self, name):
        assert self.names[self.next % len(self.names)] == name, (self.names[self.next % len(self.names)], name)
        self.next += 1
        return self.sem, 1


class Stage:
    def __init__(self, k, blocks, pe=(), act=(), dve=(), times=1):
        self.k, self.b0, self.times = k, k.blocks, times
        self.entry = {"pe": (k.pe.sem, k.pe.total), "act": (k.act.sem, k.act.total), "dve": (k.dve.sem, k.dve.total)}
        self.pe, self.act, self.dve = Steps(k.pe, pe, times), Steps(k.act, act, times), Steps(k.dve, dve, times)
        k.blocks += blocks * times

    def enter(self, eng, mine):
        for name, (sem, count) in self.entry.items():
            if count:
                eng.wait_ge(sem, count)
        if mine != "pe" and self.b0:
            eng.wait_ge(self.k.blocks_used, self.b0)


def block_kernel(nc, xT, ctxT, vec, square, first, levels, trig, lora, wstream, outT):
    nblocks = wstream.shape[0]
    with ExitStack() as ctx:
        sem = lambda name: ctx.enter_context(nc.semaphore(name))

        class K:
            pe, act, dve = Counter(sem("tensor_steps")), Counter(sem("scalar_steps")), Counter(sem("vector_steps"))
            blocks_used = sem("blocks_used")
            blocks = 0
        k = K()
        raw_full = [sem("raw_full0"), sem("raw_full1")]
        rounded = sem("rounded")
        split = sem("split")
        x_in = [sem(f"x_in{i}") for i in range(2)]
        const_in, first_in, levels_in, lora_in, vec_in, ctx_in, trig_in, sin_in, out_done = (
            sem(n) for n in ("const_in", "first_in", "levels_in", "lora_in", "vec_in", "ctx_in", "trig_in", "sin_in", "out_done"))
        tensor_ready, vector_ready = sem("tensor_ready"), sem("vector_ready")
        filled = sem("filled")

        at = [-(-nc.sbuf_base // 64) * 64]
        def fixed(name, shape, dt=F32):
            t = nc.alloc_sbuf_tensor_at(name, shape, dt, offset=at[0])
            at[0] += -(-int(np.prod(shape[1:])) * 4 // 32) * 32
            return t
        X = fixed("X", [P, KT, T])
        RAW = fixed("RAW", [P, 2, UNITS * P])
        WHI = fixed("WHI", [P, 2, UNITS * P], F32R)
        WLO = fixed("WLO", [P, 2, UNITS * P], F32R)
        VEC = fixed("VEC", [P, COL["total"]])
        SQC = fixed("SQC", [P, 3 * P])
        shared_at = at[0]
        FCC = fixed("FCC", [P, FC["total"]])
        LVL = fixed("LVL", [P, 2 * LEVELS, CHUNK], I32)
        at[0] = max(at[0], shared_at + 4 * SC["total"])
        TRIG = nc.alloc_sbuf_tensor_at("TRIG", [P, SC["total"]], F32, offset=shared_at)
        EPS = fixed("EPS", [P, 2])
        CHI = fixed("CHI", [P, KT, 2], F32R)
        CLO = fixed("CLO", [P, KT, 2], F32R)
        CS = fixed("CS", [P, KT, 2])
        MOD = fixed("MOD", [P, LAYERS * MOD_TILES, 2])
        MG = fixed("MG", [P, KT, 2])
        MX2, NM2, DEN2 = (fixed(n, [P, 4 * KB]) for n in ("MX2", "NM2", "DEN2"))
        at[0] = -(-at[0] // 64) * 64
        arena0 = at[0]
        arena = nc.sbuf_usable_end - arena0
        def place(name, shape, offset, dt=F32):
            size = int(np.prod(shape[1:])) * 4
            assert offset + size <= arena, (name, offset + size, arena)
            return nc.alloc_sbuf_tensor_at(name, shape, dt, offset=arena0 + offset)
        class Area:
            def __init__(self, at):
                self.at = at
            def __call__(self, name, shape, dt=F32):
                t = place(name, shape, self.at, dt)
                self.at += -(-int(np.prod(shape[1:])) * 4 // 32) * 32
                return t
        psum = [ctx.enter_context(nc.psum_tensor(f"psum{i}", [P, 2, 512], F32)) for i in range(4)]
        bank = [psum[i // 2][:, i % 2, :] for i in range(8)]
        two_banks = [psum[i][:, :, :].rearrange("p a n -> p (a n)") for i in range(4)]
        col = lambda name, i=0, rows=slice(0, P): VEC[rows, bass.ds(COL[name] + i, 1)]
        eye, ones, heads = SQC[:, 0:P], SQC[:, P:2 * P], SQC[:, 2 * P:3 * P]

        def round_block(act, q, i=0, nb=0):
            act.wait_ge(raw_full[q % 2], 16 * (q // 2 + 1) + i * (8 * nb))
            if q >= 2:
                act.wait_ge(k.blocks_used, q - 1 + i * nb)
            act.activation(WHI[:, q % 2, :], RAW[:, q % 2, :], ACT.Copy).then_inc(rounded, 1)

        def tile_of(t, slot, u, m=P):
            return t[:, slot, u * P:u * P + m]

        def product(pe, out, slot, units, hi, lo, last):
            mm = None
            for n, (u, kt) in enumerate(units):
                first, end = n == 0, n == len(units) - 1
                pe.matmul(out, tile_of(WHI, slot, u), hi(kt), start=first and last[0], stop=False)
                pe.matmul(out, tile_of(WHI, slot, u), lo(kt), start=False, stop=False)
                mm = pe.matmul(out, tile_of(WLO, slot, u), hi(kt), start=False, stop=end and last[1])
            return mm
        WHOLE = (True, True)

        def block_ready(pe, q, i=0, nb=0):
            pe.wait_ge(split, q + 1 + i * nb)

        def block_out(eng, q, i=0, nb=0):
            eng.wait_ge(k.blocks_used, q + 1 + i * nb)

        class Norm:
            def __init__(self, scratch, *groups):
                self.groups = groups
                self.sq4, self.hf, self.std, self.rstd = scratch
                pe, act, dve = [], [], []
                for g, (*_, shift) in enumerate(groups):
                    scaled = lambda t: [f"h{g}_{t}"] + ([f"s{g}_{t}"] if shift else [])
                    pe += [f"sum{g}_{t}" for t in range(KT)]
                    act += [f"sq{g}_{t}" for t in range(KT)] + [f"std{g}"] + [f"hi{g}_{t}" for t in range(KT)]
                    dve += [f"rstd{g}"] + scaled(0) + scaled(1)
                    for t in range(KT):
                        dve += [f"lo{g}_{t}"] + (scaled(t + 2) if t + 2 < KT else [])
                self.st = Stage(k, 0, pe, act, dve)

        def norm_tensor(pe, nm):
            st = nm.st
            st.enter(pe, "pe")
            for g, (x, n, *_) in enumerate(nm.groups):
                if g:
                    pe.wait_ge(*st.act.at(f"std{g - 1}"))
                for t in range(KT):
                    pe.wait_ge(*st.act.at(f"sq{g}_{t}"))
                    pe.matmul(bank[7][:, 0:n], ones, nm.sq4[:, t % 4, 0:n], start=t == 0, stop=t == KT - 1)\
                      .then_inc(*st.pe.inc(f"sum{g}_{t}"))

        def norm_scalar(act, nm):
            st = nm.st
            st.enter(act, "act")
            for g, (x, n, hi, lo, gain, shift) in enumerate(nm.groups):
                for t in range(KT):
                    if t >= 4:
                        act.wait_ge(*st.pe.at(f"sum{g}_{t - 4}"))
                    elif g:
                        act.wait_ge(*st.pe.at(f"sum{g - 1}_{t + 4}"))
                    act.activation(nm.sq4[:, t % 4, 0:n], x(t), ACT.Square).then_inc(*st.act.inc(f"sq{g}_{t}"))
                act.wait_ge(*st.pe.at(f"sum{g}_{KT - 1}"))
                if g:
                    act.wait_ge(*st.dve.at(f"rstd{g - 1}"))
                act.activation(nm.std[:, 0:n], bank[7][:, 0:n], ACT.Sqrt, scale=1.0 / D, bias=EPS[:, 0:1])\
                   .then_inc(*st.act.inc(f"std{g}"))
                for t in range(KT):
                    act.wait_ge(*st.dve.at(f"s{g}_{t}" if shift else f"h{g}_{t}"))
                    act.activation(hi(t), nm.hf[:, t % 4, 0:n], ACT.Copy).then_inc(*st.act.inc(f"hi{g}_{t}"))

        def norm_vector(dve, nm):
            st = nm.st
            st.enter(dve, "dve")
            for g, (x, n, hi, lo, gain, shift) in enumerate(nm.groups):
                dve.wait_ge(*st.act.at(f"std{g}"))
                dve.reciprocal(nm.rstd[:, 0:n], nm.std[:, 0:n]).then_inc(*st.dve.inc(f"rstd{g}"))
                dve.wait_ge(*st.dve.at(f"rstd{g}"))

                def scaled(t):
                    slot = nm.hf[:, t % 4, 0:n]
                    if t >= 4:
                        dve.wait_ge(*st.dve.at(f"lo{g}_{t - 4}"))
                    elif g:
                        dve.wait_ge(*st.dve.at(f"lo{g - 1}_{t + 4}"))
                    dve.scalar_tensor_tensor(out=slot, in0=x(t), scalar=gain(t), in1=nm.rstd[:, 0:n], op0=ALU.mult,
                                             op1=ALU.mult).then_inc(*st.dve.inc(f"h{g}_{t}"))
                    if shift:
                        dve.wait_ge(*st.dve.at(f"h{g}_{t}"))
                        dve.tensor_scalar(slot, slot, shift(t), None, ALU.add).then_inc(*st.dve.inc(f"s{g}_{t}"))
                scaled(0)
                scaled(1)
                for t in range(KT):
                    dve.wait_ge(*st.act.at(f"hi{g}_{t}"))
                    dve.tensor_tensor(lo(t), nm.hf[:, t % 4, 0:n], hi(t).bitcast(F32), ALU.subtract)\
                       .then_inc(*st.dve.inc(f"lo{g}_{t}"))
                    if t + 2 < KT:
                        scaled(t + 2)

        def plain_norm(gain):
            return Norm((SQ4, HF, STD, RSTD), (lambda t: X[:, t, :], T, lambda t: HHI[:, t, :], lambda t: HLO[:, t, :], lambda t: col(gain, t), None))

        class FFN:
            def __init__(self, norm_col, mod):
                self.norm = plain_norm(norm_col)
                self.up = Stage(k, 4, (), ("silu0", "hi0", "silu1", "hi1"), ("mul0", "lo0", "mul1", "lo1"), FT // 2)
                self.mod = mod
                self.nb = 2 * FFN_OUT_PER_TILE + (MOD_PER_OUT if mod is not None else 0)
                self.down = Stage(k, self.nb, (), (), ("x0",) + (("mods0",) if mod is not None else ()) + ("x1",)
                                  + (("mods1",) if mod is not None else ()), FFN_OUT_LOOPS)

        fa = Area(0)
        HHI, HLO = fa("HHI", [P, KT, T], F32R), fa("HLO", [P, KT, T], F32R)
        after_h = fa.at
        GHI, GLO = fa("GHI", [P, FT, T], F32R), fa("GLO", [P, FT, T], F32R)
        SILU, GF = fa("SILU", [P, 2, T]), fa("GF", [P, 2, T])
        upper = fa.at
        na = Area(after_h)
        SQ4, HF, STD, RSTD = na("SQ4", [P, 4, T]), na("HF", [P, 4, T]), na("STD", [P, T]), na("RSTD", [P, T])

        def mod_tile(pe, slot, out):
            return product(pe, out, slot, [(u, u) for u in range(KT)], lambda t: CHI[:, t, :], lambda t: CLO[:, t, :], WHOLE)

        def ffn_tensor(pe, f):
            norm_tensor(pe, f.norm)
            st = f.up
            st.enter(pe, "pe")
            with pe.Fori(0, FT // 2) as i:
                for q in range(4):
                    if q % 2 == 0:
                        pe.wait_ge(*st.act.before(f"silu{q // 2}", i))
                    else:
                        pe.wait_ge(*st.dve.before(f"mul{q // 2}", i))
                    block_ready(pe, st.b0 + q, i, 4)
                    product(pe, bank[q], (st.b0 + q) % 2, [(u, u) for u in range(KT)], lambda t: HHI[:, t, :],
                            lambda t: HLO[:, t, :], WHOLE).then_inc(k.blocks_used, 1)
            st = f.down
            st.enter(pe, "pe")
            with pe.Fori(0, FFN_OUT_LOOPS) as i:
                q = 0
                for n in range(2):
                    pe.wait_ge(*st.dve.before(f"x{n}", i))
                    for m in range(FFN_OUT_PER_TILE):
                        units = [(u, UNITS * m + u) for u in range(UNITS) if UNITS * m + u < FT]
                        block_ready(pe, st.b0 + q, i, f.nb)
                        product(pe, bank[4 + n], (st.b0 + q) % 2, units, lambda t: GHI[:, t, :], lambda t: GLO[:, t, :],
                                (m == 0, m == FFN_OUT_PER_TILE - 1)).then_inc(k.blocks_used, 1)
                        q += 1
                        if f.mod is not None:
                            if m == 0:
                                pe.wait_ge(*st.dve.before(f"mods{n}", i))
                            block_ready(pe, st.b0 + q, i, f.nb)
                            mod_tile(pe, (st.b0 + q) % 2, bank[6 + n][:, 2 * m:2 * m + 2]).then_inc(k.blocks_used, 1)
                            q += 1

        def ffn_scalar(act, f):
            norm_scalar(act, f.norm)
            st = f.up
            st.enter(act, "act")
            with act.Fori(0, FT // 2) as i:
                for n in range(2):
                    block_out(act, st.b0 + 2 * n, i, 4)
                    round_block(act, st.b0 + 2 * n + 2, i, 4)
                    act.wait_ge(*st.dve.before(f"mul{n}", i))
                    act.activation(SILU[:, n, :], bank[2 * n], ACT.Silu).then_inc(*st.act.inc(f"silu{n}"))
                    round_block(act, st.b0 + 2 * n + 3, i, 4)
                    act.wait_ge(*st.dve.at(f"mul{n}", i))
                    act.activation(GHI[:, i * 2 + n, :], GF[:, n, :], ACT.Copy).then_inc(*st.act.inc(f"hi{n}"))
            st = f.down
            with act.Fori(0, FFN_OUT_LOOPS) as i:
                for q in range(f.nb):
                    round_block(act, st.b0 + q + 2, i, f.nb)

        def ffn_vector(dve, f):
            norm_vector(dve, f.norm)
            st = f.up
            st.enter(dve, "dve")
            with dve.Fori(0, FT // 2) as i:
                for n in range(2):
                    block_out(dve, st.b0 + 2 * n + 1, i, 4)
                    dve.wait_ge(*st.act.at(f"silu{n}", i))
                    dve.tensor_tensor(GF[:, n, :], bank[2 * n + 1], SILU[:, n, :], ALU.mult)\
                       .then_inc(*st.dve.inc(f"mul{n}"))
                    dve.wait_ge(*st.act.at(f"hi{n}", i))
                    dve.tensor_tensor(GLO[:, i * 2 + n, :], GF[:, n, :], GHI[:, i * 2 + n, :].bitcast(F32), ALU.subtract)\
                       .then_inc(*st.dve.inc(f"lo{n}"))
            st = f.down
            with dve.Fori(0, FFN_OUT_LOOPS) as i:
                for n in range(2):
                    per = f.nb // 2
                    block_out(dve, st.b0 + per * (n + 1) - 1, i, f.nb)
                    xt = X[:, i * 2 + n, :]
                    dve.scalar_tensor_tensor(out=xt, in0=bank[4 + n], scalar=0.5, in1=xt, op0=ALU.mult, op1=ALU.add)\
                       .then_inc(*st.dve.inc(f"x{n}"))
                    if f.mod is not None:
                        m0 = FFN_OUT_PER_TILE * n
                        for m in range(FFN_OUT_PER_TILE):
                            ins = dve.tensor_scalar(MOD[:, i * MOD_PER_OUT + (f.mod * MOD_TILES + m0 + m), :],
                                                    bank[6 + n][:, 2 * m:2 * m + 2],
                                                    col(f"b_mod{f.mod}", i * MOD_PER_OUT + (m0 + m)), None, ALU.add)
                        ins.then_inc(*st.dve.inc(f"mods{n}"))

        ra = Area(after_h)
        LD = ra("LD", [P, 3, T])
        PBUF = ra("PBUF", [P, 3, T + 8])
        RKV = ra("RKV", [P, 3, T])
        YAHI, YALO = ra("YAHI", [P, KT, T], F32R), ra("YALO", [P, KT, T], F32R)
        after_ya = ra.at
        DIF = ra("DIF", [P, 3, T])
        W3S = ra("W3S", [P, 3 * P])
        SG, AA, CSUM, CPREV = (ra(n, [P, T]) for n in ("SG", "AA", "CSUM", "CPREV"))
        E1, E2, E3 = (ra(n, [P, T]) for n in ("E1", "E2", "E3"))
        KK, KP, RK, BON, GG = (ra(n, [P, T]) for n in ("KK", "KP", "RK", "BON", "GG"))
        AR = ra("AR", [P, 2, T])
        BT, KTL = ra("BT", [P, T]), ra("KTL", [P, T])
        VS = RKV[:, 2, :]
        BTOK, KTOK, VTOK = (ra(n, [P, CHUNKS, HD]) for n in ("BTOK", "KTOK", "VTOK"))
        AY = ra("AY", [P, CHUNKS, 2 * HD])
        MA1, MA2 = ra("MA1", [P, CHUNKS, 2 * CHUNK]), ra("MA2", [P, CHUNKS, 2 * CHUNK])
        AL = ra("AL", [P, CHUNKS, CHUNK])
        rb = Area(0)
        rb.at = after_ya + 4 * 3 * T + 4 * 3 * P
        XI, XIT, TS, QS = (rb(n, [P, CHUNKS, CHUNK]) for n in ("XI", "XIT", "TS", "QS"))
        rb.at += 4 * T
        ZS = rb("ZS", [P, CHUNKS, 2 * HD])
        GT = rb("GT", [P, CHUNKS, HD])
        SS = rb("SS", [P, CHUNKS, HD])
        OS = ra("OS", [P, T])
        w3_at = (arena - 4 * PAIRS * 3 * P) // 64 * 64
        W3 = place("W3", [P, PAIRS, 3 * P], w3_at)
        assert max(ra.at, upper) <= w3_at, (ra.at, upper, w3_at)

        mix_norm = None
        rw_pe = ["zw", "za", "g", "kkss", "bonus", "tok_a", "tok_b", "tok_k", "tok_v", "m1", "m2", "al"]
        for l in range(1, LEVELS):
            rw_pe += [f"t{l}"] + ([f"x{l}"] if l < LEVELS - 1 else []) + [f"xt{l}"]
        rw_pe += ["y", "z", "q", "gt"] + [f"s{n}" for n in range(CHUNKS - 1)] + ["o", "mean", "var"]
        rw_act = ["pb0", "pb1", "pb2", "sg", "aa", "gg", "kksq", "kkn", "e1", "e2", "e3", "tok_a", "tok_b", "tok_k", "tok_v"]
        rw_act += [f"t{l}" for l in range(1, LEVELS)] + ["y", "z0", "z1", "os", "dsq", "sd", "hi"]
        rw_dve = ["d0", "r", "d1", "k", "d2", "v", "mods", "w3", "csum", "cprev", "kkr", "kkmax", "kkinv", "kk",
                  "am1", "kp", "rt", "at", "bb", "bt", "ktl", "rk", "bon", "m1a", "m1b", "m2a", "m2b", "al", "xi", "xit",
                  "xi0", "xit0"]
        for l in range(1, LEVELS):
            rw_dve += ([f"x{l}"] if l < LEVELS - 1 else []) + [f"xt{l}"]
        rw_dve += ["q", "gt"] + [f"s{n}" for n in range(CHUNKS - 1)] + ["dd", "rinv", "y0", "y1", "y2", "yf", "lo"]

        def h_hi(t):
            return HHI[:, t, :]

        def h_lo(t):
            return HLO[:, t, :]
        ALLK = [(u, u) for u in range(KT)]

        def lora_tensor(pe, st):
            st.enter(pe, "pe")
            for c in range(LORA_BLOCKS):
                block_ready(pe, st.b0 + c)
                product(pe, bank[c], (st.b0 + c) % 2, ALLK, h_hi, h_lo, WHOLE).then_inc(k.blocks_used, 1)

        def lora_scalar(act, st):
            for c in range(LORA_BLOCKS):
                block_out(act, st.b0 + c)
                round_block(act, st.b0 + c + 2)
                act.activation(PBUF[:, c, 1:T + 1], bank[c], ACT.Copy).then_inc(*st.act.inc(f"pb{c}"))
            act.wait_ge(*st.dve.at("o2"))
            act.activation(LD[0:W_LORA, 0, :], LD[0:W_LORA, 0, :], ACT.Tanh).then_inc(*st.act.inc("tanh"))
            act.activation(LD[:, 1:3, :], LD[:, 1:3, :], ACT.Sigmoid).then_inc(*st.act.inc("sig"))

        def token_shift(dve, st, c, name, out, mu, i=0):
            dve.wait_ge(*st.act.at(f"pb{c}", i))
            dve.tensor_tensor(DIF[:, c, :], PBUF[:, c, 0:T], PBUF[:, c, 1:T + 1], ALU.subtract).then_inc(*st.dve.inc(f"d{c}"))
            dve.wait_ge(*st.dve.at(f"d{c}", i))
            dve.scalar_tensor_tensor(out=out, in0=DIF[:, c, :], scalar=mu, in1=PBUF[:, c, 1:T + 1], op0=ALU.mult, op1=ALU.add)\
               .then_inc(*st.dve.inc(name))

        def lora_vector(dve, st):
            st.enter(dve, "dve")
            dve.memset(PBUF[:, :, 0:1], 0.0).then_inc(*st.dve.inc("zero"))
            dve.wait_ge(*st.dve.at("zero"))
            for c in range(LORA_BLOCKS):
                token_shift(dve, st, c, f"o{c}", LD[:, c, :], col("mu_lora", c))

        def both(f):
            for h in range(2):
                f(slice(h * HD, h * HD + HD))

        def each_unit(pe, out, lhs, rhs, parts=1):
            mm = None
            pe.sem_inc(tensor_ready)
            for n in range(CHUNKS):
                for h in range(2):
                    s = slice(h * HD, h * HD + HD)
                    mm = pe.matmul(out(s, n), lhs(s, n), rhs(s, n), start=True, stop=True)
            return mm

        def rwkv_tensor(pe, st):
            st.enter(pe, "pe")
            A, V, S = st.act, st.dve, st.pe
            with pe.Fori(0, PAIRS) as j:
                for c in range(3):
                    pe.wait_ge(*(A.before("pb2", j) if c == 0 else V.before("mods", j) if c == 1 else A.at("pb0", j)))
                    block_ready(pe, st.b0 + c, j, PAIR_BLOCKS)
                    product(pe, bank[6 + c % 2], (st.b0 + c) % 2, ALLK, h_hi, h_lo, WHOLE).then_inc(k.blocks_used, 1)
                pe.wait_ge(*A.at("pb1", j))
                for m in range(MOD_PER_PAIR):
                    block_ready(pe, st.b0 + 3 + m, j, PAIR_BLOCKS)
                    mod_tile(pe, (st.b0 + 3 + m) % 2, bank[7][:, 2 * m:2 * m + 2]).then_inc(k.blocks_used, 1)
                pe.wait_ge(*V.at("w3", j))
                pe.matmul(bank[0], W3S[0:W_LORA, 0:P], LD[0:W_LORA, 0, :], start=True, stop=True).then_inc(*S.inc("zw"))
                pe.matmul(bank[1], W3S[W_LORA:P, 0:P], LD[W_LORA:P, 0, :], start=True, stop=True).then_inc(*S.inc("za"))
                pe.matmul(bank[2], W3S[:, P:2 * P], LD[:, 1, :], start=True, stop=False)
                pe.matmul(bank[2], W3S[:, 2 * P:3 * P], LD[:, 2, :], start=False, stop=True).then_inc(*S.inc("g"))
                pe.wait_ge(*A.at("kksq", j))
                pe.matmul(bank[3], heads, OS[:, :], start=True, stop=True).then_inc(*S.inc("kkss"))
                pe.wait_ge(*V.at("rk", j))
                pe.wait_ge(*A.at("kkn", j))
                pe.matmul(bank[3], heads, RK[:, :], start=True, stop=True).then_inc(*S.inc("bonus"))
                e2 = lambda s: FCC[s, FC["eye2"]:FC["eye2"] + HD]
                chunk = lambda t: lambda s, n: t[s, n * CHUNK:(n + 1) * CHUNK]
                unit = lambda t: lambda s, n: t[s, n * CHUNK:(n + 1) * CHUNK]
                pe.wait_ge(*V.at("ktl", j))
                each_unit(pe, unit(bank[4]), lambda s, n: AR[s, 0, n * CHUNK:(n + 1) * CHUNK], lambda s, n: e2(s)).then_inc(*S.inc("tok_a"))
                each_unit(pe, unit(bank[5]), chunk(BT), lambda s, n: e2(s)).then_inc(*S.inc("tok_b"))
                pe.wait_ge(*A.at("sg", j))
                each_unit(pe, unit(bank[0]), chunk(KTL), lambda s, n: e2(s)).then_inc(*S.inc("tok_k"))
                pe.wait_ge(*A.at("aa", j))
                each_unit(pe, unit(bank[1]), chunk(VS), lambda s, n: e2(s)).then_inc(*S.inc("tok_v"))
                both_rhs = lambda s, n: AR[s, :, n * CHUNK:(n + 1) * CHUNK]
                wide = lambda t: lambda s, n: t[s, n * 2 * CHUNK:(n + 1) * 2 * CHUNK]
                pe.wait_ge(*A.at("gg", j))
                pe.wait_ge(*V.at("bon", j))
                each_unit(pe, wide(two_banks[1]), chunk(BT), both_rhs).then_inc(*S.inc("m1"))
                pe.wait_ge(*A.at("tok_a", j))
                pe.wait_ge(*A.at("tok_b", j))
                each_unit(pe, wide(two_banks[2]), chunk(KTL), both_rhs).then_inc(*S.inc("m2"))
                pe.wait_ge(*A.at("tok_k", j))
                each_unit(pe, unit(bank[0]), lambda s, n: AR[s, 0, n * CHUNK:(n + 1) * CHUNK], chunk(BT)).then_inc(*S.inc("al"))
                mat = lambda t: lambda s, n: t[s, n, 0:CHUNK]
                for l in range(1, LEVELS):
                    pe.wait_ge(*V.at("xit0" if l == 1 else f"xt{l - 1}", j))
                    if l == 1:
                        pe.wait_ge(*A.at("tok_v", j))
                    each_unit(pe, unit(bank[1]), mat(MA1), mat(XI)).then_inc(*S.inc(f"t{l}"))
                    pe.wait_ge(*A.at(f"t{l}", j))
                    if l < LEVELS - 1:
                        each_unit(pe, unit(bank[2]), mat(XIT), mat(TS)).then_inc(*S.inc(f"x{l}"))
                    each_unit(pe, unit(bank[3]), mat(TS), mat(XIT)).then_inc(*S.inc(f"xt{l}"))
                pe.wait_ge(*V.at("m2b", j))
                each_unit(pe, unit(bank[4]), mat(MA2), mat(VTOK)).then_inc(*S.inc("y"))
                pe.wait_ge(*A.at("y", j))
                pe.wait_ge(*V.at(f"xt{LEVELS - 1}", j))
                each_unit(pe, wide(two_banks[1]), mat(XIT), lambda s, n: AY[s, n, :]).then_inc(*S.inc("z"))
                pe.wait_ge(*A.at("z1", j))
                each_unit(pe, unit(bank[4]), mat(ZS), lambda s, n: MA1[s, n, CHUNK:2 * CHUNK]).then_inc(*S.inc("q"))
                each_unit(pe, unit(bank[5]), mat(ZS), mat(BTOK)).then_inc(*S.inc("gt"))
                pe.wait_ge(*V.at("gt", j))
                for n in range(CHUNKS - 1):
                    o = lambda s: bank[4 * (n % 2)][s, n * HD:(n + 1) * HD]
                    if n >= 2:
                        pe.wait_ge(*V.at(f"s{n - 2}", j))
                    pe.sem_inc(tensor_ready)
                    for h in range(2):
                        s = slice(h * HD, h * HD + HD)
                        pe.matmul(o(s), BTOK[s, n, :], ZS[s, n, HD:2 * HD], start=True, stop=False)
                        mm = pe.matmul(o(s), KTOK[s, n, :], VTOK[s, n, :], start=False, stop=n == 0)
                    if n:
                        pe.wait_ge(*V.at(f"s{n - 1}", j))
                        pe.sem_inc(tensor_ready)
                        for h in range(2):
                            s = slice(h * HD, h * HD + HD)
                            mm = pe.matmul(o(s), GT[s, n, :], SS[s, n, :], start=False, stop=True)
                    mm.then_inc(*S.inc(f"s{n}"))
                pe.wait_ge(*V.at(f"s{CHUNKS - 2}", j))
                pe.sem_inc(tensor_ready)
                for n in range(CHUNKS):
                    for h in range(2):
                        s = slice(h * HD, h * HD + HD)
                        o = bank[1][s, n * CHUNK:(n + 1) * CHUNK]
                        pe.matmul(o, ZS[s, n, HD:2 * HD], MA1[s, n, CHUNK:2 * CHUNK], start=True, stop=False)
                        mm = pe.matmul(o, VTOK[s, n, :], MA2[s, n, CHUNK:2 * CHUNK], start=False, stop=n == 0)
                        if n:
                            mm = pe.matmul(o, SS[s, n, :], QS[s, n, :], start=False, stop=True)
                mm.then_inc(*S.inc("o"))
                pe.wait_ge(*A.at("os", j))
                pe.matmul(bank[2], heads, OS[:, :], start=True, stop=True).then_inc(*S.inc("mean"))
                pe.wait_ge(*A.at("dsq", j))
                pe.matmul(bank[3], heads, KK[:, :], start=True, stop=True).then_inc(*S.inc("var"))

        def rwkv_scalar(act, st):
            A, V, S = st.act, st.dve, st.pe
            with act.Fori(0, PAIRS) as j:
                for c in range(3):
                    block_out(act, st.b0 + c, j, PAIR_BLOCKS)
                    round_block(act, st.b0 + c + 2, j, PAIR_BLOCKS)
                    act.wait_ge(*V.before("lo", j))
                    act.activation(PBUF[:, c, 1:T + 1], bank[6 + c % 2], ACT.Copy).then_inc(*A.inc(f"pb{c}"))
                for m in range(MOD_PER_PAIR):
                    round_block(act, st.b0 + 3 + m + 2, j, PAIR_BLOCKS)
                act.wait_ge(*S.at("zw", j))
                act.activation(SG[:, :], bank[0], ACT.Sigmoid, bias=col("w0", j)).then_inc(*A.inc("sg"))
                act.wait_ge(*S.at("za", j))
                act.activation(AA[:, :], bank[1], ACT.Sigmoid, bias=col("a0", j)).then_inc(*A.inc("aa"))
                act.wait_ge(*S.at("g", j))
                act.activation(GG[:, :], bank[2], ACT.Copy).then_inc(*A.inc("gg"))
                act.wait_ge(*V.at("kkr", j))
                act.activation(OS[:, :], KK[:, :], ACT.Square).then_inc(*A.inc("kksq"))
                act.wait_ge(*S.at("kkss", j))
                act.activation(E3[:, :], bank[3], ACT.Sqrt).then_inc(*A.inc("kkn"))
                act.wait_ge(*V.at("cprev", j))
                act.activation(E1[:, :], CSUM[:, :], ACT.Exp, scale=-DECAY).then_inc(*A.inc("e1"))
                act.activation(E2[:, :], CSUM[:, :], ACT.Exp, scale=DECAY).then_inc(*A.inc("e2"))
                act.wait_ge(*V.at("kk", j))
                act.activation(E3[:, :], CPREV[:, :], ACT.Exp, scale=-DECAY).then_inc(*A.inc("e3"))
                flat = lambda t: t[:, :, :].rearrange("p n c -> p (n c)")
                u3 = lambda t: t.rearrange("p (n c) -> p n c", n=CHUNKS)
                act.wait_ge(*S.at("tok_a", j))
                act.activation(AY[:, :, 0:HD], u3(bank[4]), ACT.Copy).then_inc(*A.inc("tok_a"))
                act.wait_ge(*S.at("tok_b", j))
                act.activation(flat(BTOK), bank[5], ACT.Copy).then_inc(*A.inc("tok_b"))
                act.wait_ge(*S.at("tok_k", j))
                act.activation(flat(KTOK), bank[0], ACT.Copy).then_inc(*A.inc("tok_k"))
                act.wait_ge(*S.at("tok_v", j))
                act.activation(flat(VTOK), bank[1], ACT.Copy).then_inc(*A.inc("tok_v"))
                for l in range(1, LEVELS):
                    act.wait_ge(*S.at(f"t{l}", j))
                    act.activation(flat(TS), bank[1], ACT.Copy).then_inc(*A.inc(f"t{l}"))
                act.wait_ge(*S.at("y", j))
                act.activation(AY[:, :, HD:2 * HD], u3(bank[4]), ACT.Copy).then_inc(*A.inc("y"))
                act.wait_ge(*S.at("z", j))
                half = CHUNKS // 2
                for z in range(2):
                    act.activation(ZS[:, z * half:(z + 1) * half, :].rearrange("p n c -> p (n c)"), bank[2 + z], ACT.Copy)\
                       .then_inc(*A.inc(f"z{z}"))
                act.wait_ge(*S.at("o", j))
                act.activation(OS[:, :], bank[1], ACT.Copy).then_inc(*A.inc("os"))
                act.wait_ge(*V.at("dd", j))
                act.activation(KK[:, :], RK[:, :], ACT.Square).then_inc(*A.inc("dsq"))
                act.wait_ge(*S.at("var", j))
                act.activation(E1[:, :], bank[3], ACT.Sqrt, scale=1.0 / HD, bias=EPS[:, 1:2]).then_inc(*A.inc("sd"))
                act.wait_ge(*V.at("yf", j))
                act.activation(YAHI[:, j, :], RK[:, :], ACT.Copy).then_inc(*A.inc("hi"))

        def rwkv_vector(dve, st):
            st.enter(dve, "dve")
            A, V, S = st.act, st.dve, st.pe
            r, kx, v = (RKV[:, c, :] for c in range(3))
            def tt(name, out, a, b, op, *waits):
                for w in waits:
                    dve.wait_ge(*w)
                dve.tensor_tensor(out, a, b, op).then_inc(*V.inc(name))
            def stt(name, out, a, s, b, op0, op1, *waits):
                for w in waits:
                    dve.wait_ge(*w)
                dve.scalar_tensor_tensor(out=out, in0=a, scalar=s, in1=b, op0=op0, op1=op1).then_inc(*V.inc(name))
            def ts(name, out, a, s1, s2, op0, op1, *waits):
                for w in waits:
                    dve.wait_ge(*w)
                dve.tensor_scalar(out, a, s1, s2, op0, *([op1] if op1 is not None else [])).then_inc(*V.inc(name))
            n8 = lambda t: t.rearrange("p (n c) -> p n c", c=CHUNK)
            rep = lambda t, n=CHUNKS: t.rearrange("p (o c) -> p o c", o=1).to_broadcast([P, n, t.shape[1]])
            with dve.Fori(0, PAIRS) as j:
                dve.wait_ge(*S.before("var", j))
                for c, name in enumerate("rkv"):
                    token_shift(dve, st, c, name, RKV[:, c, :], col("mu_rkv", j * 3 + c), j)
                block_out(dve, st.b0 + PAIR_BLOCKS - 1, j, PAIR_BLOCKS)
                for m in range(MOD_PER_PAIR):
                    ins = dve.tensor_scalar(MOD[:, j * MOD_PER_PAIR + m, :], bank[7][:, 2 * m:2 * m + 2],
                                            col("b_mod0", j * MOD_PER_PAIR + m), None, ALU.add)
                ins.then_inc(*V.inc("mods"))
                dve.tensor_copy(W3S[:, :], W3[:, j, :]).then_inc(*V.inc("w3"))
                dve.wait_ge(*A.at("sg", j))
                dve.tensor_tensor_scan(CSUM[:, :], FCC[:, FC["scan"]:FC["scan"] + T], SG[:, :], 0.0, ALU.mult, ALU.add)\
                   .then_inc(*V.inc("csum"))
                tt("cprev", CPREV[:, :], CSUM[:, :], SG[:, :], ALU.subtract, V.at("csum", j))
                ts("kkr", KK[:, :], kx, col("k_k", j), None, ALU.mult, None, V.at("k", j))
                ts("kkmax", E3[:, :], E3[:, :], 1e-12, None, ALU.max, None, A.at("kkn", j))
                dve.wait_ge(*V.at("kkmax", j))
                dve.reciprocal(E3[:, :], E3[:, :]).then_inc(*V.inc("kkinv"))
                tt("kk", KK[:, :], KK[:, :], E3[:, :], ALU.mult, V.at("kkinv", j))
                ts("am1", RK[:, :], AA[:, :], 1.0, col("k_a", j), ALU.subtract, ALU.mult, A.at("aa", j))
                stt("kp", KP[:, :], RK[:, :], 1.0, kx, ALU.add, ALU.mult, V.at("am1", j))
                tt("rt", AR[:, 1, :], r, E1[:, :], ALU.mult, A.at("e1", j))
                stt("at", AR[:, 0, :], KK[:, :], -1.0, E3[:, :], ALU.mult, ALU.mult, A.at("e3", j), V.at("kk", j))
                tt("bb", BT[:, :], KK[:, :], AA[:, :], ALU.mult)
                tt("bt", BT[:, :], BT[:, :], E2[:, :], ALU.mult, V.at("bb", j))
                tt("ktl", KTL[:, :], KP[:, :], E2[:, :], ALU.mult, V.at("kp", j))
                stt("rk", RK[:, :], r, col("r_k", j), KP[:, :], ALU.mult, ALU.mult)
                tt("bon", BON[:, :], bank[3], v, ALU.mult, S.at("bonus", j))
                half = CHUNKS // 2
                pair_mask = rep(FCC[:, FC["before"]:FC["before"] + 2 * CHUNK], half)
                for m, (dst, name) in enumerate(((MA1, "m1"), (MA2, "m2"))):
                    for z in range(2):
                        tt(f"{name}{'ab'[z]}", dst[:, z * half:(z + 1) * half, :],
                           bank[2 + 2 * m + z].rearrange("p (n c) -> p n c", n=half), pair_mask, ALU.mult, S.at(name, j))
                tt("al", AL[:, :, :], n8(bank[0]), rep(FCC[:, FC["after"]:FC["after"] + CHUNK]), ALU.mult, S.at("al", j))
                ident = rep(FCC[:, FC["eye2"]:FC["eye2"] + CHUNK])
                level = lambda l, up: rep(LVL[:, l + LEVELS * up, :])
                dve.tensor_copy(XI[:, :, :], ident).then_inc(*V.inc("xi"))
                dve.tensor_copy(XIT[:, :, :], ident).then_inc(*V.inc("xit"))
                dve.wait_ge(*V.at("xi", j))
                dve.sem_inc(vector_ready)
                dve.copy_predicated(XI[:, :, :], level(0, 0), AL[:, :, :]).then_inc(*V.inc("xi0"))
                dve.wait_ge(*V.at("xit", j))
                dve.sem_inc(vector_ready)
                dve.copy_predicated(XIT[:, :, :], level(0, 1), MA1[:, :, 0:CHUNK]).then_inc(*V.inc("xit0"))
                for l in range(1, LEVELS):
                    if l < LEVELS - 1:
                        dve.wait_ge(*S.at(f"xt{l}", j))
                        dve.sem_inc(vector_ready)
                        dve.copy_predicated(XI[:, :, :], level(l, 0), n8(bank[2])).then_inc(*V.inc(f"x{l}"))
                    dve.wait_ge(*S.at(f"xt{l}", j))
                    dve.sem_inc(vector_ready)
                    dve.copy_predicated(XIT[:, :, :], level(l, 1), n8(bank[3])).then_inc(*V.inc(f"xt{l}"))
                tt("q", QS[:, :, :], n8(bank[4]), n8(AR[:, 1, :]), ALU.add, S.at("q", j))
                tt("gt", GT[:, :, :], n8(bank[5]), ident, ALU.add, S.at("gt", j))
                for n in range(CHUNKS - 1):
                    end = (n + 1) * CHUNK - 1
                    ts(f"s{n}", SS[:, n + 1, :], bank[4 * (n % 2)][:, n * HD:(n + 1) * HD], E1[:, end:end + 1], None, ALU.mult, None, S.at(f"s{n}", j))
                stt("dd", RK[:, :], bank[2], -1.0 / HD, OS[:, :], ALU.mult, ALU.add, S.at("mean", j))
                dve.wait_ge(*A.at("sd", j))
                dve.reciprocal(E1[:, :], E1[:, :]).then_inc(*V.inc("rinv"))
                tt("y0", RK[:, :], RK[:, :], E1[:, :], ALU.mult, V.at("rinv", j))
                ts("y1", RK[:, :], RK[:, :], col("ln_w", j), col("ln_b", j), ALU.mult, ALU.add, V.at("y0", j))
                tt("y2", RK[:, :], RK[:, :], BON[:, :], ALU.add, V.at("y1", j))
                tt("yf", RK[:, :], RK[:, :], GG[:, :], ALU.mult, V.at("y2", j))
                tt("lo", YALO[:, j, :], RK[:, :], YAHI[:, j, :].bitcast(F32), ALU.subtract, A.at("hi", j))

        free_lo = Area(after_h)
        free_hi = Area(after_ya)
        QT, KTT = free_hi("QT", [P, AT_TILES, T]), free_hi("KTT", [P, AT_TILES, T])
        VT = free_hi("VT", [P, AT_TILES, BLOCKS, P])
        UU, MM, DD = (free_hi(n, [P, 3, T]) for n in ("UU", "MM", "DD"))
        RS = free_hi("RS", [P, 2, T])
        free_hi.at = after_ya
        YBHI, YBLO = free_hi("YBHI", [P, AT_TILES, T], F32R), free_hi("YBLO", [P, AT_TILES, T], F32R)
        after_yb = free_hi.at
        SQA, VCH, RNA = (free_lo(n, [P, 2, T]) for n in ("SQA", "VCH", "RNA"))
        free_lo.at = after_h
        SMB = free_lo("SMB", [P, 2, 4 * 2 * P])
        PEX, PT = free_lo("PEX", [P, 4 * 2 * P]), nc.alloc_sbuf_tensor_at("PT", [P, 4 * 2 * P], F32, offset=arena0 + w3_at)
        MX, NM, DEN = (free_lo(n, [P, 4 * AT_TILES, BLOCKS]) for n in ("MX", "NM", "DEN"))
        assert free_lo.at <= after_h + 4 * (3 * T + 3 * (T + 8) + 3 * T), free_lo.at
        GROUPS = 3
        UNITS_AT = [(2 * g + hp, g, h) for hp in range(2) for g in range(GROUPS) for h in range(2)]

        def in_order(t, g):
            return t if g == 0 else t.rearrange("p (i d) -> p d i", d=4 if g == 1 else 16)

        def ordered(t, g):
            return t if g == 0 else t.rearrange("p (d i) -> p d i", d=4 if g == 1 else 16)

        ain_pe, ain_act, ain_dve = [], [], []
        for c in range(AT_TILES):
            ain_pe += [f"sum{c}q"] + ([f"vt{c - 1}"] if c else []) + [f"sum{c}k"]
            ain_act += [f"sq{c}q", f"sd{c}q", f"sq{c}k", f"sd{c}k", f"vc{c}"]
            ain_dve += ([f"vt{c - 1}"] if c else []) + [f"ri{c}q", f"n{c}q", f"ri{c}k", f"n{c}k"]
        ain_pe += [f"vt{AT_TILES - 1}"]
        ain_dve += [f"vt{AT_TILES - 1}"]

        def attention_in_tensor(pe, st):
            A, V, S = st.act, st.dve, st.pe
            st.enter(pe, "pe")
            def stream_tile(c, s):
                n = 3 * c + s
                if n >= 4:
                    m = n - 4
                    pe.wait_ge(*(A.at(f"vc{m // 3}") if m % 3 == 2 else V.at(f"n{m // 3}{'qk'[m % 3]}")))
                block_ready(pe, st.b0 + n)
                product(pe, bank[n % 4], (st.b0 + n) % 2, ALLK, h_hi, h_lo, WHOLE).then_inc(k.blocks_used, 1)
            def head_sum(c, s):
                name = f"{c}{'qk'[s]}"
                pe.wait_ge(*A.at(f"sq{name}"))
                if c:
                    pe.wait_ge(*A.at(f"sd{c - 1}{'qk'[s]}"))
                pe.matmul(bank[4 + s], heads, SQA[:, s, :], start=True, stop=True).then_inc(*S.inc(f"sum{name}"))
            def v_tokens(c):
                pe.wait_ge(*A.at(f"vc{c}"))
                if c >= 2:
                    pe.wait_ge(*V.at(f"vt{c - 2}"))
                for b in range(BLOCKS):
                    mm = pe.transpose(bank[6 + c % 2][:, b * P:(b + 1) * P], VCH[:, c % 2, b * P:(b + 1) * P], eye)
                mm.then_inc(*S.inc(f"vt{c}"))
            for c in range(AT_TILES):
                stream_tile(c, 0)
                stream_tile(c, 1)
                head_sum(c, 0)
                if c:
                    v_tokens(c - 1)
                stream_tile(c, 2)
                head_sum(c, 1)
            v_tokens(AT_TILES - 1)

        def attention_in_scalar(act, st):
            A, V, S = st.act, st.dve, st.pe
            st.enter(act, "act")
            for c in range(AT_TILES):
                for s in range(3):
                    n = 3 * c + s
                    block_out(act, st.b0 + n)
                    round_block(act, st.b0 + n + 2)
                    if s == 2:
                        if c >= 2:
                            act.wait_ge(*S.at(f"vt{c - 2}"))
                        act.activation(ordered(VCH[:, c % 2, :], c // 2), in_order(bank[n % 4], c // 2), ACT.Copy)\
                           .then_inc(*A.inc(f"vc{c}"))
                        continue
                    name = f"{c}{'qk'[s]}"
                    if c:
                        act.wait_ge(*S.at(f"sum{c - 1}{'qk'[s]}"))
                    act.activation(SQA[:, s, :], bank[n % 4], ACT.Square).then_inc(*A.inc(f"sq{name}"))
                    act.wait_ge(*S.at(f"sum{name}"))
                    if c:
                        act.wait_ge(*V.at(f"n{c - 1}{'qk'[s]}"))
                    act.activation(RNA[:, s, :], bank[4 + s], ACT.Sqrt, scale=1.0 / HD, bias=EPS[:, 0:1])\
                       .then_inc(*A.inc(f"sd{name}"))

        def attention_in_vector(dve, st):
            A, V, S = st.act, st.dve, st.pe
            st.enter(dve, "dve")
            def v_out(c):
                dve.wait_ge(*S.at(f"vt{c}"))
                dve.tensor_copy(VT[:, c, :, :].rearrange("p b n -> p (b n)"), bank[6 + c % 2]).then_inc(*V.inc(f"vt{c}"))
            for c in range(AT_TILES):
                if c:
                    v_out(c - 1)
                for s, (dst, gain) in enumerate(((QT, "q_norm"), (KTT, "k_norm"))):
                    name = f"{c}{'qk'[s]}"
                    dve.wait_ge(*A.at(f"sd{name}"))
                    dve.reciprocal(RNA[:, s, :], RNA[:, s, :]).then_inc(*V.inc(f"ri{name}"))
                    dve.wait_ge(*V.at(f"ri{name}"))
                    g = c // 2
                    dve.scalar_tensor_tensor(out=ordered(dst[:, c, :], g), in0=in_order(bank[(3 * c + s) % 4], g), scalar=col(gain),
                                             in1=in_order(RNA[:, s, :], g), op0=ALU.mult, op1=ALU.mult).then_inc(*V.inc(f"n{name}"))
            v_out(AT_TILES - 1)

        NU = len(UNITS_AT)
        att_pe, att_act, att_dve = ["sc0"], [], ["neg"]
        for u in range(NU):
            att_pe += ([f"sc{u + 1}"] if u + 1 < NU else []) + [f"tr{u}", f"pv{u}", f"mb{u}", f"db{u}"]
            att_act += [f"ex{u}", f"pt{u}", f"u{u}", f"m{u}"]
            att_dve += [f"mk{u}", f"mx{u}", f"nm{u}"] + ([f"d{u - 1}"] if u else [])
            if u % 6 == 0 and u:
                att_dve += [f"{n}{u // 6 - 1}" for n in ("max0", "max", "sub", "de", "s0", "s1", "ri", "al", "y", "lo")]
            if u % 6 == 5:
                att_act += [f"e{u // 6}", f"hi{u // 6}"]
        att_dve += [f"d{NU - 1}"] + [f"{n}1" for n in ("max0", "max", "sub", "de", "s0", "s1", "ri", "al", "y", "lo")]

        def width(g):
            return 2 if g == 0 else 1

        def attention_tensor(pe, st):
            A, V, S = st.act, st.dve, st.pe
            st.enter(pe, "pe")
            def scores(u):
                c, g, h = UNITS_AT[u]
                hs = slice(h * HD, h * HD + HD)
                if u >= 2:
                    pe.wait_ge(*V.at(f"d{u - 2}"))
                for b in range(BLOCKS):
                    k0 = max(b - width(g) + 1, 0)
                    dst = two_banks[u % 2][:, (2 * b + 2 - (b + 1 - k0)) * P:(2 * b + 2) * P]
                    mm = pe.matmul(dst, QT[hs, c, b * P:(b + 1) * P], KTT[hs, c, k0 * P:(b + 1) * P], start=True, stop=True)
                mm.then_inc(*S.inc(f"sc{u}"))
            scores(0)
            for u, (c, g, h) in enumerate(UNITS_AT):
                hs = slice(h * HD, h * HD + HD)
                if u + 1 < NU:
                    scores(u + 1)
                keys = [(b, w) for b in range(BLOCKS) for w in range(2 - width(g), 2) if b + w >= 1]
                pe.wait_ge(*A.at(f"ex{u}"))
                if u:
                    pe.wait_ge(*A.at(f"pt{u - 1}"))
                for b, w in keys:
                    mm = pe.transpose(two_banks[2][:, (2 * b + w) * P:(2 * b + w + 1) * P], PEX[:, (2 * b + w) * P:(2 * b + w + 1) * P], eye)
                mm.then_inc(*S.inc(f"tr{u}"))
                pe.wait_ge(*A.at(f"pt{u}"))
                if u >= 2:
                    pe.wait_ge(*A.at(f"u{u - 2}"))
                for b, w in keys:
                    first = w == 1 and (width(g) == 1 or b == 0)
                    mm = pe.matmul(bank[6][hs, b * P:(b + 1) * P], VT[:, c, b + w - 1, hs], PT[:, (2 * b + w) * P:(2 * b + w + 1) * P],
                                   start=first or w == 0, stop=w == 1)
                mm.then_inc(*S.inc(f"pv{u}"))
                if u >= 2:
                    pe.wait_ge(*A.at(f"m{u - 2}"))
                for b in range(BLOCKS):
                    mm = pe.matmul(bank[7][hs, b * P:(b + 1) * P], MX[:, u, b:b + 1].to_broadcast([P, HD]), eye, start=True, stop=True)
                mm.then_inc(*S.inc(f"mb{u}"))
                for b in range(BLOCKS):
                    mm = pe.matmul(two_banks[u % 2][hs, b * P:(b + 1) * P], DEN[:, u, b:b + 1].to_broadcast([P, HD]), eye, start=True, stop=True)
                mm.then_inc(*S.inc(f"db{u}"))

        def attention_scalar(act, st):
            A, V, S = st.act, st.dve, st.pe
            st.enter(act, "act")
            for u, (c, g, h) in enumerate(UNITS_AT):
                hs = slice(h * HD, h * HD + HD)
                act.wait_ge(*V.at(f"nm{u}"))
                if u:
                    act.wait_ge(*S.at(f"tr{u - 1}"))
                for b in range(BLOCKS):
                    cols = slice((2 * b + 2 - width(g)) * P, (2 * b + 2) * P)
                    ins = act.activation(PEX[:, cols], SMB[:, u % 2, cols], ACT.Exp, scale=HD ** -0.5, bias=NM[:, u, b:b + 1],
                                         accum_out=DEN[:, u, b:b + 1])
                ins.then_inc(*A.inc(f"ex{u}"))
                act.wait_ge(*S.at(f"tr{u}"))
                if u:
                    act.wait_ge(*S.at(f"pv{u - 1}"))
                four = lambda t: t.rearrange("p (b w n) -> p b w n", b=BLOCKS, w=2)[:, :, 2 - width(g):, :]
                if g == 0:
                    act.activation(PT[:, P:], two_banks[2][:, P:], ACT.Copy).then_inc(*A.inc(f"pt{u}"))
                else:
                    act.activation(four(PT[:, :]), four(two_banks[2]), ACT.Copy).then_inc(*A.inc(f"pt{u}"))
                if u == 6:
                    act.wait_ge(*V.at("lo0"))
                act.wait_ge(*S.at(f"pv{u}"))
                act.activation(in_order(UU[hs, g, :], g), ordered(bank[6][hs, :], g), ACT.Copy).then_inc(*A.inc(f"u{u}"))
                act.wait_ge(*S.at(f"mb{u}"))
                act.activation(in_order(MM[hs, g, :], g), ordered(bank[7][hs, :], g), ACT.Copy).then_inc(*A.inc(f"m{u}"))
                if u % 6 == 5:
                    hp = u // 6
                    act.wait_ge(*V.at(f"sub{hp}"))
                    act.activation(MM[:, :, :], MM[:, :, :], ACT.Exp, scale=HD ** -0.5).then_inc(*A.inc(f"e{hp}"))
                    act.wait_ge(*V.at(f"y{hp}"))
                    for g2 in range(GROUPS):
                        ins = act.activation(YBHI[:, 2 * g2 + hp, :], UU[:, g2, :], ACT.Copy)
                    ins.then_inc(*A.inc(f"hi{hp}"))

        def attention_vector(dve, st):
            A, V, S = st.act, st.dve, st.pe
            st.enter(dve, "dve")
            dve.memset(SMB[:, :, 0:P], NEG_INF).then_inc(*V.inc("neg"))
            dve.wait_ge(*V.at("neg"))
            mask = lambda n, w: FCC[:, FC["masks"] + n * P:FC["masks"] + (n + w) * P]
            four = lambda t: t.rearrange("p (b n) -> p b n", b=BLOCKS)
            all3 = lambda t: t.rearrange("p (o n) -> p o n", o=1).to_broadcast([P, GROUPS, T])
            def den_out(u):
                c, g, h = UNITS_AT[u]
                hs = slice(h * HD, h * HD + HD)
                dve.wait_ge(*S.at(f"db{u}"))
                dve.tensor_copy(in_order(DD[hs, g, :], g), ordered(two_banks[u % 2][hs, 0:T], g)).then_inc(*V.inc(f"d{u}"))
            def combine(hp):
                tt = lambda name, out, a, b, op: dve.tensor_tensor(out, a, b, op).then_inc(*V.inc(f"{name}{hp}"))
                after = lambda name: dve.wait_ge(*V.at(f"{name}{hp}"))
                dve.wait_ge(*A.at(f"m{hp * 6 + 5}"))
                dve.wait_ge(*V.at(f"d{hp * 6 + 5}"))
                tt("max0", RS[:, 0, :], MM[:, 0, :], MM[:, 1, :], ALU.max)
                after("max0")
                tt("max", RS[:, 1, :], RS[:, 0, :], MM[:, 2, :], ALU.max)
                after("max")
                tt("sub", MM[:, :, :], MM[:, :, :], all3(RS[:, 1, :]), ALU.subtract)
                dve.wait_ge(*A.at(f"e{hp}"))
                tt("de", DD[:, :, :], DD[:, :, :], MM[:, :, :], ALU.mult)
                after("de")
                tt("s0", RS[:, 0, :], DD[:, 0, :], DD[:, 1, :], ALU.add)
                after("s0")
                tt("s1", RS[:, 1, :], RS[:, 0, :], DD[:, 2, :], ALU.add)
                after("s1")
                dve.reciprocal(RS[:, 0, :], RS[:, 1, :]).then_inc(*V.inc(f"ri{hp}"))
                after("ri")
                tt("al", MM[:, :, :], MM[:, :, :], all3(RS[:, 0, :]), ALU.mult)
                after("al")
                tt("y", UU[:, :, :], UU[:, :, :], MM[:, :, :], ALU.mult)
                dve.wait_ge(*A.at(f"hi{hp}"))
                for g in range(GROUPS):
                    ins = dve.tensor_tensor(YBLO[:, 2 * g + hp, :], UU[:, g, :], YBHI[:, 2 * g + hp, :].bitcast(F32), ALU.subtract)
                ins.then_inc(*V.inc(f"lo{hp}"))
            for u, (c, g, h) in enumerate(UNITS_AT):
                sm = SMB[:, u % 2, :]
                sc = two_banks[u % 2]
                dve.wait_ge(*S.at(f"sc{u}"))
                if u >= 2:
                    dve.wait_ge(*A.at(f"ex{u - 2}"))
                if g == 0:
                    dve.tensor_tensor(sm[:, P:2 * P], sc[:, P:2 * P], mask(1, 1), ALU.add)
                    dve.tensor_tensor(four(sm)[:, 1:, :], four(sc)[:, 1:, :], mask(0, 2).rearrange("p (o n) -> p o n", o=1)
                                      .to_broadcast([P, BLOCKS - 1, 2 * P]), ALU.add).then_inc(*V.inc(f"mk{u}"))
                else:
                    dve.tensor_tensor(four(sm)[:, :, P:], four(sc)[:, :, P:], mask(g, 1).rearrange("p (o n) -> p o n", o=1)
                                      .to_broadcast([P, BLOCKS, P]), ALU.add).then_inc(*V.inc(f"mk{u}"))
                dve.wait_ge(*V.at(f"mk{u}"))
                dve.tensor_reduce(MX[:, u, :], four(sm)[:, :, (2 - width(g)) * P:], AX, ALU.max).then_inc(*V.inc(f"mx{u}"))
                dve.wait_ge(*V.at(f"mx{u}"))
                dve.tensor_scalar(NM[:, u, :], MX[:, u, :], -HD ** -0.5, None, ALU.mult).then_inc(*V.inc(f"nm{u}"))
                if u:
                    den_out(u - 1)
                if u % 6 == 0 and u:
                    combine(u // 6 - 1)
            den_out(NU - 1)
            combine(1)

        ma = Area(after_h)
        MHI = ma("MHI", [P, KT, T], F32R)
        ma.at = after_yb
        MLO = ma("MLO", [P, KT, T], F32R)
        GAB, PAB, MF = ma("GAB", [P, 2, T]), ma("PAB", [P, 2, T]), ma("MF", [P, T])
        xc_at = (arena - 4 * KT * TC) // 64 * 64
        XC = place("XC", [P, KT, TC], xc_at)
        SIN = place("SIN", [P, T], xc_at - 4 * T)
        assert max(ma.at, upper) <= xc_at - 4 * T and after_h + 4 * KT * T <= after_ya - 8 * KT * T

        def merge_tensor(pe, st):
            A, V = st.act, st.dve
            st.enter(pe, "pe")
            ALLB = [(u, u) for u in range(AT_TILES)]
            with pe.Fori(0, KT) as n:
                for q in range(4):
                    pe.wait_ge(*(A.before(f"gate{q}", n) if q < 2 else V.before(f"mul{q - 2}", n)))
                    block_ready(pe, st.b0 + q, n, 4)
                    hi, lo = ((h_hi, h_lo), (h_hi, h_lo), (lambda t: YAHI[:, t, :], lambda t: YALO[:, t, :]),
                              (lambda t: YBHI[:, t, :], lambda t: YBLO[:, t, :]))[q]
                    product(pe, bank[q], (st.b0 + q) % 2, ALLB if q == 3 else ALLK, hi, lo, WHOLE).then_inc(k.blocks_used, 1)

        def merge_scalar(act, st):
            A, V = st.act, st.dve
            st.enter(act, "act")
            act.dma_start(XC[:, :, :], ctxT).then_inc(ctx_in, 16)
            act.dma_start(TRIG[:, :], trig[:, 0:SC["total"]]).then_inc(trig_in, 16)
            act.dma_start(SIN[:, :], trig[:, SC["total"]:]).then_inc(sin_in, 16)
            with act.Fori(0, KT) as n:
                for q in range(4):
                    block_out(act, st.b0 + q, n, 4)
                    round_block(act, st.b0 + q + 2, n, 4)
                    if q < 2:
                        act.wait_ge(*V.before(f"mul{q}", n))
                        act.activation(GAB[:, q, :], bank[q], ACT.Sigmoid, bias=col("b_gate", n + q * KT)).then_inc(*A.inc(f"gate{q}"))
                act.wait_ge(*V.at("sum", n))
                act.activation(MHI[:, n, :], MF[:, :], ACT.Copy).then_inc(*A.inc("hi"))

        def merge_vector(dve, st):
            A, V = st.act, st.dve
            st.enter(dve, "dve")
            with dve.Fori(0, KT) as n:
                for q in range(2):
                    block_out(dve, st.b0 + 2 + q, n, 4)
                    dve.wait_ge(*V.before("lo", n))
                    dve.wait_ge(*A.at(f"gate{q}", n))
                    dve.tensor_tensor(PAB[:, q, :], bank[2 + q], GAB[:, q, :], ALU.mult).then_inc(*V.inc(f"mul{q}"))
                dve.wait_ge(*V.at("mul1", n))
                dve.tensor_tensor(MF[:, :], PAB[:, 0, :], PAB[:, 1, :], ALU.add).then_inc(*V.inc("sum"))
                dve.wait_ge(*A.at("hi", n))
                dve.tensor_tensor(MLO[:, n, :], MF[:, :], MHI[:, n, :].bitcast(F32), ALU.subtract).then_inc(*V.inc("lo"))

        def out_tensor(pe, st):
            st.enter(pe, "pe")
            with pe.Fori(0, KT // 2) as i:
                for n in range(2):
                    pe.wait_ge(*st.dve.before(f"x{n}", i))
                    block_ready(pe, st.b0 + n, i, 2)
                    product(pe, bank[4 + n], (st.b0 + n) % 2, ALLK, lambda t: MHI[:, t, :], lambda t: MLO[:, t, :], WHOLE)\
                        .then_inc(k.blocks_used, 1)

        def out_scalar(act, st):
            with act.Fori(0, KT // 2) as i:
                for n in range(2):
                    round_block(act, st.b0 + n + 2, i, 2)

        def out_vector(dve, st):
            st.enter(dve, "dve")
            with dve.Fori(0, KT // 2) as i:
                for n in range(2):
                    block_out(dve, st.b0 + n, i, 2)
                    dve.tensor_tensor(X[:, i * 2 + n, :], bank[4 + n], X[:, i * 2 + n, :], ALU.add).then_inc(*st.dve.inc(f"x{n}"))

        class Layer:
            def __init__(self, l):
                self.l, self.last = l, l == LAYERS - 1
                self.width = T if self.last else TT
                self.parts = [(0, T)] if self.last else [(0, T), (T, TC)]
                l0 = l * MOD_TILES
                self.gain = Stage(k, 0, (), (), ("gain",))
                self.norm = Norm((SQ4B, HFB, STDB, RSTDB), *[
                    ((lambda t, src=src: src[:, t, :]), n, (lambda t, at=at, n=n: H2HI[:, t, at:at + n]),
                     (lambda t, at=at, n=n: H2LO[:, t, at:at + n]), (lambda t, c=c: MG[:, t, c:c + 1]),
                     (lambda t, c=c: MOD[:, l0 + t, c:c + 1])) for c, (src, at, n) in enumerate(((X, 0, T), (XC, T, TC)))])
                pe, act, dve = self.win_steps()
                self.win = Stage(k, len(WIN2), pe, act, dve)
                self.gate = Stage(k, 2, (), ("gate0", "gate1"), (), GATE2_BLOCKS // 2)
                self.taps = Stage(k, 0, (), (), ["first0", "first1", "bias0", "bias1"])
                self.tap = Stage(k, 0, (), (), ["tap0", "tap1"], CONV_K - 1)
                pe, act, dve = self.small_steps()
                self.small = Stage(k, SMALL2_BLOCKS, pe, act, dve)
                pe, act, dve = self.heads_steps()
                self.heads = Stage(k, 0, pe, act, dve, GQA_HEADS // GQA_KV)
                self.merge = Stage(k, 0, [f"tr{n}" for n in range(6)], [f"hi{n}" for n in range(8)],
                                   [s for n in range(8) for s in (f"y{n}", f"lo{n}")])
                self.out = Stage(k, 2, (), (), ("x0", "x1") if self.last else ("x0", "c0", "x1", "c1"), KT // 2)

            def parts_of(self, t):
                return [(0, T, t % 2)] + ([(T, TC, 2 + t % 2)] if not self.last or WIN2[t] in ("mkv", "kr", "gk", "gv") else [])

            def tokens(self, t):
                return sum(n for _, n, _ in self.parts_of(t))

            NORMED = (("mq", (0, 1)), ("mkv", (2,)), ("gk", (4,)), ("gq0", (6,)), ("gq1", (7,)), ("gq2", (8,)))

            def win_plan(self):
                return {2: ["sum mq"], 3: ["sum mkv"], 5: ["sum gk"], 6: ["gv tokens", "swap gk"], 7: ["sum gq0"],
                        8: ["swap gq0", "sum gq1"], 9: ["swap gq1", "sum gq2"], 11: ["swap gq2"]}

            def win_steps(self):
                pe = [s for t in range(len(WIN2)) for s in self.win_plan().get(t, ())]
                act, dve = [], ["pads"]
                norm_of = {ts[-1]: name for name, ts in self.NORMED}
                for t, tile in enumerate(WIN2):
                    act += [f"copy{t}"] + ([f"sq{t}"] if tile not in ("kr", "gv", "ca0", "cg0", "ca1", "cg1") else [])
                    for s in self.win_plan().get(t, ()):
                        kind, name = s.split(" ")
                        if kind == "sum":
                            act += [f"sd {name}"]
                            dve += [f"ri {name}"]
                            if name == "mq":
                                dve += ["f mq0", "f mq1", "lo mq"]
                                act += ["hi mq"]
                            else:
                                dve += [f"f {name}"] + (["lo mkv"] if name == "mkv" else [])
                                act += ["hi mkv"] if name == "mkv" else []
                        elif kind == "swap":
                            dve += [f"{n} {name}" for n in ("cos", "sin", "rope")]
                            act += [f"ctx {name}"] if name == "gk" or not self.last else []
                        else:
                            dve += ["gv tokens"]
                    if tile == "kr":
                        dve += ["kr sin", "kr cos", "kr rope", "kr ctx"]
                    if tile in ("cg0", "cg1"):
                        dve += [tile]
                return pe, act, dve

            def small_steps(self):
                pe, act, dve = [], [], []
                for h in range(MLA_HEADS):
                    pe, dve = pe + [f"q{h}"], dve + [f"q{h}"]
                for h in range(MLA_HEADS):
                    pe, act, dve = pe + [f"kn{h}"], act + [f"kn{h}"], dve + [f"kr{h}"]
                for b in range(KB):
                    pe, act = pe + [f"v{b}"], act + [f"v{b}"]
                pe += ["mean", "var", "pw0", "pw1"]
                act += ["sq", "sd", "silu0", "silu1", "hi", "pw0", "pw1"]
                dve += ["dev", "ri", "normed", "lo"]
                return pe, act, dve

            def units(self):
                return [(kind, a, qb) for kind in ("mla", "gqa") for a in range(2) for qb in range(BLOCKS if self.last else KB)]

            def heads_steps(self):
                n = len(self.units())
                pe, act, dve = ["sc0"], [], ["q", "mx0", "nm0"]
                for u in range(n):
                    if u:
                        dve += [f"ri{u - 1}"]
                    if u + 1 < n:
                        pe, dve = pe + [f"sc{u + 1}"], dve + [f"mx{u + 1}", f"nm{u + 1}"]
                    act += [f"ex{u}"]
                    if u:
                        pe += [f"pv{u - 1}"]
                    pe += [f"tr{u}"]
                    act += [f"pt{u}"]
                    dve += [f"pt{u}"]
                    if u:
                        dve += [f"o{u - 1}"]
                return pe + [f"pv{n - 1}"], act, dve + [f"ri{n - 1}", f"o{n - 1}"]

        sa = Area(0)
        H2HI, H2LO = sa("H2HI", [P, KT, TT], F32R), sa("H2LO", [P, KT, TT], F32R)
        after_h2 = sa.at
        KAG, VAG = sa("KAG", [P, TT]), sa("VAG", [P, KB, GQA_KV, HD])
        QAG = sa("QAG", [P, GQA_HEADS // GQA_KV, TT])
        gates_at = sa.at
        GATES = sa("GATES", [P, Y_TILES, TT])
        CW = HALO + T + HALO + TC + HALO
        SPAN = T + HALO + TC
        cin_at = sa.at
        CIN = sa("CIN", [P, 2, CW + 3])
        cacc_at = sa.at
        CACC = sa("CACC", [P, 2, SPAN + 1])
        ranks_at = sa.at
        CQHI, CQLO = sa("CQHI", [P, 2, TT], F32R), sa("CQLO", [P, 2, TT], F32R)
        CKHI, CKLO = sa("CKHI", [P, TT], F32R), sa("CKLO", [P, TT], F32R)
        KR = sa("KR", [P, TT])
        work_at = sa.at
        RW, SQ2, RN = sa("RW", [P, 4, TT]), sa("SQ2", [P, 2, TT]), sa("RN", [P, 2, TT])
        assert sa.at <= xc_at - 4 * T, (sa.at, xc_at)
        sn = Area(gates_at)
        SQ4B, HFB, STDB, RSTDB = sn("SQ4B", [P, 4, T]), sn("HFB", [P, 4, T]), sn("STDB", [P, T]), sn("RSTDB", [P, T])
        assert sn.at <= cin_at
        sh = Area(0)
        KAM, QAM = sh("KAM", [P, MLA_HEADS, TT]), sh("QAM", [P, MLA_HEADS, TT])
        VAM = sh("VAM", [P, KB, MLA_HEADS, HD])
        assert sh.at <= after_h2
        CHI2, CLO2 = place("CHI2", [P, 2, TT], work_at + 8 * TT, F32R), place("CLO2", [P, 2, TT], cin_at, F32R)
        YC = place("YC", [P, 2, TT], cacc_at)
        sw = Area(work_at)
        PX, PTS, QST = sw("PX", [P, 2, TT]), sw("PTS", [P, 2, TT]), sw("QST", [P, 3, TT])
        assert sw.at <= sa.at
        OT = place("OT", [P, KB, MLA_HEADS + GQA_HEADS, HD], ranks_at)
        assert ranks_at + 4 * KB * (MLA_HEADS + GQA_HEADS) * HD <= work_at
        YHI, YLO = place("YHI", [P, Y_TILES, TT], 0, F32R), place("YLO", [P, Y_TILES, TT], 4 * Y_TILES * TT, F32R)
        YF = place("YF", [P, 2, TT], work_at)

        def gain_vector(dve, L):
            st = L.gain
            st.enter(dve, "dve")
            for c in range(2):
                at = L.l * MOD_TILES + KT
                ins = dve.scalar_tensor_tensor(out=MG[:, :, c:c + 1], in0=MOD[:, at:at + KT, c:c + 1], scalar=1.0,
                                               in1=VEC[:, COL[f"norm{L.l}"]:COL[f"norm{L.l}"] + KT].rearrange("p (t o) -> p t o", o=1),
                                               op0=ALU.add, op1=ALU.mult)
            ins.then_inc(*st.dve.inc("gain"))
            dve.wait_ge(*st.dve.at("gain"))

        NORM_AT = {name: n for n, (name, _) in enumerate(Layer.NORMED)}
        SQ_SLOT = {0: 0, 1: 1, 2: 0, 4: 1, 6: 0, 7: 1, 8: 0}

        def win_tensor(pe, L):
            st = L.win
            A, V, S = st.act, st.dve, st.pe
            st.enter(pe, "pe")
            for t in range(len(WIN2)):
                if t >= 2:
                    pe.wait_ge(*A.at(f"copy{t - 2}"))
                    if f"sq{t - 2}" in A.index:
                        pe.wait_ge(*A.at(f"sq{t - 2}"))
                block_ready(pe, st.b0 + t)
                for at, n, b in L.parts_of(t):
                    mm = product(pe, bank[b][:, 0:n], (st.b0 + t) % 2, ALLK, lambda u: H2HI[:, u, at:at + n],
                                 lambda u: H2LO[:, u, at:at + n], WHOLE)
                mm.then_inc(k.blocks_used, 1)
                for s in L.win_plan().get(t, ()):
                    kind, name = s.split(" ")
                    if kind == "sum":
                        i = NORM_AT[name]
                        tiles_of = Layer.NORMED[i][1]
                        if i:
                            pe.wait_ge(*A.at(f"sd {Layer.NORMED[i - 1][0]}"))
                        pe.wait_ge(*A.at(f"sq{tiles_of[-1]}"))
                        for at, n, b in L.parts_of(tiles_of[0]):
                            for m, tt in enumerate(tiles_of):
                                mm = pe.matmul(bank[4 + b // 2][:, 0:n], ones if name in ("mq", "mkv") else heads,
                                               SQ2[:, SQ_SLOT[tt], at:at + n], start=m == 0, stop=m == len(tiles_of) - 1)
                    elif kind == "swap":
                        tile = Layer.NORMED[NORM_AT[name]][1][0]
                        pe.wait_ge(*V.at(f"f {name}"))
                        pe.wait_ge(*V.at("gv tokens" if name == "gk" else f"sin {Layer.NORMED[NORM_AT[name] - 1][0]}"))
                        mm = pe.matmul(bank[6], TRIG[:, SC["swap"]:SC["swap"] + P], RW[:, tile % 4, 0:T], start=True, stop=True)
                    else:
                        pe.wait_ge(*A.at("copy5"))
                        for b in range(KB):
                            mm = pe.transpose(two_banks[3][:, b * P:(b + 1) * P], RW[:, 5 % 4, b * P:(b + 1) * P], eye)
                    mm.then_inc(*S.inc(s))

        RW_LAST = {0: ("dve", "lo mq"), 1: ("dve", "lo mq"), 2: ("dve", "lo mkv"), 3: ("dve", "kr ctx"), 4: ("act", "ctx gk"),
                   5: ("pe", "gv tokens"), 6: ("dve", "rope gq0"), 7: ("dve", "rope gq1"), 8: ("dve", "rope gq2")}

        def win_scalar(act, L):
            st = L.win
            A, V, S = st.act, st.dve, st.pe
            st.enter(act, "act")
            for t, tile in enumerate(WIN2):
                block_out(act, st.b0 + t)
                round_block(act, st.b0 + t + 2)
                if t >= 4:
                    eng, name = RW_LAST[t - 4]
                    act.wait_ge(*{"dve": V, "pe": S, "act": A}[eng].at(name))
                    if t - 4 in (6, 7, 8) and not L.last:
                        act.wait_ge(*A.at(f"ctx {WIN2[t - 4]}"))
                    if t - 4 == 4:
                        act.wait_ge(*V.at("rope gk"))
                for at, n, b in L.parts_of(t):
                    ins = act.activation(RW[:, t % 4, at:at + n], bank[b][:, 0:n], ACT.Sigmoid if tile in ("cg0", "cg1") else ACT.Copy)
                ins.then_inc(*A.inc(f"copy{t}"))
                if t in SQ_SLOT:
                    users = [ts for _, ts in Layer.NORMED]
                    before = [u for u in range(t) if SQ_SLOT.get(u) == SQ_SLOT[t]]
                    if before:
                        name = [nm for nm, ts in Layer.NORMED if before[-1] in ts][0]
                        act.wait_ge(*S.at(f"sum {name}"))
                    for at, n, b in L.parts_of(t):
                        ins = act.activation(SQ2[:, SQ_SLOT[t], at:at + n], bank[b][:, 0:n], ACT.Square)
                    ins.then_inc(*A.inc(f"sq{t}"))
                for s in L.win_plan().get(t, ()):
                    kind, name = s.split(" ")
                    if kind == "sum":
                        i = NORM_AT[name]
                        t0 = Layer.NORMED[i][1][0]
                        act.wait_ge(*S.at(s))
                        if i >= 2:
                            prev = Layer.NORMED[i - 2][0]
                            act.wait_ge(*V.at(f"rope {prev}" if prev[0] == "g" else f"lo {prev}"))
                        size = {"mq": MLA_Q_RANK, "mkv": MLA_KV_RANK}.get(name, HD)
                        for at, n, b in L.parts_of(t0):
                            ins = act.activation(RN[:, i % 2, at:at + n], bank[4 + b // 2][:, 0:n], ACT.Sqrt, scale=1.0 / size, bias=EPS[:, 0:1])
                        ins.then_inc(*A.inc(f"sd {name}"))
                        w = L.tokens(t0)
                        if name == "mq":
                            act.wait_ge(*V.at("f mq1"))
                            act.activation(CQHI[:, :, 0:w], RW[:, 0:2, 0:w], ACT.Copy).then_inc(*A.inc("hi mq"))
                        if name == "mkv":
                            act.wait_ge(*V.at("f mkv"))
                            act.activation(CKHI[:, 0:w], RW[:, 2, 0:w], ACT.Copy).then_inc(*A.inc("hi mkv"))
                    elif kind == "swap" and (name == "gk" or not L.last):
                        tile_at = Layer.NORMED[NORM_AT[name]][1][0]
                        act.wait_ge(*V.at(f"f {name}"))
                        dst = KAG[:, T:] if name == "gk" else QAG[:, int(name[2]), T:]
                        act.activation(dst, RW[:, tile_at % 4, T:], ACT.Copy).then_inc(*A.inc(f"ctx {name}"))

        def win_vector(dve, L):
            st = L.win
            A, V, S = st.act, st.dve, st.pe
            l = L.l
            st.enter(dve, "dve")
            if L.l == 0:
                dve.wait_ge(trig_in, 16)
                dve.wait_ge(sin_in, 16)
            dve.memset(CIN[:, :, :], 0.0).then_inc(*V.inc("pads"))
            for t, tile in enumerate(WIN2):
                for s in L.win_plan().get(t, ()):
                    kind, name = s.split(" ")
                    if kind == "tokens" or s == "gv tokens":
                        dve.wait_ge(*S.at(s))
                        dve.tensor_copy(VAG[:, :, :, :].rearrange("p b g n -> p (b g n)"), two_banks[3][:, 0:TT]).then_inc(*V.inc(s))
                        continue
                    i = NORM_AT[name]
                    tiles_of = Layer.NORMED[i][1]
                    w = L.tokens(tiles_of[0])
                    rn = RN[:, i % 2, :]
                    if kind == "sum":
                        dve.wait_ge(*A.at(f"sd {name}"))
                        dve.reciprocal(rn[:, 0:w], rn[:, 0:w]).then_inc(*V.inc(f"ri {name}"))
                        dve.wait_ge(*V.at(f"ri {name}"))
                        for m, tt in enumerate(tiles_of):
                            rw = RW[:, tt % 4, 0:w]
                            gain = col(f"mla_q{l}", m) if name == "mq" else col(f"mla_kv{l}") if name == "mkv" else col(f"gqa_{name[1]}{l}")
                            dve.scalar_tensor_tensor(out=rw, in0=rw, scalar=gain, in1=rn[:, 0:w], op0=ALU.mult, op1=ALU.mult)\
                               .then_inc(*V.inc(f"f mq{m}" if name == "mq" else f"f {name}"))
                        if name in ("mq", "mkv"):
                            src, hi, lo = ((RW[:, 0:2, 0:w], CQHI[:, :, 0:w], CQLO[:, :, 0:w]) if name == "mq" else
                                           (RW[:, 2, 0:w], CKHI[:, 0:w], CKLO[:, 0:w]))
                            dve.wait_ge(*A.at(f"hi {name}"))
                            dve.tensor_tensor(lo, src, hi.bitcast(F32), ALU.subtract).then_inc(*V.inc(f"lo {name}"))
                    else:
                        rw = RW[:, tiles_of[0] % 4, 0:T]
                        dst = KAG[:, 0:T] if name == "gk" else QAG[:, int(name[2]), 0:T]
                        dve.wait_ge(*V.at(f"f {name}"))
                        dve.tensor_tensor(dst, rw, TRIG[:, SC["cos"]:SC["cos"] + T], ALU.mult).then_inc(*V.inc(f"cos {name}"))
                        dve.wait_ge(*S.at(s))
                        dve.tensor_tensor(rn[:, 0:T], bank[6], SIN[:, :], ALU.mult).then_inc(*V.inc(f"sin {name}"))
                        dve.wait_ge(*V.at(f"sin {name}"))
                        dve.tensor_tensor(dst, dst, rn[:, 0:T], ALU.add).then_inc(*V.inc(f"rope {name}"))
                if tile == "kr":
                    lo, up = slice(0, HD), slice(HD, P)
                    trig_of = lambda s: TRIG[s, SC["kr"]:SC["kr"] + T]
                    dve.wait_ge(*A.at(f"copy{t}"))
                    dve.tensor_tensor(KR[up, 0:T], RW[lo, t % 4, 0:T], trig_of(lo), ALU.mult).then_inc(*V.inc("kr sin"))
                    dve.tensor_tensor(RW[up, t % 4, 0:T], RW[up, t % 4, 0:T], trig_of(up), ALU.mult).then_inc(*V.inc("kr cos"))
                    dve.wait_ge(*V.at("kr cos"))
                    dve.tensor_tensor(KR[up, 0:T], KR[up, 0:T], RW[up, t % 4, 0:T], ALU.add).then_inc(*V.inc("kr rope"))
                    dve.tensor_copy(KR[up, T:], RW[up, t % 4, T:]).then_inc(*V.inc("kr ctx"))
                if tile in ("cg0", "cg1"):
                    dve.wait_ge(*A.at(f"copy{t}"))
                    dve.wait_ge(*V.at("pads"))
                    for at, n, _ in L.parts_of(t):
                        to = HALO + at + (HALO if at else 0)
                        ins = dve.tensor_tensor(CIN[:, int(tile[2]), to:to + n], RW[:, (t - 1) % 4, at:at + n], RW[:, t % 4, at:at + n], ALU.mult)
                    ins.then_inc(*V.inc(tile))

        def gate_tensor(pe, L):
            st = L.gate
            st.enter(pe, "pe")
            with pe.Fori(0, GATE2_BLOCKS // 2) as i:
                for n in range(2):
                    pe.wait_ge(*st.act.before(f"gate{n}", i))
                    block_ready(pe, st.b0 + n, i, 2)
                    for at, w in L.parts:
                        mm = product(pe, bank[n + (2 if at else 0)][:, 0:w], (st.b0 + n) % 2, ALLK, lambda u: H2HI[:, u, at:at + w],
                                     lambda u: H2LO[:, u, at:at + w], WHOLE)
                    mm.then_inc(k.blocks_used, 1)

        def gate_scalar(act, L):
            st = L.gate
            st.enter(act, "act")
            with act.Fori(0, GATE2_BLOCKS // 2) as i:
                for n in range(2):
                    block_out(act, st.b0 + n, i, 2)
                    round_block(act, st.b0 + n + 2, i, 2)
                    for at, w in L.parts:
                        ins = act.activation(GATES[:, i * 2 + n, at:at + w], bank[n + (2 if at else 0)][:, 0:w], ACT.Silu)
                    ins.then_inc(*st.act.inc(f"gate{n}"))

        def taps_vector(dve, L):
            l, V = L.l, L.taps.dve
            span = T if L.last else SPAN
            L.taps.enter(dve, "dve")
            for i in range(2):
                dve.tensor_scalar(CACC[:, i, 0:span], CIN[:, i, 0:span], col(f"dw_w{l}", i * CONV_K), None, ALU.mult)\
                   .then_inc(*V.inc(f"first{i}"))
            for i in range(2):
                dve.wait_ge(*V.at(f"first{i}"))
                dve.tensor_scalar(CACC[:, i, 0:span], CACC[:, i, 0:span], col(f"dw_b{l}", i), None, ALU.add).then_inc(*V.inc(f"bias{i}"))
            V = L.tap.dve
            with dve.Fori(0, CONV_K - 1) as s:
                for i in range(2):
                    dve.wait_ge(*V.before(f"tap{i}", s))
                    dve.scalar_tensor_tensor(out=CACC[:, i, 0:span], in0=CIN[:, i, bass.ds(s + 1, span)],
                                             scalar=col(f"dw_w{l}", s + (i * CONV_K + 1)), in1=CACC[:, i, 0:span],
                                             op0=ALU.mult, op1=ALU.add).then_inc(*V.inc(f"tap{i}"))

        def conv_parts(L):
            return [(0, T, 0)] if L.last else [(0, T, 0), (T, TC, T + HALO)]

        def small_tensor(pe, L):
            st = L.small
            A, V, S = st.act, st.dve, st.pe
            st.enter(pe, "pe")
            done = -1
            def ready(idx):
                nonlocal done
                b = idx // UNITS
                if b != done:
                    block_ready(pe, st.b0 + b)
                    done = b
                return (st.b0 + b) % 2
            def used(mm, idx, name):
                mm.then_inc(*S.inc(name))
                if idx % UNITS == UNITS - 1 or idx == V0 + 2:
                    pe.wait_ge(*S.at(name))
                    pe.sem_inc(k.blocks_used)
            parts = [(at, w) for at, w in L.parts]
            for h in range(MLA_HEADS):
                idx = UQ0 + 2 * h
                slot = ready(idx)
                if h >= 2:
                    pe.wait_ge(*V.at(f"q{h - 2}"))
                for at, w in parts:
                    mm = product(pe, bank[h % 2 + (2 if at else 0)][:, 0:w], slot, [(idx % UNITS + t, t) for t in range(2)],
                                 lambda t: CQHI[:, t, at:at + w], lambda t: CQLO[:, t, at:at + w], WHOLE)
                used(mm, idx + 1, f"q{h}")
            for h in range(MLA_HEADS):
                idx = KN0 + h
                slot = ready(idx)
                if h >= 2:
                    pe.wait_ge(*A.at(f"kn{h - 2}"))
                for at, w in ((0, T), (T, TC)):
                    mm = product(pe, bank[4 + h % 2 + (2 if at else 0)][:, 0:w], slot, [(idx % UNITS, 0)],
                                 lambda t: CKHI[:, at:at + w], lambda t: CKLO[:, at:at + w], WHOLE)
                used(mm, idx, f"kn{h}")
            slot = ready(V0)
            u0 = V0 % UNITS
            nv = MLA_HEADS * MLA_V
            for b in range(KB):
                pe.wait_ge(*(V.at(f"q{4 + b}") if b < 2 else A.at(f"v{b - 2}")))
                out = bank[b % 2][:, 0:nv]
                toks = slice(b * P, (b + 1) * P)
                pe.matmul(out, CKHI[:, toks], WHI[:, slot, u0 * P:u0 * P + nv], start=True, stop=False)
                pe.matmul(out, CKLO[:, toks], WHI[:, slot, u0 * P:u0 * P + nv], start=False, stop=False)
                mm = pe.matmul(out, CKHI[:, toks], WLO[:, slot, u0 * P:u0 * P + nv], start=False, stop=True)
                if b < KB - 1:
                    mm.then_inc(*S.inc(f"v{b}"))
                else:
                    used(mm, V0 + 2, f"v{b}")
            cp = conv_parts(L)
            pe.wait_ge(*A.at(f"kn{MLA_HEADS - 1}"))
            for name, src, b0 in (("mean", CACC, 4), ("var", SQ2, 6)):
                if name == "var":
                    pe.wait_ge(*A.at("sq"))
                for m, (at, n, place_at) in enumerate(cp):
                    for i in range(2):
                        mm = pe.matmul(bank[b0 + m][:, 0:n], ones, src[:, i, (place_at if name == "mean" else at):][:, 0:n],
                                       start=i == 0, stop=i == 1)
                mm.then_inc(*S.inc(name))
            slot = ready(PW0)
            pe.wait_ge(*A.at(f"v{KB - 1}"))
            pe.wait_ge(*V.at("lo"))
            for i in range(2):
                for m, (at, n, _) in enumerate(cp):
                    mm = product(pe, bank[i + 2 * m][:, 0:n], slot, [(2 * i + t, t) for t in range(2)],
                                 lambda t: CHI2[:, t, at:at + n], lambda t: CLO2[:, t, at:at + n], WHOLE)
                mm.then_inc(*S.inc(f"pw{i}"))
            pe.wait_ge(*S.at("pw1"))
            pe.sem_inc(k.blocks_used)

        def small_scalar(act, L):
            st = L.small
            A, V, S = st.act, st.dve, st.pe
            l = L.l
            st.enter(act, "act")
            cp = conv_parts(L)
            round_block(act, st.b0 + 2)
            for h in range(MLA_HEADS):
                act.wait_ge(*S.at(f"kn{h}"))
                if h == KN0 + MLA_HEADS - 1 - KN0:
                    round_block(act, st.b0 + 3)
                for at, w, b in ((0, T, 4), (T, TC, 6)):
                    ins = act.activation(KAM[0:MLA_NOPE, h, at:at + w], bank[b + h % 2][0:MLA_NOPE, 0:w], ACT.Copy)
                ins.then_inc(*A.inc(f"kn{h}"))
            nv = MLA_HEADS * MLA_V
            for b in range(KB):
                act.wait_ge(*S.at(f"v{b}"))
                act.activation(VAM[:, b, :, :].rearrange("p h n -> p (h n)"), bank[b % 2][:, 0:nv], ACT.Copy).then_inc(*A.inc(f"v{b}"))
            round_block(act, st.b0 + 4)
            act.wait_ge(*V.at("dev"))
            for at, n, place_at in cp:
                ins = act.activation(SQ2[:, :, at:at + n], CACC[:, :, place_at:place_at + n], ACT.Square)
            ins.then_inc(*A.inc("sq"))
            act.wait_ge(*S.at("var"))
            for m, (at, n, _) in enumerate(cp):
                ins = act.activation(RN[:, 0, at:at + n], bank[6 + m][:, 0:n], ACT.Sqrt, scale=1.0 / CONV_CH, bias=EPS[:, 0:1])
            ins.then_inc(*A.inc("sd"))
            act.wait_ge(*V.at("normed"))
            for i in range(2):
                for at, n, place_at in cp:
                    ins = act.activation(RW[:, i, at:at + n], CACC[:, i, place_at:place_at + n], ACT.Silu,
                                         scale=col(f"cln_w{l}", i), bias=col(f"cln_b{l}", i))
                ins.then_inc(*A.inc(f"silu{i}"))
            act.wait_ge(*A.at("silu1"))
            act.activation(CHI2[:, :, 0:L.width], RW[:, 0:2, 0:L.width], ACT.Copy).then_inc(*A.inc("hi"))
            for i in range(2):
                act.wait_ge(*S.at(f"pw{i}"))
                for m, (at, n, _) in enumerate(cp):
                    ins = act.activation(YC[:, i, at:at + n], bank[i + 2 * m][:, 0:n], ACT.Identity, bias=col(f"pw_b{l}", i))
                ins.then_inc(*A.inc(f"pw{i}"))
            round_block(act, st.b0 + 5)

        def small_vector(dve, L):
            st = L.small
            A, V, S = st.act, st.dve, st.pe
            st.enter(dve, "dve")
            up = slice(MLA_NOPE, P)
            for h in range(MLA_HEADS):
                dve.wait_ge(*S.at(f"q{h}"))
                for at, w in L.parts:
                    ins = dve.tensor_tensor(QAM[:, h, at:at + w], bank[h % 2 + (2 if at else 0)][:, 0:w],
                                            TRIG[:, SC["mla"] + at:SC["mla"] + at + w], ALU.mult)
                ins.then_inc(*V.inc(f"q{h}"))
            for h in range(MLA_HEADS):
                dve.tensor_copy(KAM[up, h, :], KR[up, :]).then_inc(*V.inc(f"kr{h}"))
            cp = conv_parts(L)
            two = lambda t: t.rearrange("p (o n) -> p o n", o=1).to_broadcast([P, 2, t.shape[1]])
            dve.wait_ge(*S.at("mean"))
            for m, (at, n, place_at) in enumerate(cp):
                c = CACC[:, :, place_at:place_at + n]
                ins = dve.scalar_tensor_tensor(out=c, in0=two(bank[4 + m][:, 0:n]), scalar=-1.0 / CONV_CH, in1=c, op0=ALU.mult, op1=ALU.add)
            ins.then_inc(*V.inc("dev"))
            dve.wait_ge(*A.at("sd"))
            dve.reciprocal(RN[:, 0, 0:L.width], RN[:, 0, 0:L.width]).then_inc(*V.inc("ri"))
            dve.wait_ge(*V.at("ri"))
            for m, (at, n, place_at) in enumerate(cp):
                c = CACC[:, :, place_at:place_at + n]
                ins = dve.tensor_tensor(c, c, two(RN[:, 0, at:at + n]), ALU.mult)
            ins.then_inc(*V.inc("normed"))
            dve.wait_ge(*A.at("hi"))
            dve.tensor_tensor(CLO2[:, :, 0:L.width], RW[:, 0:2, 0:L.width], CHI2[:, :, 0:L.width].bitcast(F32), ALU.subtract)\
               .then_inc(*V.inc("lo"))

        def keys_of(qb):
            return range(KB) if qb < BLOCKS else range(BLOCKS, KB)

        def scale_of(kind):
            return (MLA_NOPE + MLA_ROPE if kind == "mla" else HD) ** -0.5

        def heads_tensor(pe, L):
            st = L.heads
            A, V, S = st.act, st.dve, st.pe
            us = L.units()
            st.enter(pe, "pe")
            with pe.Fori(0, st.times) as i:
                def scores(u):
                    kind, a, qb = us[u]
                    pe.wait_ge(*(V.at("q", i) if u < 2 else A.at(f"ex{u - 2}", i)))
                    pe.sem_inc(tensor_ready)
                    for at, w in ((0, T), (T, TC)):
                        if qb >= BLOCKS and not at:
                            continue
                        hs = slice(a * HD, a * HD + HD)
                        lhs, rhs = ((QST[:, a, qb * P:(qb + 1) * P], KAM[:, i * 2 + a, at:at + w]) if kind == "mla" else
                                    (QST[hs, 2, qb * P:(qb + 1) * P], KAG[hs, at:at + w]))
                        mm = pe.matmul(two_banks[u % 2][:, at:at + w], lhs, rhs, start=True, stop=True)
                    mm.then_inc(*S.inc(f"sc{u}"))
                def values(u):
                    kind, a, qb = us[u]
                    pe.wait_ge(*V.at(f"pt{u}", i))
                    pe.wait_ge(*A.at(f"pt{u}", i))
                    pe.sem_inc(tensor_ready)
                    ks = keys_of(qb)
                    for b in ks:
                        rhs = VAM[:, b, i * 2 + a, :] if kind == "mla" else VAG[:, b, a, :]
                        mm = pe.matmul(two_banks[2 + u % 2][:, TT:TT + HD], PTS[:, u % 2, b * P:(b + 1) * P], rhs,
                                       start=b == ks[0], stop=b == ks[-1])
                    mm.then_inc(*S.inc(f"pv{u}"))
                scores(0)
                for u, (kind, a, qb) in enumerate(us):
                    if u + 1 < len(us):
                        scores(u + 1)
                    if u:
                        values(u - 1)
                    pe.wait_ge(*A.at(f"ex{u}", i))
                    if u >= 2:
                        pe.wait_ge(*V.at(f"o{u - 2}", i))
                    pe.sem_inc(tensor_ready)
                    for b in keys_of(qb):
                        mm = pe.transpose(two_banks[2 + u % 2][:, b * P:(b + 1) * P], PX[:, u % 2, b * P:(b + 1) * P], eye)
                    mm.then_inc(*S.inc(f"tr{u}"))
                values(len(us) - 1)

        def heads_scalar(act, L):
            st = L.heads
            A, V, S = st.act, st.dve, st.pe
            us = L.units()
            st.enter(act, "act")
            with act.Fori(0, st.times) as i:
                for u, (kind, a, qb) in enumerate(us):
                    c0 = 0 if qb < BLOCKS else T
                    act.wait_ge(*V.at(f"nm{u}", i))
                    if u >= 2:
                        act.wait_ge(*S.at(f"tr{u - 2}", i))
                    act.activation(PX[:, u % 2, c0:], two_banks[u % 2][:, c0:TT], ACT.Exp, scale=scale_of(kind), bias=NM2[:, u:u + 1],
                                   accum_out=DEN2[:, u:u + 1]).then_inc(*A.inc(f"ex{u}"))
                    act.wait_ge(*S.at(f"tr{u}", i))
                    if u >= 2:
                        act.wait_ge(*S.at(f"pv{u - 2}", i))
                    if qb < BLOCKS:
                        act.activation(PTS[:, u % 2, 0:T], two_banks[2 + u % 2][:, 0:T], ACT.Copy).then_inc(*A.inc(f"pt{u}"))
                    else:
                        act.sem_inc(A.inc(f"pt{u}")[0])

        def heads_vector(dve, L):
            st = L.heads
            A, V, S = st.act, st.dve, st.pe
            us = L.units()
            st.enter(dve, "dve")
            with dve.Fori(0, st.times) as i:
                dve.wait_ge(*S.before(f"sc{len(us) - 1}", i))
                dve.tensor_copy(QST[:, 0:2, 0:L.width], QAM[:, bass.ds(i * 2, 2), 0:L.width])
                dve.tensor_copy(QST[:, 2, 0:L.width], QAG[:, i, 0:L.width]).then_inc(*V.inc("q"))
                def largest(u):
                    kind, a, qb = us[u]
                    dve.wait_ge(*S.at(f"sc{u}", i))
                    dve.tensor_reduce(MX2[:, u:u + 1], two_banks[u % 2][:, (0 if qb < BLOCKS else T):TT], AX, ALU.max).then_inc(*V.inc(f"mx{u}"))
                    dve.wait_ge(*V.at(f"mx{u}", i))
                    dve.tensor_scalar(NM2[:, u:u + 1], MX2[:, u:u + 1], -scale_of(kind), None, ALU.mult).then_inc(*V.inc(f"nm{u}"))
                def inverse(u):
                    dve.wait_ge(*A.at(f"ex{u}", i))
                    dve.reciprocal(DEN2[:, u:u + 1], DEN2[:, u:u + 1]).then_inc(*V.inc(f"ri{u}"))
                def result(u):
                    kind, a, qb = us[u]
                    head = a + i * 2 + (MLA_HEADS if kind == "gqa" else 0)
                    dve.wait_ge(*V.at(f"ri{u}", i))
                    dve.wait_ge(*S.at(f"pv{u}", i))
                    dve.tensor_scalar(OT[:, qb, head, :], two_banks[2 + u % 2][:, TT:TT + HD], DEN2[:, u:u + 1], None, ALU.mult)\
                       .then_inc(*V.inc(f"o{u}"))
                largest(0)
                for u in range(len(us)):
                    if u:
                        inverse(u - 1)
                    if u + 1 < len(us):
                        largest(u + 1)
                    dve.wait_ge(*S.at(f"tr{u}", i))
                    dve.tensor_copy(PTS[:, u % 2, T:], two_banks[2 + u % 2][:, T:TT]).then_inc(*V.inc(f"pt{u}"))
                    if u:
                        result(u - 1)
                inverse(len(us) - 1)
                result(len(us) - 1)

        def gated_tensor(pe, L):
            st = L.merge
            st.enter(pe, "pe")
            for n in range(6):
                if n >= 2:
                    pe.wait_ge(*st.dve.at(f"y{n - 2}"))
                for b in range(L.width // P):
                    mm = pe.transpose(two_banks[n % 2][:, b * P:(b + 1) * P], OT[:, b, 2 * n:2 * n + 2, :].rearrange("p h n -> p (h n)"), eye)
                mm.then_inc(*st.pe.inc(f"tr{n}"))

        def gated_scalar(act, L):
            st = L.merge
            st.enter(act, "act")
            for n in range(Y_TILES):
                act.wait_ge(*st.dve.at(f"y{n}"))
                act.activation(YHI[:, n, 0:L.width], YF[:, n % 2, 0:L.width], ACT.Copy).then_inc(*st.act.inc(f"hi{n}"))

        def gated_vector(dve, L):
            st = L.merge
            st.enter(dve, "dve")
            w = L.width
            for n in range(Y_TILES):
                if n < 6:
                    dve.wait_ge(*st.pe.at(f"tr{n}"))
                if n >= 2:
                    dve.wait_ge(*st.dve.at(f"lo{n - 2}"))
                dve.tensor_tensor(YF[:, n % 2, 0:w], two_banks[n % 2][:, 0:w] if n < 6 else YC[:, n - 6, 0:w], GATES[:, n, 0:w], ALU.mult)\
                   .then_inc(*st.dve.inc(f"y{n}"))
                dve.wait_ge(*st.act.at(f"hi{n}"))
                dve.tensor_tensor(YLO[:, n, 0:w], YF[:, n % 2, 0:w], YHI[:, n, 0:w].bitcast(F32), ALU.subtract).then_inc(*st.dve.inc(f"lo{n}"))

        def out2_tensor(pe, L):
            st = L.out
            st.enter(pe, "pe")
            with pe.Fori(0, KT // 2) as i:
                for n in range(2):
                    pe.wait_ge(*st.dve.before(f"x{n}" if L.last else f"c{n}", i))
                    block_ready(pe, st.b0 + n, i, 2)
                    for at, w in L.parts:
                        mm = product(pe, bank[4 + n + (2 if at else 0)][:, 0:w], (st.b0 + n) % 2, ALLK, lambda u: YHI[:, u, at:at + w],
                                     lambda u: YLO[:, u, at:at + w], WHOLE)
                    mm.then_inc(k.blocks_used, 1)

        def out2_scalar(act, L):
            st = L.out
            full = KT // 2 - (1 if L.last else 0)
            with act.Fori(0, full) as i:
                for n in range(2):
                    round_block(act, st.b0 + n + 2, i, 2)
            if L.last:
                round_block(act, st.b0 + KT)

        def out2_vector(dve, L):
            st = L.out
            st.enter(dve, "dve")
            with dve.Fori(0, KT // 2) as i:
                for n in range(2):
                    block_out(dve, st.b0 + n, i, 2)
                    for c, (at, w) in enumerate(L.parts):
                        x = (XC if c else X)[:, i * 2 + n, :]
                        dve.scalar_tensor_tensor(out=x, in0=bank[4 + n + 2 * c][:, 0:w],
                                                 scalar=MOD[:, i * 2 + (L.l * MOD_TILES + 2 * KT + n), c:c + 1], in1=x,
                                                 op0=ALU.mult, op1=ALU.add).then_inc(*st.dve.inc(f"{'xc'[c]}{n}"))

        OUT = place("OUT", [P, KT, T], 0)
        SQF, RF = place("SQF", [P, 4, T], after_h2), place("RF", [P, 2, T], after_h2 + 16 * T)

        def final_tensor(pe, st):
            st.enter(pe, "pe")
            for t in range(KT):
                pe.wait_ge(*st.act.at(f"sq{t}"))
                pe.matmul(bank[0], ones, SQF[:, t % 4, :], start=t == 0, stop=t == KT - 1).then_inc(*st.pe.inc(f"sum{t}"))

        def final_scalar(act, st):
            st.enter(act, "act")
            for t in range(KT):
                if t >= 4:
                    act.wait_ge(*st.pe.at(f"sum{t - 4}"))
                act.activation(SQF[:, t % 4, :], X[:, t, :], ACT.Square).then_inc(*st.act.inc(f"sq{t}"))
            act.wait_ge(*st.pe.at(f"sum{KT - 1}"))
            act.activation(RF[:, 0, :], bank[0], ACT.Sqrt, scale=1.0 / D, bias=EPS[:, 0:1]).then_inc(*st.act.inc("sd"))

        def final_vector(dve, st):
            st.enter(dve, "dve")
            dve.wait_ge(*st.act.at("sd"))
            dve.reciprocal(RF[:, 1, :], RF[:, 0, :]).then_inc(*st.dve.inc("ri"))
            dve.wait_ge(*st.dve.at("ri"))
            for t in range(KT):
                dve.scalar_tensor_tensor(out=OUT[:, t, :], in0=X[:, t, :], scalar=col("final_norm", t), in1=RF[:, 1, :],
                                         op0=ALU.mult, op1=ALU.mult).then_inc(*st.dve.inc(f"out{t}"))

        cond = Stage(k, 0, (), ("silu", "hi"), ("lo",))
        ffn1 = FFN("ffn1_norm", None)
        mix = plain_norm("mix_norm")
        lora_st = Stage(k, LORA_BLOCKS, (), ("pb0", "pb1", "pb2", "tanh", "sig"), ("zero", "d0", "o0", "d1", "o1", "d2", "o2"))
        pairs_st = Stage(k, PAIR_BLOCKS, rw_pe, rw_act, rw_dve, PAIRS)
        att_in = Stage(k, ATT_BLOCKS, ain_pe, ain_act, ain_dve)
        att = Stage(k, 0, att_pe, att_act, att_dve)
        merge = Stage(k, 4, (), ("gate0", "gate1", "hi"), ("mul0", "mul1", "sum", "lo"), KT)
        way_out = Stage(k, 2, (), (), ("x0", "x1"), KT // 2)
        ffn2 = FFN("ffn2_norm", 1)
        layers = []
        for l in range(LAYERS):
            layers.append(Layer(l))
        final = Stage(k, 0, [f"sum{t}" for t in range(KT)], [f"sq{t}" for t in range(KT)] + ["sd"], ["ri"] + [f"out{t}" for t in range(KT)])
        k.planned = k.blocks

        block = ctx.enter_context(nc.Block())

        @block.sync
        def _(sp):
            sp.dma_start(VEC[:, :], vec).then_inc(vec_in, 16)
            sp.dma_start(X[:, 0:4, :], xT[:, 0:4, :]).then_inc(x_in[0], 16)
            sp.dma_start(X[:, 4:8, :], xT[:, 4:8, :]).then_inc(x_in[1], 16)
            sp.dma_start(SQC[:, :], square).then_inc(const_in, 16)
            for s in range(2):
                sp.dma_start(RAW[:, s, :], wstream[s]).then_inc(raw_full[s], 16)
            sp.dma_start(FCC[:, :], first).then_inc(first_in, 16)
            sp.dma_start(LVL[:, :, :], levels.rearrange("p (l c) -> p l c", c=CHUNK)).then_inc(levels_in, 16)
            sp.dma_start(W3[:, :, :], lora).then_inc(lora_in, 16)
            with sp.Fori(1, nblocks // 2) as i:
                for s in range(2):
                    sp.wait_ge(split, i * 2 + (s - 1))
                    sp.dma_start(RAW[:, s, :], wstream[i * 2 + s]).then_inc(raw_full[s], 16)
            for z in range(4):
                sp.wait_ge(*final.dve.at(f"out{2 * z + 1}"))
                sp.dma_start(outT[:, 2 * z:2 * z + 2, :], OUT[:, 2 * z:2 * z + 2, :]).then_inc(out_done, 16)
            sp.wait_ge(out_done, 4 * 16)

        @block.gpsimd
        def _(pool):
            pool.memset(EPS[:, 0:1], RMS_EPS).then_inc(filled, 1)
            pool.memset(EPS[:, 1:2], GN_EPS).then_inc(filled, 1)
            for s in range(2):
                pool.wait_ge(rounded, s + 1)
                pool.tensor_tensor(WLO[:, s, :], RAW[:, s, :], WHI[:, s, :].bitcast(F32), ALU.subtract).then_inc(split, 1)
            with pool.Fori(1, nblocks // 2) as i:
                for s in range(2):
                    pool.wait_ge(rounded, i * 2 + (s + 1))
                    pool.tensor_tensor(WLO[:, s, :], RAW[:, s, :], WHI[:, s, :].bitcast(F32), ALU.subtract)\
                        .then_inc(split, 1)

        @block.tensor
        def _(pe):
            pe.wait_ge(const_in, 16)
            pe.wait_ge(first_in, 16)
            ffn_tensor(pe, ffn1)
            norm_tensor(pe, mix)
            lora_tensor(pe, lora_st)
            rwkv_tensor(pe, pairs_st)
            attention_in_tensor(pe, att_in)
            attention_tensor(pe, att)
            merge_tensor(pe, merge)
            out_tensor(pe, way_out)
            ffn_tensor(pe, ffn2)
            pe.wait_ge(trig_in, 16)
            for L in layers:
                norm_tensor(pe, L.norm)
                win_tensor(pe, L)
                gate_tensor(pe, L)
                small_tensor(pe, L)
                heads_tensor(pe, L)
                gated_tensor(pe, L)
                out2_tensor(pe, L)
            final_tensor(pe, final)

        @block.scalar
        def _(act):
            act.wait_ge(vec_in, 16)
            act.wait_ge(filled, 2)
            c2 = VEC[:, COL["cond"]:COL["cond"] + 2 * KT].rearrange("p (t c) -> p t c", c=2)
            act.activation(CS[:, :, :], c2, ACT.Silu).then_inc(*cond.act.inc("silu"))
            act.wait_ge(*cond.act.at("silu"))
            act.activation(CHI[:, :, :], CS[:, :, :], ACT.Copy).then_inc(*cond.act.inc("hi"))
            round_block(act, 0)
            round_block(act, 1)
            act.wait_ge(x_in[0], 16)
            act.wait_ge(x_in[1], 16)
            ffn_scalar(act, ffn1)
            norm_scalar(act, mix)
            lora_scalar(act, lora_st)
            rwkv_scalar(act, pairs_st)
            attention_in_scalar(act, att_in)
            attention_scalar(act, att)
            merge_scalar(act, merge)
            out_scalar(act, way_out)
            ffn_scalar(act, ffn2)
            act.wait_ge(ctx_in, 16)
            for L in layers:
                norm_scalar(act, L.norm)
                win_scalar(act, L)
                gate_scalar(act, L)
                small_scalar(act, L)
                heads_scalar(act, L)
                gated_scalar(act, L)
                out2_scalar(act, L)
            final_scalar(act, final)

        @block.vector
        def _(dve):
            dve.wait_ge(vec_in, 16)
            dve.wait_ge(x_in[0], 16)
            dve.wait_ge(x_in[1], 16)
            dve.wait_ge(*cond.act.at("hi"))
            dve.tensor_tensor(CLO[:, :, :], CS[:, :, :], CHI[:, :, :].bitcast(F32), ALU.subtract).then_inc(*cond.dve.inc("lo"))
            dve.wait_ge(first_in, 16)
            dve.wait_ge(levels_in, 16)
            dve.wait_ge(lora_in, 16)
            ffn_vector(dve, ffn1)
            norm_vector(dve, mix)
            lora_vector(dve, lora_st)
            rwkv_vector(dve, pairs_st)
            attention_in_vector(dve, att_in)
            attention_vector(dve, att)
            merge_vector(dve, merge)
            out_vector(dve, way_out)
            ffn_vector(dve, ffn2)
            dve.wait_ge(ctx_in, 16)
            for L in layers:
                gain_vector(dve, L)
                norm_vector(dve, L.norm)
                win_vector(dve, L)
                taps_vector(dve, L)
                small_vector(dve, L)
                heads_vector(dve, L)
                gated_vector(dve, L)
                out2_vector(dve, L)
            final_vector(dve, final)

        return k




def tiles(w):
    kt, nt = -(-w.shape[0] // P), -(-w.shape[1] // P)
    full = np.zeros((kt * P, nt * P), w.dtype)
    full[:w.shape[0], :w.shape[1]] = w
    return full.reshape(kt, P, nt, P).transpose(0, 2, 1, 3)


def blocks_of(w):
    t = tiles(w)
    out = []
    for n in range(t.shape[1]):
        for m in range(0, t.shape[0], UNITS):
            b = np.zeros((UNITS, P, P), w.dtype)
            b[:min(UNITS, t.shape[0] - m)] = t[m:m + UNITS, n]
            out.append(b)
    return out


def columns_of(v):
    v = v.reshape(-1)
    full = np.zeros(-(-v.size // P) * P, v.dtype)
    full[:v.size] = v
    return full.reshape(-1, P).T


def stream(a):
    def ffn(n, mod):
        w = a[f"ffn{n}_w_in"][0]
        gate, up, down = blocks_of(w[:, :D_FF]), blocks_of(w[:, D_FF:]), blocks_of(a[f"ffn{n}_w_out"][0])
        out = [b for pair in zip(gate, up) for b in pair]
        if mod is None:
            return out + down
        return out + [b for pair in zip(down, blocks_of(a["w_mod_2"][mod])) for b in pair]
    out = ffn(1, None)
    w = a["w_in"][0]
    cuts = np.cumsum([0, D, D, D, W_LORA + A_LORA, G_LORA, AT_WIDTH, AT_WIDTH, AT_WIDTH, D, D])
    r, kx, v, wa, g, aq, ak, av, ga, gb = (blocks_of(w[:, cuts[i]:cuts[i + 1]]) for i in range(10))
    out += wa + g
    mod = blocks_of(a["w_mod_2"][0])
    for j in range(PAIRS):
        out += [r[j], kx[j], v[j]] + mod[j * MOD_PER_PAIR:(j + 1) * MOD_PER_PAIR]
    for c in range(AT_TILES):
        out += [aq[c], ak[c], av[c]]
    pa, pb = blocks_of(a["w_proj_rwkv"][0]), blocks_of(a["w_proj_attn"][0])
    for n in range(KT):
        out += [ga[n], gb[n], pa[n], pb[n]]
    out += blocks_of(a["w_out"][0])
    out += ffn(2, 1)
    for l in range(LAYERS):
        out += second_layer(a, l)
    return out


GQA_ORDER = [h for j in range(GQA_HEADS // GQA_KV) for h in (j, GQA_HEADS // GQA_KV + j)]


def in_tiles(parts):
    out = []
    for m in range(0, len(parts), UNITS):
        b = np.zeros((UNITS, P, P), parts[0].dtype)
        for u, part in enumerate(parts[m:m + UNITS]):
            b[u, :part.shape[0], :part.shape[1]] = part
        out.append(b)
    return out


def second_layer(a, l):
    w = a["w_in_2"][l]
    cut = np.cumsum([0, MLA_Q_RANK, MLA_KV_RANK, MLA_ROPE, GQA_KV * HD, GQA_KV * HD, GQA_HEADS * HD, 2 * CONV_CH, D])
    mq, mkv, kr, gk, gv, gq, conv, gate = (w[:, cut[i]:cut[i + 1]] for i in range(8))
    partner = rope_tables(MLA_ROPE)[2]
    kr = np.concatenate([kr[:, partner]] * 2 + [kr] * 2, 1)
    def heads_in_order(m, axis):
        return np.concatenate([np.take(m, range(h * HD, (h + 1) * HD), axis) for h in GQA_ORDER], axis)
    g0, g1 = MLA_HEADS * MLA_V, MLA_HEADS * MLA_V + GQA_HEADS * HD
    gate = np.concatenate([gate[:, :g0], heads_in_order(gate[:, g0:g1], 1), gate[:, g1:]], 1)
    a0, a1, c0, c1 = (conv[:, i * P:(i + 1) * P] for i in range(4))
    out = []
    for m in (mq, mkv, kr, gk, gv, heads_in_order(gq, 1), a0, c0, a1, c1):
        out += blocks_of(m)
    uq = a["mla_w_uq_2"][l].reshape(MLA_Q_RANK, MLA_HEADS, MLA_NOPE + MLA_ROPE)
    uq = np.concatenate([uq, uq[:, :, MLA_NOPE:][:, :, partner]], 2)
    ukv = a["mla_w_ukv_2"][l].reshape(MLA_KV_RANK, MLA_HEADS, MLA_NOPE + MLA_V)
    small = [uq[t * P:(t + 1) * P, h] for h in range(MLA_HEADS) for t in range(2)]
    small += [ukv[:, h, :MLA_NOPE] for h in range(MLA_HEADS)]
    v = ukv[:, :, MLA_NOPE:].reshape(MLA_KV_RANK, MLA_HEADS * MLA_V)
    small += [v[:, i * P:(i + 1) * P] for i in range(3)]
    pw = a["conv_pw_w_2"][l]
    small += [np.zeros((P, P), pw.dtype)] * (PW0 - len(small))
    small += [pw[t * P:(t + 1) * P, n * P:(n + 1) * P] for n in range(2) for t in range(2)]
    out += blocks_of(gate) + in_tiles(small)
    wo = a["w_out_2"][l]
    wo = np.concatenate([wo[:g0], heads_in_order(wo[g0:g1], 0), wo[g1:]], 0)
    return out + blocks_of(wo)


def vectors(a):
    out = np.zeros((P, COL["total"]), np.float32)
    def put(name, v):
        c = columns_of(v)
        out[:, COL[name]:COL[name] + c.shape[1]] = c
    for n in ("ffn1_norm", "mix_norm", "ffn2_norm", "b_gate"):
        put(n, a[n])
    mu = a["rwkv_mu"][0]
    put("mu_lora", mu[3 * D:])
    put("mu_rkv", mu[:3 * D].reshape(3, PAIRS, P).transpose(1, 0, 2))
    for n in ("w0", "a0", "k_k", "k_a", "r_k", "ln_w", "ln_b"):
        put(n, a[f"rwkv_{n}"])
    put("q_norm", np.concatenate([a["attn_q_norm"][0]] * 2))
    put("k_norm", np.concatenate([a["attn_k_norm"][0]] * 2))
    put("final_norm", a["final_norm_w_2"])
    cond = np.stack([columns_of(a["c_2"]), columns_of(a["c_ctx_2"])], 2)
    out[:, COL["cond"]:COL["cond"] + 2 * KT] = cond.reshape(P, 2 * KT)
    for l in range(LAYERS):
        put(f"norm{l}", a["norm_w_2"][l])
        put(f"b_mod{l}", a["b_mod_2"][l])
        put(f"mla_q{l}", a["mla_q_norm_2"][l])
        put(f"mla_kv{l}", a["mla_kv_norm_2"][l])
        put(f"gqa_q{l}", np.concatenate([a["gqa_q_norm_2"][l]] * 2))
        put(f"gqa_k{l}", np.concatenate([a["gqa_k_norm_2"][l]] * 2))
        put(f"dw_w{l}", a["conv_dw_w_2"][l].reshape(CONV_K, 2, P).transpose(1, 0, 2))
        put(f"dw_b{l}", a["conv_dw_b_2"][l])
        put(f"cln_w{l}", a["conv_ln_w_2"][l])
        put(f"cln_b{l}", a["conv_ln_b_2"][l])
        put(f"pw_b{l}", a["conv_pw_b_2"][l])
    return out


def low_ranks(a):
    out = np.zeros((P, PAIRS, 3, P), np.float32)
    out[:W_LORA, :, 0] = a["rwkv_w2"][0].reshape(W_LORA, PAIRS, P)
    out[W_LORA:, :, 0] = a["rwkv_a2"][0].reshape(A_LORA, PAIRS, P)
    g = a["rwkv_g2"][0].reshape(G_LORA, PAIRS, P)
    out[:, :, 1] = g[:P]
    out[:G_LORA - P, :, 2] = g[P:]
    return out.reshape(P, PAIRS, 3 * P)


def channel_major(x):
    return np.ascontiguousarray(x.reshape(x.shape[0], KT, P).transpose(2, 1, 0))


def even(w):
    return np.concatenate([w, np.zeros_like(w[:len(w) % 2])])


def layout(a):
    square, first, levels, second = constant_arrays()
    return {
        "xT": channel_major(a["x"][0]), "ctxT": channel_major(a["ctx_2"][0]), "vec": vectors(a), "square": square,
        "first": first, "levels": levels, "trig": second, "lora": low_ranks(a),
        "wstream": even(np.stack([b.transpose(1, 0, 2).reshape(P, UNITS * P) for b in stream(a)])),
    }


def kernel(**inputs):
    import concourse.bacc as bacc
    from concourse.bass_utils import run_bass_kernel_spmd

    arrays = layout({name: np.asarray(v) for name, v in inputs.items()})
    nc = bacc.Bacc("TRN2", target_bir_lowering=False, num_devices=1)
    ins = [nc.dram_tensor(f"in_{name}", v.shape, mybir.dt.from_np(v.dtype), kind="ExternalInput").ap() for name, v in arrays.items()]
    out = nc.dram_tensor("out_T", (P, KT, T), F32, kind="ExternalOutput").ap()
    block_kernel(nc, *ins, out)
    r = run_bass_kernel_spmd(nc, [{f"in_{name}": v for name, v in arrays.items()}], core_ids=[0])
    return np.ascontiguousarray(r.results[0]["out_T"].transpose(2, 1, 0)).reshape(1, T, D)
```

```python
from contextlib import ExitStack

import numpy as np

import concourse.bass as bass
from concourse import mybir

F32 = mybir.dt.float32
F32R = mybir.dt.float32r
I32 = mybir.dt.int32
ACT = mybir.ActivationFunctionType
ALU = mybir.AluOpType
AX = mybir.AxisListType.X

P = 128
D = 1024
T = 512
TC = 256
TT = T + TC
KT = D // P
HD = 64
D_FF = 2816
FT = D_FF // P
UNITS = 8
RMS_EPS = 1e-6
GN_EPS = 64e-5
NEG_INF = -1e30

RW_HEADS = D // HD
PAIRS = RW_HEADS // 2
W_LORA, A_LORA, G_LORA = 64, 64, 160
RW_COLS = 3 * D + W_LORA + A_LORA + G_LORA
CHUNK = 64
CHUNKS = T // CHUNK
LEVELS = 6
DECAY = float(np.exp(-0.5))

AT_TILES = 6
AT_WIDTH = AT_TILES * P
BLOCKS = T // P

LAYERS = 2
GRID_W = 64
ROPE_THETA = 10000.0
MLA_HEADS, MLA_NOPE, MLA_ROPE, MLA_V = 6, 64, 32, 64
MLA_Q_RANK, MLA_KV_RANK = 256, 128
GQA_HEADS, GQA_KV = 6, 2
CONV_CH, CONV_K = 256, 31
HALO = CONV_K // 2
Y_TILES = 8
KB = TT // P

MOD_TILES = 3 * D // P
FFN_IN_BLOCKS = 2 * FT
FFN_OUT_PER_TILE = -(-FT // UNITS)
FFN_OUT_BLOCKS = KT * FFN_OUT_PER_TILE
FFN_OUT_LOOPS = KT // 2
LORA_BLOCKS = 3
ROUND_ORDER = "SMMMMSMSMSMSMSMMMM"
ATT_BLOCKS = 3 * (AT_TILES - 2)
MERGE_BLOCKS = 4 * KT
OUT_BLOCKS = KT
WIN2 = ["mq0", "mq1", "mkv", "kr", "gk", "gv", "gq0", "gq1", "gq2", "ca0", "cg0", "ca1", "cg1"]
GATE2_BLOCKS = Y_TILES
UQ0, KN0, V0 = 0, 2 * MLA_HEADS, 3 * MLA_HEADS
PW0 = -(-(V0 + 3) // UNITS) * UNITS
SMALL2_BLOCKS = PW0 // UNITS + 1


def columns():
    out, at = {}, 0
    def put(name, n):
        nonlocal at
        out[name] = at
        at += n
    for name, n in (("ffn1_norm", KT), ("mix_norm", KT), ("ffn2_norm", KT), ("b_gate", 2 * KT), ("mu_lora", 3),
                    ("mu_rkv", 3 * PAIRS), ("w0", KT), ("a0", KT), ("k_k", KT), ("k_a", KT), ("r_k", KT), ("ln_w", KT),
                    ("ln_b", KT), ("q_norm", 1), ("k_norm", 1), ("final_norm", KT), ("cond", 2 * KT)):
        put(name, n)
    for l in range(LAYERS):
        for name, n in (("norm", KT), ("b_mod", MOD_TILES), ("mla_q", 2), ("mla_kv", 1), ("gqa_q", 1), ("gqa_k", 1),
                        ("dw_w", 2 * CONV_K), ("dw_b", 2), ("cln_w", 2), ("cln_b", 2), ("pw_b", 2)):
            put(f"{name}{l}", n)
    out["total"] = at
    return out


COL = columns()


def rope_tables(dim):
    r = dim // 2
    half = r // 2
    freqs = (np.float32(ROPE_THETA) ** (-np.arange(half, dtype=np.float32) / np.float32(half))).astype(np.float32)
    t = np.arange(T)
    cos, sin, partner = np.zeros((dim, T), np.float32), np.zeros((dim, T), np.float32), np.zeros(dim, int)
    for d in range(dim):
        pos = (t // GRID_W if d < r else t % GRID_W).astype(np.float32)
        ang = pos * freqs[d % half]
        first = d % r < half
        cos[d] = np.cos(ang)
        sin[d] = np.sin(ang) * (-1 if first else 1)
        partner[d] = d + half if first else d - half
    return cos, sin, partner


def constant_arrays():
    p = np.arange(P)[:, None]
    f = np.arange(P)[None, :]
    eye = np.eye(P, dtype=np.float32)
    ones = np.ones((P, P), np.float32)
    heads = (p // HD == f // HD).astype(np.float32)
    s = p % HD
    c = np.arange(CHUNK)[None, :]
    before = (s < c).astype(np.float32)
    upto = (s <= c).astype(np.float32)
    after = (s > c).astype(np.float32)
    eye2 = (s == c).astype(np.float32)
    square = np.concatenate([eye, ones, heads, before, upto, after, eye2], 1)
    lower, upper = [], []
    for l in range(LEVELS):
        w = 1 << l
        low = (s // (2 * w) == c // (2 * w)) & (s % (2 * w) >= w) & (c % (2 * w) < w)
        up = (s // (2 * w) == c // (2 * w)) & (s % (2 * w) < w) & (c % (2 * w) >= w)
        lower.append(low)
        upper.append(up)
    levels = np.concatenate(lower + upper, 1).astype(np.int32)
    scan = np.ones((P, T), np.float32)
    scan[:, ::CHUNK] = 0
    cur = np.where(f <= p, 0, NEG_INF)
    prev = np.where(f >= p, 0, NEG_INF)
    dil = np.where((f <= p) & (f // 32 == p // 32), 0, NEG_INF)
    masks = np.concatenate([prev, cur, dil], 1).astype(np.float32)
    first = np.concatenate([square[:, 3 * P:], scan, masks], 1)
    cos, sin, partner = rope_tables(MLA_ROPE)
    mla = np.ones((P, TT), np.float32)
    mla[MLA_NOPE:MLA_NOPE + MLA_ROPE, :T] = cos
    mla[MLA_NOPE + MLA_ROPE:, :T] = sin
    mla[MLA_NOPE + MLA_ROPE:, T:] = 0
    kr = np.concatenate([sin, sin, cos, cos], 0)
    cos, sin, partner = rope_tables(HD)
    swap = np.zeros((P, P), np.float32)
    for h in range(2):
        for d in range(HD):
            swap[h * HD + partner[d], h * HD + d] = 1
    second = np.concatenate([mla, kr, np.concatenate([cos, cos], 0), swap, np.concatenate([sin, sin], 0)], 1)
    return square[:, :3 * P], first, levels, second


FC = {"before": 0, "after": 2 * CHUNK, "eye2": 3 * CHUNK, "scan": 4 * CHUNK, "masks": 4 * CHUNK + T,
      "total": 4 * CHUNK + T + 3 * P}
SC = {"mla": 0, "kr": TT, "cos": TT + T, "swap": TT + 2 * T, "total": TT + 2 * T + P}


class Counter:
    def __init__(self, sem):
        self.sem, self.total = sem, 0


class Steps:
    def __init__(self, counter, names, times=1):
        self.sem, self.base, self.names, self.times, self.next = counter.sem, counter.total, list(names), times, 0
        self.index = {n: k for k, n in enumerate(self.names)}
        assert len(self.index) == len(self.names)
        counter.total += len(self.names) * times

    def at(self, name, i=0):
        return self.sem, self.base + self.index[name] + 1 + i * len(self.names)

    def before(self, name, i):
        assert self.base + self.index[name] + 1 > len(self.names), "a wait below one"
        return self.sem, self.base + self.index[name] + 1 - len(self.names) + i * len(self.names)

    def last(self):
        return self.sem, self.base + len(self.names) * self.times

    def inc(self, name):
        assert self.names[self.next % len(self.names)] == name, (self.names[self.next % len(self.names)], name)
        self.next += 1
        return self.sem, 1


class Stage:
    def __init__(self, k, blocks, pe=(), act=(), dve=(), times=1):
        self.k, self.b0, self.times = k, k.blocks, times
        self.entry = {"pe": (k.pe.sem, k.pe.total), "act": (k.act.sem, k.act.total), "dve": (k.dve.sem, k.dve.total)}
        self.pe, self.act, self.dve = Steps(k.pe, pe, times), Steps(k.act, act, times), Steps(k.dve, dve, times)
        k.blocks += blocks * times

    def enter(self, eng, mine):
        for name, (sem, count) in self.entry.items():
            if count:
                eng.wait_ge(sem, count)
        if mine != "pe" and self.b0:
            eng.wait_ge(self.k.blocks_used, self.b0)


def block_kernel(nc, xT, ctxT, vec, square, first, levels, trig, lora, wstream, outT):
    nblocks = wstream.shape[0]
    with ExitStack() as ctx:
        sem = lambda name: ctx.enter_context(nc.semaphore(name))

        class K:
            pe, act, dve = Counter(sem("tensor_steps")), Counter(sem("scalar_steps")), Counter(sem("vector_steps"))
            blocks_used = sem("blocks_used")
            blocks = 0
        k = K()
        raw_full = [sem("raw_full0"), sem("raw_full1")]
        rounded = sem("rounded")
        split = sem("split")
        x_in = [sem(f"x_in{i}") for i in range(2)]
        const_in, first_in, levels_in, lora_in, vec_in, ctx_in, trig_in, sin_in, out_done = (
            sem(n) for n in ("const_in", "first_in", "levels_in", "lora_in", "vec_in", "ctx_in", "trig_in", "sin_in", "out_done"))
        tensor_ready, vector_ready = sem("tensor_ready"), sem("vector_ready")
        filled = sem("filled")

        at = [-(-nc.sbuf_base // 64) * 64]
        def fixed(name, shape, dt=F32):
            t = nc.alloc_sbuf_tensor_at(name, shape, dt, offset=at[0])
            at[0] += -(-int(np.prod(shape[1:])) * 4 // 32) * 32
            return t
        X = fixed("X", [P, KT, T])
        RAW = fixed("RAW", [P, 2, UNITS * P])
        WHI = fixed("WHI", [P, 2, UNITS * P], F32R)
        WLO = fixed("WLO", [P, 2, UNITS * P], F32R)
        VEC = fixed("VEC", [P, COL["total"]])
        SQC = fixed("SQC", [P, 3 * P])
        shared_at = at[0]
        FCC = fixed("FCC", [P, FC["total"]])
        LVL = fixed("LVL", [P, 2 * LEVELS, CHUNK], I32)
        at[0] = max(at[0], shared_at + 4 * SC["total"])
        TRIG = nc.alloc_sbuf_tensor_at("TRIG", [P, SC["total"]], F32, offset=shared_at)
        EPS = fixed("EPS", [P, 2])
        CHL = fixed("CHL", [P, KT, 4], F32R)
        CS = fixed("CS", [P, KT, 2])
        MOD = fixed("MOD", [P, LAYERS * MOD_TILES, 2])
        MG = fixed("MG", [P, KT, 2])
        MX2, NM2, DEN2 = (fixed(n, [P, 4 * KB]) for n in ("MX2", "NM2", "DEN2"))
        at[0] = -(-at[0] // 64) * 64
        arena0 = at[0]
        arena = nc.sbuf_usable_end - arena0
        def place(name, shape, offset, dt=F32):
            size = int(np.prod(shape[1:])) * 4
            assert offset + size <= arena, (name, offset + size, arena)
            return nc.alloc_sbuf_tensor_at(name, shape, dt, offset=arena0 + offset)
        class Area:
            def __init__(self, at):
                self.at = at
            def __call__(self, name, shape, dt=F32):
                t = place(name, shape, self.at, dt)
                self.at += -(-int(np.prod(shape[1:])) * 4 // 32) * 32
                return t
        psum = [ctx.enter_context(nc.psum_tensor(f"psum{i}", [P, 2, 512], F32)) for i in range(4)]
        bank = [psum[i // 2][:, i % 2, :] for i in range(8)]
        two_banks = [psum[i][:, :, :].rearrange("p a n -> p (a n)") for i in range(4)]
        col = lambda name, i=0, rows=slice(0, P): VEC[rows, bass.ds(COL[name] + i, 1)]
        eye, ones, heads = SQC[:, 0:P], SQC[:, P:2 * P], SQC[:, 2 * P:3 * P]

        def round_block(act, q, i=0, nb=0):
            act.wait_ge(raw_full[q % 2], 16 * (q // 2 + 1) + i * (8 * nb))
            if q >= 2:
                act.wait_ge(k.blocks_used, q - 1 + i * nb)
            act.activation(WHI[:, q % 2, :], RAW[:, q % 2, :], ACT.Copy).then_inc(rounded, 1)

        def tile_of(t, slot, u, m=P):
            return t[:, slot, u * P:u * P + m]

        def product(pe, out, slot, units, hi, lo, last):
            mm = None
            for n, (u, kt) in enumerate(units):
                first, end = n == 0, n == len(units) - 1
                pe.matmul(out, tile_of(WHI, slot, u), hi(kt), start=first and last[0], stop=False)
                pe.matmul(out, tile_of(WHI, slot, u), lo(kt), start=False, stop=False)
                mm = pe.matmul(out, tile_of(WLO, slot, u), hi(kt), start=False, stop=end and last[1])
            return mm
        WHOLE = (True, True)

        def block_ready(pe, q, i=0, nb=0):
            pe.wait_ge(split, q + 1 + i * nb)

        def block_out(eng, q, i=0, nb=0):
            eng.wait_ge(k.blocks_used, q + 1 + i * nb)

        class Norm:
            def __init__(self, scratch, *groups):
                self.groups = groups
                self.sq4, self.hf, self.std, self.rstd = scratch
                pe, act, dve = [], [], []
                for g in range(len(groups)):
                    pe += [f"sum{g}_{t}" for t in range(KT)]
                    act += [f"sq{g}_{t}" for t in range(KT)] + [f"std{g}"]
                for g in range(len(groups)):
                    act += [f"hi{g}_{t}" for t in range(KT)]
                    dve += [f"rstd{g}", f"h{g}_0", f"h{g}_1"]
                    for t in range(KT):
                        dve += [f"lo{g}_{t}"] + ([f"h{g}_{t + 2}"] if t + 2 < KT else [])
                self.st = Stage(k, 0, pe, act, dve)

        def norm_tensor(pe, nm):
            st = nm.st
            st.enter(pe, "pe")
            for g, (x, n, *_) in enumerate(nm.groups):
                for t in range(KT):
                    pe.wait_ge(*st.act.at(f"sq{g}_{t}"))
                    pe.matmul(bank[7 - g][:, 0:n], ones, nm.sq4[:, t % 4, 0:n], start=t == 0, stop=t == KT - 1)\
                      .then_inc(*st.pe.inc(f"sum{g}_{t}"))

        def norm_scalar(act, nm):
            st = nm.st
            st.enter(act, "act")
            for g, (x, n, *_) in enumerate(nm.groups):
                for t in range(KT):
                    if t >= 4:
                        act.wait_ge(*st.pe.at(f"sum{g}_{t - 4}"))
                    elif g:
                        act.wait_ge(*st.pe.at(f"sum{g - 1}_{t + 4}"))
                    act.activation(nm.sq4[:, t % 4, 0:n], x(t), ACT.Square).then_inc(*st.act.inc(f"sq{g}_{t}"))
                act.wait_ge(*st.pe.at(f"sum{g}_{KT - 1}"))
                act.activation(nm.std[:, g, 0:n], bank[7 - g][:, 0:n], ACT.Sqrt, scale=1.0 / D, bias=EPS[:, 0:1])\
                   .then_inc(*st.act.inc(f"std{g}"))
            for g, (x, n, hi, lo, gain, shift) in enumerate(nm.groups):
                for t in range(KT):
                    act.wait_ge(*st.dve.at(f"h{g}_{t}"))
                    src = nm.hf[:, t % 4, 0:n]
                    if shift:
                        ins = act.activation(hi(t), src, ACT.Identity, bias=shift(t))
                    else:
                        ins = act.activation(hi(t), src, ACT.Copy)
                    ins.then_inc(*st.act.inc(f"hi{g}_{t}"))

        def norm_vector(dve, nm):
            st = nm.st
            st.enter(dve, "dve")
            for g, (x, n, hi, lo, gain, shift) in enumerate(nm.groups):
                dve.wait_ge(*st.act.at(f"std{g}"))
                dve.reciprocal(nm.rstd[:, g, 0:n], nm.std[:, g, 0:n]).then_inc(*st.dve.inc(f"rstd{g}"))
                dve.wait_ge(*st.dve.at(f"rstd{g}"))

                def scaled(t):
                    if t >= 4:
                        dve.wait_ge(*st.dve.at(f"lo{g}_{t - 4}"))
                    elif g:
                        dve.wait_ge(*st.dve.at(f"lo{g - 1}_{t + 4}"))
                    dve.scalar_tensor_tensor(out=nm.hf[:, t % 4, 0:n], in0=x(t), scalar=gain(t), in1=nm.rstd[:, g, 0:n], op0=ALU.mult,
                                             op1=ALU.mult).then_inc(*st.dve.inc(f"h{g}_{t}"))
                scaled(0)
                scaled(1)
                for t in range(KT):
                    dve.wait_ge(*st.act.at(f"hi{g}_{t}"))
                    src, high = nm.hf[:, t % 4, 0:n], hi(t).bitcast(F32)
                    if shift:
                        ins = dve.scalar_tensor_tensor(out=lo(t), in0=src, scalar=shift(t), in1=high, op0=ALU.add, op1=ALU.subtract)
                    else:
                        ins = dve.tensor_tensor(lo(t), src, high, ALU.subtract)
                    ins.then_inc(*st.dve.inc(f"lo{g}_{t}"))
                    if t + 2 < KT:
                        scaled(t + 2)

        def plain_norm(gain):
            return Norm((SQ4, HF, STD, RSTD), (lambda t: X[:, t, :], T, lambda t: HHI[:, t, :], lambda t: HLO[:, t, :], lambda t: col(gain, t), None))

        class FFN:
            def __init__(self, norm_col):
                self.norm = plain_norm(norm_col)
                self.up = Stage(k, 4, (), ("silu0", "hi0", "silu1", "hi1"), ("mul0", "lo0", "mul1", "lo1"), FT // 2)
                self.nb = 2 * FFN_OUT_PER_TILE
                self.down = Stage(k, self.nb, (), (), ("x0", "x1"), FFN_OUT_LOOPS)

        fa = Area(0)
        HHI, HLO = fa("HHI", [P, KT, T], F32R), fa("HLO", [P, KT, T], F32R)
        after_h = fa.at
        GHI, GLO = fa("GHI", [P, FT, T], F32R), fa("GLO", [P, FT, T], F32R)
        SILU, GF = fa("SILU", [P, 2, T]), fa("GF", [P, 2, T])
        upper = fa.at
        na = Area(after_h)
        SQ4, HF, STD, RSTD = na("SQ4", [P, 4, T]), na("HF", [P, 4, T]), na("STD", [P, 1, T]), na("RSTD", [P, 1, T])

        def ffn_tensor(pe, f):
            norm_tensor(pe, f.norm)
            st = f.up
            st.enter(pe, "pe")
            with pe.Fori(0, FT // 2) as i:
                for q in range(4):
                    if q % 2 == 0:
                        pe.wait_ge(*st.act.before(f"silu{q // 2}", i))
                    else:
                        pe.wait_ge(*st.dve.before(f"mul{q // 2}", i))
                    block_ready(pe, st.b0 + q, i, 4)
                    product(pe, bank[q], (st.b0 + q) % 2, [(u, u) for u in range(KT)], lambda t: HHI[:, t, :],
                            lambda t: HLO[:, t, :], WHOLE).then_inc(k.blocks_used, 1)
            st = f.down
            st.enter(pe, "pe")
            with pe.Fori(0, FFN_OUT_LOOPS) as i:
                q = 0
                for n in range(2):
                    pe.wait_ge(*st.dve.before(f"x{n}", i))
                    for m in range(FFN_OUT_PER_TILE):
                        units = [(u, UNITS * m + u) for u in range(UNITS) if UNITS * m + u < FT]
                        block_ready(pe, st.b0 + q, i, f.nb)
                        product(pe, bank[4 + n], (st.b0 + q) % 2, units, lambda t: GHI[:, t, :], lambda t: GLO[:, t, :],
                                (m == 0, m == FFN_OUT_PER_TILE - 1)).then_inc(k.blocks_used, 1)
                        q += 1

        def ffn_scalar(act, f):
            norm_scalar(act, f.norm)
            st = f.up
            st.enter(act, "act")
            with act.Fori(0, FT // 2) as i:
                for n in range(2):
                    block_out(act, st.b0 + 2 * n, i, 4)
                    round_block(act, st.b0 + 2 * n + 2, i, 4)
                    act.wait_ge(*st.dve.before(f"mul{n}", i))
                    act.activation(SILU[:, n, :], bank[2 * n], ACT.Silu).then_inc(*st.act.inc(f"silu{n}"))
                    round_block(act, st.b0 + 2 * n + 3, i, 4)
                    act.wait_ge(*st.dve.at(f"mul{n}", i))
                    act.activation(GHI[:, i * 2 + n, :], GF[:, n, :], ACT.Copy).then_inc(*st.act.inc(f"hi{n}"))
            st = f.down
            with act.Fori(0, FFN_OUT_LOOPS) as i:
                for q in range(f.nb):
                    round_block(act, st.b0 + q + 2, i, f.nb)

        def ffn_vector(dve, f):
            norm_vector(dve, f.norm)
            st = f.up
            st.enter(dve, "dve")
            with dve.Fori(0, FT // 2) as i:
                for n in range(2):
                    block_out(dve, st.b0 + 2 * n + 1, i, 4)
                    dve.wait_ge(*st.act.at(f"silu{n}", i))
                    dve.tensor_tensor(GF[:, n, :], bank[2 * n + 1], SILU[:, n, :], ALU.mult)\
                       .then_inc(*st.dve.inc(f"mul{n}"))
                    dve.wait_ge(*st.act.at(f"hi{n}", i))
                    dve.tensor_tensor(GLO[:, i * 2 + n, :], GF[:, n, :], GHI[:, i * 2 + n, :].bitcast(F32), ALU.subtract)\
                       .then_inc(*st.dve.inc(f"lo{n}"))
            st = f.down
            with dve.Fori(0, FFN_OUT_LOOPS) as i:
                for n in range(2):
                    per = f.nb // 2
                    block_out(dve, st.b0 + per * (n + 1) - 1, i, f.nb)
                    xt = X[:, i * 2 + n, :]
                    dve.scalar_tensor_tensor(out=xt, in0=bank[4 + n], scalar=0.5, in1=xt, op0=ALU.mult, op1=ALU.add)\
                       .then_inc(*st.dve.inc(f"x{n}"))

        ra = Area(after_h)
        YA = ra("YA", [P, KT, T])
        after_ya = ra.at
        LD = ra("LD", [P, 3, T])
        W3S = ra("W3S", [P, 2, 3 * P])
        KA1 = ra("KA1", [P, KT])
        sets_at = ra.at

        class PairSet:
            def __init__(self, p, a):
                new = lambda name, shape, dt=F32: a(f"{name}{p}", shape, dt)
                at0 = a.at
                self.RKV = new("RKV", [P, 3, T])
                sg_at = a.at
                self.SG, self.CSUM = new("SG", [P, T]), new("CSUM", [P, T])
                self.E1 = new("E1", [P, T])
                e2_at = a.at
                self.E2, self.E3, self.KK = new("E2", [P, T]), new("E3", [P, T]), new("KK", [P, T])
                aa_at = a.at
                self.AA = new("AA", [P, T])
                self.GG, self.BON = new("GG", [P, T]), new("BON", [P, T])
                kp_at = a.at
                self.KP, self.RK = new("KP", [P, T]), new("RK", [P, T])
                ar_at = a.at
                self.AR = new("AR", [P, 2, T])
                bt_at = a.at
                self.BT, self.KTL = new("BT", [P, T]), new("KTL", [P, T])
                over = lambda name, at, *shape: place(f"{name}{p}", [P, *shape], at)
                row = 4 * T
                self.VS = self.RKV[:, 2, :]
                self.MA1 = over("MA1", at0, CHUNKS, 2 * CHUNK)
                self.TS = over("TS", at0 + 2 * row, CHUNKS, CHUNK)
                self.SS = over("SS", at0 + 2 * row, CHUNKS, HD)
                self.MA2 = over("MA2", sg_at, CHUNKS, 2 * CHUNK)
                self.DSQ = over("DSQ", sg_at, T)
                self.BTOK, self.KTOK, self.VTOK = (over(n, e2_at + m * row, CHUNKS, HD) for m, n in enumerate(("BTOK", "KTOK", "VTOK")))
                self.AL = over("AL", aa_at, CHUNKS, CHUNK)
                self.GT = over("GT", aa_at, CHUNKS, HD)
                self.AY = over("AY", kp_at, CHUNKS, 2 * HD)
                self.OS, self.DV = over("OS", kp_at, T), over("DV", kp_at + row, T)
                self.QS = over("QS", ar_at, CHUNKS, CHUNK)
                self.XI, self.XIT = over("XI", bt_at, CHUNKS, CHUNK), over("XIT", bt_at + row, CHUNKS, CHUNK)
                self.ZS = over("ZS", bt_at, CHUNKS, 2 * HD)
                self.B = [bank[3 * p + m] for m in range(3)]
        SETS = [PairSet(p, ra) for p in range(2)]
        pbuf_at = ra.at
        PBUF = [ra(f"PBUF{p}", [P, 3, T + 8]) for p in range(2)]
        after_pairs = ra.at
        lp = Area(sets_at)
        LP, LDIF = lp("LP", [P, 3, T + 8]), lp("LDIF", [P, 3, T])
        assert after_pairs <= arena, (after_pairs, arena)

        TWO = range(2)
        STREAMED, MODS, LOOP_BLOCKS = ROUND_ORDER.count("S"), ROUND_ORDER.count("M"), len(ROUND_ORDER)
        S_AT, M_AT = ([n for n, kind in enumerate(ROUND_ORDER) if kind == which] for which in "SM")
        PER_LAYER = MODS // LAYERS
        MOD_SUM = ra("MOD_SUM", [P, MODS, 2])
        ROW = 2 * P
        ROWS = ra("ROWS", [4, ROW])
        named = lambda p, *names: [f"{n}_{p}" for n in names]
        rw_pe = named(0, "zw", "za", "g") + named(1, "zw", "za", "g") + ["kkss_0", "kkss_1"]
        rw_pe += ["turn0"] + named(0, "bonus", "toka", "tokb", "tokk", "tokv", "m1", "al", "m2") + ["bonus_1", "toka_1", "turn1"] + named(1, "tokb", "tokk", "tokv")
        rw_pe += ["t1_0", "m1_1", "x1_0", "xt1_0", "al_1", "t2_0", "m2_1", "t1_1"]
        for l in range(2, LEVELS):
            rw_pe += [f"x{l}_0"] * (l < LEVELS - 1) + [f"xt{l}_0", f"x{l - 1}_1"] + [f"xt{l - 1}_1"]
            rw_pe += [f"t{l + 1}_0" if l + 1 < LEVELS else "y_0"] + ["turn2"] * (l == 3) + [f"t{l}_1"]
        rw_pe += [f"xt{LEVELS - 1}_1", "z_0", "y_1", "q_0", "z_1", "gt_0", "q_1", "gt_1"]
        rw_pe += [f"s{n}_{p}" for n in range(CHUNKS - 1) for p in TWO] + ["o_0", "o_1", "mean_0", "mean_1", "turn3", "var_0", "var_1", "turn4", "turn5"]
        rw_act = named(0, "sg", "aa", "gg") + named(1, "sg", "aa", "gg") + ["kksq_0", "kksq_1", "pb0", "kkn_0", "kkn_1"]
        rw_act += ["e1_0", "e2_0", "e1_1", "e2_1", "row0", "am1_0", "am1_1", "e3_0", "row1", *named(0, "toka", "tokb", "tokk", "tokv")]
        rw_act += ["e3_1", "pb1", *named(1, "toka", "tokb", "tokk", "tokv"), "t1_0", "pb2", "t2_0", "row2", "t1_1", "t3_0", "t2_1", "t4_0", "pb3", "t3_1"]
        rw_act += ["t5_0", "t4_1", "y_0", "t5_1", "z0_0", "z1_0", "pb4", "y_1", "row3", "z0_1", "z1_1"]
        rw_act += ["pb5", "os_0", "os_1", "dsq_0", "dsq_1", "row4", "sd_0", "sd_1", "row5"]
        rw_dve = ["dk_0", "k_0", "dk_1", "k_1"]
        for p in TWO:
            rw_dve += named(p, "dr", "r", "dv", "v", "csum", "cprev")
        rw_dve += named(0, "kkmax", "kkinv", "kk", "kp", "rk", "rt", "bb", "at", "bt", "ktl", "bon")
        first_level = ("al", "xi", "xi0", "m2a", "m2b", "xit", "xit0")
        rw_dve += named(1, "kkmax", "kkinv", "kk", "kp", "rk") + ["m1a_0", "m1b_0"] + named(1, "rt", "bb", "at")
        rw_dve += named(0, *first_level) + named(1, "bt", "ktl", "bon") + ["x1_0", "xt1_0"]
        rw_dve += named(1, "m1a", "m1b", *first_level)
        for l in range(2, LEVELS):
            rw_dve += [f"x{l}_0"] * (l < LEVELS - 1) + [f"xt{l}_0", f"x{l - 1}_1", f"xt{l - 1}_1"]
        rw_dve += [f"xt{LEVELS - 1}_1", "q_0", "gt_0", "q_1", "gt_1"] + [f"s{n}_{p}" for n in range(CHUNKS - 1) for p in TWO]
        rw_dve += ["dd_0", "dd_1", "rinv_0", "n0_0", "n1_0", "n2_0", "yf_0", "rinv_1", "n0_1", "n1_1", "n2_1", "yf_1", "mod_sum", "mods"]

        def h_hi(t):
            return HHI[:, t, :]

        def h_lo(t):
            return HLO[:, t, :]
        ALLK = [(u, u) for u in range(KT)]

        PRO_BLOCKS = LORA_BLOCKS + STREAMED

        def lora_tensor(pe, st):
            st.enter(pe, "pe")
            for c in range(PRO_BLOCKS):
                if c >= 8:
                    pe.wait_ge(*st.act.at(f"pb{c - 8}"))
                block_ready(pe, st.b0 + c)
                product(pe, bank[c % 8], (st.b0 + c) % 2, ALLK, h_hi, h_lo, WHOLE).then_inc(k.blocks_used, 1)

        def lora_scalar(act, st):
            st.enter(act, "act")
            act.dma_start(W3S[:, :, :], lora[:, 0:2, :]).then_inc(lora_in, 16)
            for c in range(PRO_BLOCKS):
                block_out(act, st.b0 + c)
                round_block(act, st.b0 + c + 2)
                if c == 0:
                    act.wait_ge(*st.dve.at("zero"))
                dst = LP[:, c, :] if c < LORA_BLOCKS else PBUF[(c - LORA_BLOCKS) // 3][:, (c - LORA_BLOCKS) % 3, :]
                act.activation(dst[:, 1:T + 1], bank[c % 8], ACT.Copy).then_inc(*st.act.inc(f"pb{c}"))
                if c == LORA_BLOCKS:
                    act.wait_ge(*st.dve.at("o2"))
                    act.activation(LD[0:W_LORA, 0, :], LD[0:W_LORA, 0, :], ACT.Tanh).then_inc(*st.act.inc("tanh"))
                    act.activation(LD[:, 1:3, :], LD[:, 1:3, :], ACT.Sigmoid).then_inc(*st.act.inc("sig"))

        def lora_vector(dve, st):
            V = st.dve
            st.enter(dve, "dve")
            dve.memset(LP[:, :, 0:1], 0.0)
            for p in TWO:
                ins = dve.memset(PBUF[p][:, :, 0:1], 0.0)
            ins.then_inc(*V.inc("zero"))
            dve.tensor_scalar(KA1[:, :], VEC[:, COL["k_a"]:COL["k_a"] + KT], -1.0, 1.0, ALU.mult, ALU.add).then_inc(*V.inc("ka1"))
            for c in range(LORA_BLOCKS):
                dve.wait_ge(*st.act.at(f"pb{c}"))
                dve.tensor_tensor(LDIF[:, c, :], LP[:, c, 0:T], LP[:, c, 1:T + 1], ALU.subtract).then_inc(*V.inc(f"d{c}"))
                dve.wait_ge(*V.at(f"d{c}"))
                dve.scalar_tensor_tensor(out=LD[:, c, :], in0=LDIF[:, c, :], scalar=col("mu_lora", c), in1=LP[:, c, 1:T + 1], op0=ALU.mult, op1=ALU.add)\
                   .then_inc(*V.inc(f"o{c}"))

        HALF = CHUNKS // 2

        def each_unit(pe, out, lhs, rhs, between=None):
            mm = None
            pe.sem_inc(tensor_ready)
            for n in range(CHUNKS):
                for h in range(2):
                    s = slice(h * HD, h * HD + HD)
                    mm = pe.matmul(out(s, n), lhs(s, n), rhs(s, n), start=True, stop=True)
                if between and n == HALF - 1:
                    between(1)
            return mm

        def rwkv_tensor(pe, st):
            st.enter(pe, "pe")
            A, V, S = st.act, st.dve, st.pe
            pe.wait_ge(lora_in, 16)
            e2 = lambda s: FCC[s, FC["eye2"]:FC["eye2"] + HD]
            unit = lambda t: lambda s, n: t[s, n * CHUNK:(n + 1) * CHUNK]
            wide = lambda lo, hi: lambda s, n: (lo if n < HALF else hi)[s, (n % HALF) * 2 * CHUNK:(n % HALF + 1) * 2 * CHUNK]
            mat = lambda t: lambda s, n: t[s, n, 0:CHUNK]
            with pe.Fori(0, PAIRS // 2) as i:
                def modulation(m):
                    half = m % 2
                    if half == 0:
                        if m:
                            turn(m // 2 - 1)
                        pe.wait_ge(*(A.at(f"row{m // 2 - 1}", i) if m else V.before("mods", i)))
                    block_ready(pe, st.b0 + M_AT[m], i, LOOP_BLOCKS)
                    slot, out = (st.b0 + M_AT[m]) % 2, bank[7][0:4, 0:ROW]
                    for u in range(KT // 2):
                        kt, cols = half * (KT // 2) + u, slice(u * ROW, (u + 1) * ROW)
                        pe.matmul(out, CHL[:, kt, :], WHI[:, slot, cols], start=kt == 0, stop=False)
                        mm = pe.matmul(out[0:2], CHL[:, kt, 0:2], WLO[:, slot, cols], start=False, stop=kt == KT - 1)
                        if u == KT // 2 - 1:
                            mm.then_inc(k.blocks_used, 1)
                        yield
                def turn(g):
                    pe.wait_ge(*A.at(f"row{g}", i))
                    for n in range(2):
                        mm = pe.matmul(bank[7][:, ROW + 4 * (2 * g + n):ROW + 4 * (2 * g + n) + 4], ROWS[0:4, n * P:(n + 1) * P], eye[0:4, 0:4],
                                       start=True, stop=True)
                    mm.then_inc(*S.inc(f"turn{g}"))
                def streamed(q):
                    b = S_AT[q]
                    pe.wait_ge(*(A.at(f"pb{q - 1}", i) if q else A.before("pb5", i)))
                    block_ready(pe, st.b0 + b, i, LOOP_BLOCKS)
                    slot, last = (st.b0 + b) % 2, KT - 1
                    for u in range(KT):
                        pe.matmul(bank[6], tile_of(WHI, slot, u), h_hi(u), start=u == 0, stop=False)
                        yield
                        pe.matmul(bank[6], tile_of(WHI, slot, u), h_lo(u), start=False, stop=False)
                        yield
                        mm = pe.matmul(bank[6], tile_of(WLO, slot, u), h_hi(u), start=False, stop=u == last)
                        if u == last:
                            mm.then_inc(k.blocks_used, 1)
                        yield
                def whole(*blocks):
                    for block in blocks:
                        for _ in block:
                            pass
                def unit_products(out, lhs, rhs, name, between=None, after=1):
                    each_unit(pe, out, lhs, rhs, between).then_inc(*S.inc(name))
                    dense(after)
                def low_ranks(p):
                    d = SETS[p]
                    pe.wait_ge(*A.before(f"sd_{p}", i))
                    pe.wait_ge(*V.before(f"dd_{p}", i))
                    if p == 0:
                        pe.wait_ge(lora_in, 16 + i * 16)
                    pe.sem_inc(tensor_ready)
                    pe.matmul(d.B[0], W3S[0:W_LORA, p, 0:P], LD[0:W_LORA, 0, :], start=True, stop=True).then_inc(*S.inc(f"zw_{p}"))
                    pe.matmul(d.B[1], W3S[W_LORA:P, p, 0:P], LD[W_LORA:P, 0, :], start=True, stop=True).then_inc(*S.inc(f"za_{p}"))
                    pe.matmul(d.B[2], W3S[:, p, P:2 * P], LD[:, 1, :], start=True, stop=False)
                    pe.matmul(d.B[2], W3S[:, p, 2 * P:3 * P], LD[:, 2, :], start=False, stop=True).then_inc(*S.inc(f"g_{p}"))
                def head_sums(name, p, out, src, *waits):
                    for w in waits:
                        pe.wait_ge(*w)
                    pe.matmul(out, heads, src, start=True, stop=True).then_inc(*S.inc(f"{name}_{p}"))
                def tokens(p):
                    d = SETS[p]
                    between = dense if p == 0 else None
                    pe.wait_ge(*V.at(f"ktl_{p}", i))
                    pe.wait_ge(*A.at(f"kkn_{p}", i))
                    unit_products(unit(d.B[0]), unit(d.AR[:, 0, :]), lambda s, n: e2(s), f"toka_{p}", between)
                    unit_products(unit(d.B[2]), unit(d.BT), lambda s, n: e2(s), f"tokb_{p}", between)
                    pe.wait_ge(*V.at(f"bon_{p}", i))
                    unit_products(unit(d.B[1]), unit(d.KTL), lambda s, n: e2(s), f"tokk_{p}", between)
                    pe.wait_ge(*A.at(f"toka_{p}", i))
                    unit_products(unit(d.B[0]), unit(d.VS), lambda s, n: e2(s), f"tokv_{p}", between)
                def before_b(p):
                    d = SETS[p]
                    pe.wait_ge(*A.at(f"tokk_{p}", i))
                    unit_products(wide(d.B[2], d.B[1]), unit(d.BT), lambda s, n: d.AR[s, :, n * CHUNK:(n + 1) * CHUNK], f"m1_{p}", after=0)
                def before_a(p):
                    d = SETS[p]
                    pe.wait_ge(*A.at(f"tokv_{p}", i))
                    unit_products(unit(d.B[0]), unit(d.AR[:, 0, :]), unit(d.BT), f"al_{p}", dense)
                def before_k(p):
                    d = SETS[p]
                    pe.wait_ge(*V.at(f"m1b_{p}", i))
                    unit_products(wide(d.B[1], d.B[2]), unit(d.KTL), lambda s, n: d.AR[s, :, n * CHUNK:(n + 1) * CHUNK], f"m2_{p}", after=0)
                def level_first(l, p):
                    d = SETS[p]
                    pe.wait_ge(*V.at(f"xi0_{p}" if l == 1 else f"xt{l - 1}_{p}", i))
                    unit_products(unit(d.B[0]), mat(d.MA1), mat(d.XI), f"t{l}_{p}", dense)
                def level_second(l, p):
                    d = SETS[p]
                    pe.wait_ge(*A.at(f"t{l}_{p}", i))
                    if l == 1:
                        pe.wait_ge(*V.at(f"xit0_{p}", i))
                    if l < LEVELS - 1:
                        unit_products(unit(d.B[1]), mat(d.XIT), mat(d.TS), f"x{l}_{p}", dense)
                    unit_products(unit(d.B[2]), mat(d.TS), mat(d.XIT), f"xt{l}_{p}", dense)
                def masked_values(p):
                    d = SETS[p]
                    pe.wait_ge(*A.at(f"t{LEVELS - 1}_{p}", i))
                    unit_products(unit(d.B[0]), mat(d.MA2), mat(d.VTOK), f"y_{p}", dense)
                def solved(p):
                    d = SETS[p]
                    pe.wait_ge(*A.at(f"y_{p}", i))
                    pe.wait_ge(*V.at(f"xt{LEVELS - 1}_{p}", i))
                    unit_products(wide(d.B[1], d.B[2]), mat(d.XIT), lambda s, n: d.AY[s, n, :], f"z_{p}", dense)
                def state_queries(p):
                    d = SETS[p]
                    pe.wait_ge(*A.at(f"z1_{p}", i))
                    unit_products(unit(d.B[0]), mat(d.ZS), lambda s, n: d.MA1[s, n, CHUNK:2 * CHUNK], f"q_{p}", dense)
                def state_step_in(p):
                    d = SETS[p]
                    unit_products(unit(d.B[1]), mat(d.ZS), mat(d.BTOK), f"gt_{p}", dense)
                def state_step(n, p):
                    d = SETS[p]
                    o = lambda s: d.B[2 if n % 2 == 0 else 0][s, n * HD:(n + 1) * HD]
                    pe.wait_ge(*V.at(f"s{n - 2}_{p}" if n >= 2 else f"gt_{p}", i))
                    pe.sem_inc(tensor_ready)
                    for h in range(2):
                        s = slice(h * HD, h * HD + HD)
                        pe.matmul(o(s), d.BTOK[s, n, :], d.ZS[s, n, HD:2 * HD], start=True, stop=False)
                        mm = pe.matmul(o(s), d.KTOK[s, n, :], d.VTOK[s, n, :], start=False, stop=n == 0)
                    if n:
                        pe.wait_ge(*V.at(f"s{n - 1}_{p}", i))
                        pe.sem_inc(tensor_ready)
                        for h in range(2):
                            s = slice(h * HD, h * HD + HD)
                            mm = pe.matmul(o(s), d.GT[s, n, :], d.SS[s, n, :], start=False, stop=True)
                    mm.then_inc(*S.inc(f"s{n}_{p}"))
                def result(p):
                    d = SETS[p]
                    pe.wait_ge(*V.at(f"s{CHUNKS - 2}_{p}", i))
                    pe.sem_inc(tensor_ready)
                    for n in range(CHUNKS):
                        for h in range(2):
                            s = slice(h * HD, h * HD + HD)
                            o = d.B[1][s, n * CHUNK:(n + 1) * CHUNK]
                            pe.matmul(o, d.ZS[s, n, HD:2 * HD], d.MA1[s, n, CHUNK:2 * CHUNK], start=True, stop=False)
                            mm = pe.matmul(o, d.VTOK[s, n, :], d.MA2[s, n, CHUNK:2 * CHUNK], start=False, stop=n == 0)
                            if n:
                                mm = pe.matmul(o, d.SS[s, n, :], d.QS[s, n, :], start=False, stop=True)
                    mm.then_inc(*S.inc(f"o_{p}"))

                def stream_of_products():
                    for q in range(1, STREAMED - 1):
                        yield from streamed(q)
                        yield from modulation(q + 3)
                    yield from streamed(STREAMED - 1)
                products = stream_of_products()
                def dense(n):
                    for _ in range(n):
                        next(products)
                low_ranks(0)
                low_ranks(1)
                whole(streamed(0), modulation(0))
                for p in TWO:
                    head_sums("kkss", p, SETS[p].B[0], SETS[p].E1[:, :], A.at(f"kksq_{p}", i))
                whole(modulation(1), modulation(2), modulation(3))
                head_sums("bonus", 0, SETS[0].B[1], SETS[0].RK[:, :], V.at("rk_0", i))
                dense(6)
                tokens(0)
                before_b(0)
                before_a(0)
                before_k(0)
                head_sums("bonus", 1, SETS[1].B[1], SETS[1].RK[:, :], V.at("rk_1", i))
                dense(8)
                tokens(1)
                dense(18)
                level_first(1, 0)
                before_b(1)
                level_second(1, 0)
                before_a(1)
                level_first(2, 0)
                before_k(1)
                level_first(1, 1)
                for l in range(2, LEVELS):
                    level_second(l, 0)
                    level_second(l - 1, 1)
                    if l + 1 < LEVELS:
                        level_first(l + 1, 0)
                    else:
                        masked_values(0)
                    level_first(l, 1)
                level_second(LEVELS - 1, 1)
                solved(0)
                masked_values(1)
                state_queries(0)
                solved(1)
                state_step_in(0)
                state_queries(1)
                state_step_in(1)
                for n in range(CHUNKS - 1):
                    for p in TWO:
                        state_step(n, p)
                    dense(3 if n < 2 else 2)
                for p in TWO:
                    result(p)
                for p in TWO:
                    head_sums("mean", p, SETS[p].B[2], SETS[p].OS[:, :], A.at(f"os_{p}", i))
                whole(modulation(8), modulation(9))
                for p in TWO:
                    head_sums("var", p, SETS[p].B[0], SETS[p].DSQ[:, :], A.at(f"dsq_{p}", i))
                whole(modulation(10), modulation(11))
                turn(5)

        def rwkv_scalar(act, st):
            A, V, S = st.act, st.dve, st.pe
            flat = lambda t: t[:, :, :].rearrange("p n c -> p (n c)")
            u3 = lambda t: t.rearrange("p (n c) -> p n c", n=CHUNKS)
            with act.Fori(0, PAIRS // 2) as i:
                def run(name, p, out, src, func, *waits, **more):
                    for w in waits:
                        act.wait_ge(*w)
                    act.activation(out, src, func, **more).then_inc(*A.inc(f"{name}_{p}"))
                def after(b):
                    round_block(act, st.b0 + b + 2, i, LOOP_BLOCKS)
                def after_mods(*ms):
                    for m in ms:
                        after(M_AT[m])
                        if m % 2:
                            g = m // 2
                            block_out(act, st.b0 + M_AT[m], i, LOOP_BLOCKS)
                            if g:
                                act.wait_ge(*S.at(f"turn{g - 1}", i))
                            act.activation(ROWS[:, :], bank[7][0:4, 0:ROW], ACT.Copy).then_inc(*A.inc(f"row{g}"))
                def raw(q):
                    block_out(act, st.b0 + S_AT[q], i, LOOP_BLOCKS)
                    after(S_AT[q])
                    act.wait_ge(*V.at(f"{'rkv'[q % 3]}_{q // 3}", i))
                    act.activation(PBUF[q // 3][:, q % 3, 1:T + 1], bank[6], ACT.Copy).then_inc(*A.inc(f"pb{q}"))
                def tokens(p):
                    d = SETS[p]
                    run("toka", p, d.AY[:, :, 0:HD], u3(d.B[0]), ACT.Copy, S.at(f"toka_{p}", i))
                    run("tokb", p, flat(d.BTOK), d.B[2], ACT.Copy, S.at(f"tokb_{p}", i))
                    run("tokk", p, flat(d.KTOK), d.B[1], ACT.Copy, S.at(f"tokk_{p}", i))
                    run("tokv", p, flat(d.VTOK), d.B[0], ACT.Copy, S.at(f"tokv_{p}", i))
                def level(l, p):
                    run(f"t{l}", p, flat(SETS[p].TS), SETS[p].B[0], ACT.Copy, S.at(f"t{l}_{p}", i))
                act.wait_ge(*V.before("yf_1", i))
                for p in TWO:
                    d = SETS[p]
                    j = i * 2 + p
                    run("sg", p, d.SG[:, :], d.B[0], ACT.Sigmoid, S.at(f"zw_{p}", i), bias=col("w0", j))
                    run("aa", p, d.AA[:, :], d.B[1], ACT.Sigmoid, S.at(f"za_{p}", i), bias=col("a0", j))
                    run("gg", p, d.GG[:, :], d.B[2], ACT.Copy, S.at(f"g_{p}", i))
                act.dma_start(W3S[:, :, :], lora[:, bass.ds(i * 2 + 2, 2), :]).then_inc(lora_in, 16)
                for p in TWO:
                    d = SETS[p]
                    run("kksq", p, d.E1[:, :], d.RKV[:, 1, :], ACT.Square, V.at(f"k_{p}", i), scale=col("k_k", i * 2 + p))
                raw(0)
                after_mods(0)
                for p in TWO:
                    d = SETS[p]
                    run("kkn", p, d.E3[:, :], d.B[0], ACT.Sqrt, S.at(f"kkss_{p}", i))
                for p in TWO:
                    d = SETS[p]
                    run("e1", p, d.E1[:, :], d.CSUM[:, :], ACT.Exp, V.at(f"csum_{p}", i), scale=-DECAY)
                    run("e2", p, d.E2[:, :], d.CSUM[:, :], ACT.Exp, scale=DECAY)
                after_mods(1)
                for p in TWO:
                    d = SETS[p]
                    run("am1", p, d.RK[:, :], d.AA[:, :], ACT.Identity, A.at(f"aa_{p}", i), scale=col("k_a", i * 2 + p), bias=KA1[:, bass.ds(i * 2 + p, 1)])
                def since_before(p):
                    d = SETS[p]
                    run("e3", p, d.E3[:, :], d.SG[:, :], ACT.Exp, V.at(f"cprev_{p}", i), V.at(f"kk_{p}", i), scale=-DECAY)
                after_mods(2)
                since_before(0)
                after_mods(3)
                tokens(0)
                since_before(1)
                raw(1)
                tokens(1)
                after_mods(4)
                level(1, 0)
                raw(2)
                level(2, 0)
                after_mods(5)
                level(1, 1)
                level(3, 0)
                level(2, 1)
                level(4, 0)
                raw(3)
                level(3, 1)
                after_mods(6)
                level(5, 0)
                level(4, 1)
                def masked_values(p):
                    run("y", p, SETS[p].AY[:, :, HD:2 * HD], u3(SETS[p].B[0]), ACT.Copy, S.at(f"y_{p}", i))
                def solved(p):
                    d = SETS[p]
                    for z in range(2):
                        run(f"z{z}", p, d.ZS[:, z * HALF:(z + 1) * HALF, :].rearrange("p n c -> p (n c)"), d.B[1 + z], ACT.Copy, S.at(f"z_{p}", i))
                masked_values(0)
                level(5, 1)
                solved(0)
                raw(4)
                masked_values(1)
                after_mods(7)
                solved(1)
                raw(5)
                for p in TWO:
                    run("os", p, SETS[p].OS[:, :], SETS[p].B[1], ACT.Copy, S.at(f"o_{p}", i))
                for p in TWO:
                    run("dsq", p, SETS[p].DSQ[:, :], SETS[p].DV[:, :], ACT.Square, V.at(f"dd_{p}", i))
                after_mods(8, 9)
                for p in TWO:
                    run("sd", p, SETS[p].E1[:, :], SETS[p].B[0], ACT.Sqrt, S.at(f"var_{p}", i), scale=1.0 / HD, bias=EPS[:, 1:2])
                after_mods(10, 11)

        def rwkv_vector(dve, st):
            st.enter(dve, "dve")
            A, V, S = st.act, st.dve, st.pe
            n8 = lambda t: t.rearrange("p (n c) -> p n c", c=CHUNK)
            rep = lambda t, n=CHUNKS: t.rearrange("p (o c) -> p o c", o=1).to_broadcast([P, n, t.shape[1]])
            ident = rep(FCC[:, FC["eye2"]:FC["eye2"] + CHUNK])
            pair_mask = rep(FCC[:, FC["before"]:FC["before"] + 2 * CHUNK], HALF)
            after_mask = rep(FCC[:, FC["after"]:FC["after"] + CHUNK])
            with dve.Fori(0, PAIRS // 2) as i:
                def tt(name, out, a, b, op, *waits):
                    for w in waits:
                        dve.wait_ge(*w)
                    dve.tensor_tensor(out, a, b, op).then_inc(*V.inc(name))
                def stt(name, out, a, s, b, op0, op1, *waits):
                    for w in waits:
                        dve.wait_ge(*w)
                    dve.scalar_tensor_tensor(out=out, in0=a, scalar=s, in1=b, op0=op0, op1=op1).then_inc(*V.inc(name))
                def ts(name, out, a, s1, s2, op0, op1, *waits):
                    for w in waits:
                        dve.wait_ge(*w)
                    dve.tensor_scalar(out, a, s1, s2, op0, *([op1] if op1 is not None else [])).then_inc(*V.inc(name))
                def inverse(name, t, *waits):
                    for w in waits:
                        dve.wait_ge(*w)
                    dve.reciprocal(t, t).then_inc(*V.inc(name))
                def shift(c, p):
                    n, out, b = "rkv"[c], SETS[p].RKV[:, c, :], PBUF[p]
                    tt(f"d{n}_{p}", out, b[:, c, 0:T], b[:, c, 1:T + 1], ALU.subtract)
                    stt(f"{n}_{p}", out, out, col("mu_rkv", i * 6 + (p * 3 + c)), b[:, c, 1:T + 1], ALU.mult, ALU.add, V.at(f"d{n}_{p}", i))
                def unit_key(p):
                    d = SETS[p]
                    ts(f"kkmax_{p}", d.E3[:, :], d.E3[:, :], 1e-12, None, ALU.max, None, A.at(f"kkn_{p}", i))
                    inverse(f"kkinv_{p}", d.E3[:, :], V.at(f"kkmax_{p}", i))
                    stt(f"kk_{p}", d.KK[:, :], d.RKV[:, 1, :], col("k_k", i * 2 + p), d.E3[:, :], ALU.mult, ALU.mult, V.at(f"kkinv_{p}", i))
                    tt(f"kp_{p}", d.KP[:, :], d.RK[:, :], d.RKV[:, 1, :], ALU.mult, A.at(f"am1_{p}", i))
                    stt(f"rk_{p}", d.RK[:, :], d.RKV[:, 0, :], col("r_k", i * 2 + p), d.KP[:, :], ALU.mult, ALU.mult, V.at(f"kp_{p}", i))
                def decayed_a(p):
                    d = SETS[p]
                    tt(f"rt_{p}", d.AR[:, 1, :], d.RKV[:, 0, :], d.E1[:, :], ALU.mult, A.at(f"e1_{p}", i))
                    tt(f"bb_{p}", d.BT[:, :], d.KK[:, :], d.AA[:, :], ALU.mult)
                    stt(f"at_{p}", d.AR[:, 0, :], d.KK[:, :], -1.0, d.E3[:, :], ALU.mult, ALU.mult, A.at(f"e3_{p}", i))
                def decayed_b(p):
                    d = SETS[p]
                    tt(f"bt_{p}", d.BT[:, :], d.BT[:, :], d.E2[:, :], ALU.mult, V.at(f"bb_{p}", i))
                    tt(f"ktl_{p}", d.KTL[:, :], d.KP[:, :], d.E2[:, :], ALU.mult)
                    tt(f"bon_{p}", d.BON[:, :], d.B[1], d.VS, ALU.mult, S.at(f"bonus_{p}", i))
                def masked(name, p, dst, banks):
                    for z in range(2):
                        tt(f"{name}{'ab'[z]}_{p}", dst[:, z * HALF:(z + 1) * HALF, :], banks[z].rearrange("p (n c) -> p n c", n=HALF),
                           pair_mask, ALU.mult, S.at(f"{name}_{p}", i))
                def first_level(p):
                    d = SETS[p]
                    tt(f"al_{p}", d.AL[:, :, :], n8(d.B[0]), after_mask, ALU.mult, S.at(f"al_{p}", i))
                    dve.tensor_copy(d.XI[:, :, :], ident).then_inc(*V.inc(f"xi_{p}"))
                    dve.wait_ge(*V.at(f"xi_{p}", i))
                    dve.sem_inc(vector_ready)
                    dve.copy_predicated(d.XI[:, :, :], rep(LVL[:, 0, :]), d.AL[:, :, :]).then_inc(*V.inc(f"xi0_{p}"))
                    masked("m2", p, d.MA2, (d.B[1], d.B[2]))
                    dve.tensor_copy(d.XIT[:, :, :], ident).then_inc(*V.inc(f"xit_{p}"))
                    dve.wait_ge(*V.at(f"xit_{p}", i))
                    dve.sem_inc(vector_ready)
                    dve.copy_predicated(d.XIT[:, :, :], rep(LVL[:, LEVELS, :]), d.MA1[:, :, 0:CHUNK]).then_inc(*V.inc(f"xit0_{p}"))
                def level(l, p):
                    d = SETS[p]
                    dve.wait_ge(*S.at(f"xt{l}_{p}", i))
                    dve.sem_inc(vector_ready)
                    if l < LEVELS - 1:
                        dve.copy_predicated(d.XI[:, :, :], rep(LVL[:, l, :]), n8(d.B[1])).then_inc(*V.inc(f"x{l}_{p}"))
                    dve.copy_predicated(d.XIT[:, :, :], rep(LVL[:, l + LEVELS, :]), n8(d.B[2])).then_inc(*V.inc(f"xt{l}_{p}"))
                for p in TWO:
                    shift(1, p)
                for p in TWO:
                    d = SETS[p]
                    shift(0, p)
                    shift(2, p)
                    dve.wait_ge(*A.at(f"sg_{p}", i))
                    dve.tensor_tensor_scan(d.CSUM[:, :], FCC[:, FC["scan"]:FC["scan"] + T], d.SG[:, :], 0.0, ALU.mult, ALU.add)\
                       .then_inc(*V.inc(f"csum_{p}"))
                    tt(f"cprev_{p}", d.SG[:, :], d.CSUM[:, :], d.SG[:, :], ALU.subtract, V.at(f"csum_{p}", i))
                unit_key(0)
                decayed_a(0)
                decayed_b(0)
                unit_key(1)
                masked("m1", 0, SETS[0].MA1, (SETS[0].B[2], SETS[0].B[1]))
                decayed_a(1)
                first_level(0)
                decayed_b(1)
                level(1, 0)
                masked("m1", 1, SETS[1].MA1, (SETS[1].B[2], SETS[1].B[1]))
                first_level(1)
                for l in range(2, LEVELS):
                    level(l, 0)
                    level(l - 1, 1)
                level(LEVELS - 1, 1)
                for p in TWO:
                    d = SETS[p]
                    tt(f"q_{p}", d.QS[:, :, :], n8(d.B[0]), n8(d.AR[:, 1, :]), ALU.add, S.at(f"q_{p}", i))
                    tt(f"gt_{p}", d.GT[:, :, :], n8(d.B[1]), ident, ALU.add, S.at(f"gt_{p}", i))
                for n in range(CHUNKS - 1):
                    end = (n + 1) * CHUNK - 1
                    for p in TWO:
                        d = SETS[p]
                        ts(f"s{n}_{p}", d.SS[:, n + 1, :], d.B[2 if n % 2 == 0 else 0][:, n * HD:(n + 1) * HD], d.E1[:, end:end + 1], None,
                           ALU.mult, None, S.at(f"s{n}_{p}", i))
                for p in TWO:
                    d = SETS[p]
                    stt(f"dd_{p}", d.DV[:, :], d.B[2], -1.0 / HD, d.OS[:, :], ALU.mult, ALU.add, S.at(f"mean_{p}", i))
                for p in TWO:
                    d = SETS[p]
                    dv = d.DV[:, :]
                    inverse(f"rinv_{p}", d.E1[:, :], A.at(f"sd_{p}", i))
                    tt(f"n0_{p}", dv, dv, d.E1[:, :], ALU.mult, V.at(f"rinv_{p}", i))
                    ts(f"n1_{p}", dv, dv, col("ln_w", i * 2 + p), col("ln_b", i * 2 + p), ALU.mult, ALU.add, V.at(f"n0_{p}", i))
                    tt(f"n2_{p}", dv, dv, d.BON[:, :], ALU.add, V.at(f"n1_{p}", i))
                    tt(f"yf_{p}", YA[:, i * 2 + p, :], dv, d.GG[:, :], ALU.mult, V.at(f"n2_{p}", i))
                dve.wait_ge(*S.at("turn5", i))
                turned = bank[7][:, ROW:ROW + 4 * MODS].rearrange("p (m c) -> p m c", c=4)
                for l in range(LAYERS):
                    ms = slice(l * PER_LAYER, (l + 1) * PER_LAYER)
                    bias = VEC[:, bass.ds(COL[f"b_mod{l}"] + i * PER_LAYER, PER_LAYER)].rearrange("p (n o) -> p n o", o=1).to_broadcast([P, PER_LAYER, 2])
                    ins = dve.tensor_tensor(MOD_SUM[:, ms, :], turned[:, ms, 0:2], bias, ALU.add)
                ins.then_inc(*V.inc("mod_sum"))
                dve.wait_ge(*V.at("mod_sum", i))
                for l in range(LAYERS):
                    ms = slice(l * PER_LAYER, (l + 1) * PER_LAYER)
                    ins = dve.tensor_tensor(MOD[:, bass.ds(l * MOD_TILES + i * PER_LAYER, PER_LAYER), :], turned[:, ms, 2:4], MOD_SUM[:, ms, :], ALU.add)
                ins.then_inc(*V.inc("mods"))
        YALO = place("YALO", [P, KT, T], after_h, F32R)
        att_at = Area(after_ya)
        YAHI = att_at("YAHI", [P, KT, T], F32R)
        after_yh = att_at.at
        QT, KTT = att_at("QT", [P, AT_TILES, T]), att_at("KTT", [P, AT_TILES, T])
        VT = att_at("VT", [P, AT_TILES, BLOCKS, P])
        UU, MM, DD = (att_at(n, [P, 3, T]) for n in ("UU", "MM", "DD"))
        RS = att_at("RS", [P, 2, T])
        PT = att_at("PT", [P, 4 * 2 * P])
        assert att_at.at <= pbuf_at, (att_at.at, pbuf_at)
        att_at.at = after_yh
        YBHI, YBLO = att_at("YBHI", [P, AT_TILES, T], F32R), att_at("YBLO", [P, AT_TILES, T], F32R)
        after_yb = att_at.at
        att_at.at = after_pairs
        SQA, VCH, RNA = (att_at(n, [P, 2, T]) for n in ("SQA", "VCH", "RNA"))
        att_at.at = after_pairs
        SMB = att_at("SMB", [P, 2, 4 * 2 * P])
        PEX = att_at("PEX", [P, 4 * 2 * P])
        MX, NM, DEN = (att_at(n, [P, 4 * AT_TILES, BLOCKS]) for n in ("MX", "NM", "DEN"))
        GROUPS = 3
        att_at.at = pbuf_at
        UU2, DD2 = att_at("UU2", [P, 3, T]), att_at("DD2", [P, 3, T])
        assert att_at.at <= after_pairs
        PARTS = [(UU[:, :, :], MM[:, :, :], DD[:, :, :]),
                 (UU2[:, :, :], VT[:, :, :, :].rearrange("p (g h) b n -> p g h (b n)", h=2)[:, :, 0, :], DD2[:, :, :])]
        UNITS_AT = [(2 * g + hp, g, h) for hp in range(2) for g in range(GROUPS) for h in range(2)]

        def in_order(t, g):
            return t if g == 0 else t.rearrange("p (i d) -> p d i", d=4 if g == 1 else 16)

        def ordered(t, g):
            return t if g == 0 else t.rearrange("p (d i) -> p d i", d=4 if g == 1 else 16)

        ain_pe, ain_act, ain_dve = [], [], []
        for c in range(AT_TILES):
            ain_pe += [f"sum{c}q"] + ([f"vt{c - 1}"] if c else []) + [f"sum{c}k"]
            ain_act += [f"sq{c}q", f"sd{c}q", f"sq{c}k", f"sd{c}k", f"vc{c}", f"yh{c}"]
            ain_dve += ([f"vt{c - 1}"] if c else []) + [f"ri{c}q", f"n{c}q", f"ri{c}k", f"n{c}k", f"yl{c}"]
        ain_pe += [f"vt{AT_TILES - 1}"]
        ain_act += [f"yh{t}" for t in range(AT_TILES, KT)]
        ain_dve += [f"vt{AT_TILES - 1}"] + [f"yl{t}" for t in range(AT_TILES, KT)]

        def projected(c, s):
            return PBUF[c][:, s, 1:T + 1] if c < 2 else bank[(3 * (c - 2) + s) % 4]

        def attention_in_tensor(pe, st):
            A, V, S = st.act, st.dve, st.pe
            st.enter(pe, "pe")
            def stream_tile(c, s):
                if c < 2:
                    return
                n = 3 * (c - 2) + s
                if n >= 4:
                    m = n - 4
                    pe.wait_ge(*(A.at(f"vc{m // 3 + 2}") if m % 3 == 2 else V.at(f"n{m // 3 + 2}{'qk'[m % 3]}")))
                block_ready(pe, st.b0 + n)
                product(pe, bank[n % 4], (st.b0 + n) % 2, ALLK, h_hi, h_lo, WHOLE).then_inc(k.blocks_used, 1)
            def head_sum(c, s):
                name = f"{c}{'qk'[s]}"
                pe.wait_ge(*A.at(f"sq{name}"))
                if c:
                    pe.wait_ge(*A.at(f"sd{c - 1}{'qk'[s]}"))
                pe.matmul(bank[4 + s], heads, SQA[:, s, :], start=True, stop=True).then_inc(*S.inc(f"sum{name}"))
            def v_tokens(c):
                pe.wait_ge(*A.at(f"vc{c}"))
                if c >= 2:
                    pe.wait_ge(*V.at(f"vt{c - 2}"))
                for b in range(BLOCKS):
                    mm = pe.transpose(bank[6 + c % 2][:, b * P:(b + 1) * P], VCH[:, c % 2, b * P:(b + 1) * P], eye)
                mm.then_inc(*S.inc(f"vt{c}"))
            stream_tile(2, 0)
            stream_tile(2, 1)
            for c in range(AT_TILES):
                if c > 2:
                    stream_tile(c, 0)
                    stream_tile(c, 1)
                head_sum(c, 0)
                if c:
                    v_tokens(c - 1)
                stream_tile(c, 2)
                head_sum(c, 1)
            v_tokens(AT_TILES - 1)

        def attention_in_scalar(act, st):
            A, V, S = st.act, st.dve, st.pe
            st.enter(act, "act")
            act.wait_ge(lora_in, 16 * (PAIRS // 2 + 1))
            def split_y(t):
                act.activation(YAHI[:, t, :], YA[:, t, :], ACT.Copy).then_inc(*A.inc(f"yh{t}"))
            for c in range(AT_TILES):
                for s in range(3):
                    if c >= 2:
                        n = 3 * (c - 2) + s
                        block_out(act, st.b0 + n)
                        round_block(act, st.b0 + n + 2)
                    if s == 2:
                        if c >= 2:
                            act.wait_ge(*S.at(f"vt{c - 2}"))
                        act.activation(ordered(VCH[:, c % 2, :], c // 2), in_order(projected(c, s), c // 2), ACT.Copy)\
                           .then_inc(*A.inc(f"vc{c}"))
                        continue
                    name = f"{c}{'qk'[s]}"
                    if c:
                        act.wait_ge(*S.at(f"sum{c - 1}{'qk'[s]}"))
                    act.activation(SQA[:, s, :], projected(c, s), ACT.Square).then_inc(*A.inc(f"sq{name}"))
                    act.wait_ge(*S.at(f"sum{name}"))
                    if c:
                        act.wait_ge(*V.at(f"n{c - 1}{'qk'[s]}"))
                    act.activation(RNA[:, s, :], bank[4 + s], ACT.Sqrt, scale=1.0 / HD, bias=EPS[:, 0:1])\
                       .then_inc(*A.inc(f"sd{name}"))
                split_y(c)
            for t in range(AT_TILES, KT):
                split_y(t)

        def attention_in_vector(dve, st):
            A, V, S = st.act, st.dve, st.pe
            st.enter(dve, "dve")
            def v_out(c):
                dve.wait_ge(*S.at(f"vt{c}"))
                dve.tensor_copy(VT[:, c, :, :].rearrange("p b n -> p (b n)"), bank[6 + c % 2]).then_inc(*V.inc(f"vt{c}"))
            def split_y(t):
                dve.wait_ge(*A.at(f"yh{t}"))
                dve.tensor_tensor(YALO[:, t, :], YA[:, t, :], YAHI[:, t, :].bitcast(F32), ALU.subtract).then_inc(*V.inc(f"yl{t}"))
            for c in range(AT_TILES):
                if c:
                    v_out(c - 1)
                for s, (dst, gain) in enumerate(((QT, "q_norm"), (KTT, "k_norm"))):
                    name = f"{c}{'qk'[s]}"
                    dve.wait_ge(*A.at(f"sd{name}"))
                    dve.reciprocal(RNA[:, s, :], RNA[:, s, :]).then_inc(*V.inc(f"ri{name}"))
                    dve.wait_ge(*V.at(f"ri{name}"))
                    g = c // 2
                    dve.scalar_tensor_tensor(out=ordered(dst[:, c, :], g), in0=in_order(projected(c, s), g), scalar=col(gain),
                                             in1=in_order(RNA[:, s, :], g), op0=ALU.mult, op1=ALU.mult).then_inc(*V.inc(f"n{name}"))
                split_y(c)
            v_out(AT_TILES - 1)
            for t in range(AT_TILES, KT):
                split_y(t)

        NU = len(UNITS_AT)
        COMBINE = (("max0", "max", "sub"), ("de", "s0", "s1"), ("ri", "al"), ("y",), ("lo",))
        att_pe, att_act, att_dve = ["sc0"], [], ["neg"]
        for u in range(NU):
            att_pe += ([f"sc{u + 1}"] if u + 1 < NU else []) + [f"tr{u}", f"pv{u}", f"mb{u}", f"db{u}"]
            att_act += [f"ex{u}", f"pt{u}", f"u{u}", f"m{u}"]
            att_dve += [f"mk{u}", f"mx{u}", f"nm{u}"] + ([f"d{u - 1}"] if u else [])
            att_dve += [f"{n}0" for n in COMBINE[u - NU // 2]] if 0 <= u - NU // 2 < len(COMBINE) else []
            att_act += {NU // 2: ["e0"], NU // 2 + 3: ["hi0"], NU - 1: ["e1", "hi1"]}.get(u, [])
        att_dve += [f"d{NU - 1}"] + [f"{n}1" for names in COMBINE for n in names]

        def width(g):
            return 2 if g == 0 else 1

        def attention_tensor(pe, st):
            A, V, S = st.act, st.dve, st.pe
            st.enter(pe, "pe")
            def scores(u):
                c, g, h = UNITS_AT[u]
                hs = slice(h * HD, h * HD + HD)
                if u >= 2:
                    pe.wait_ge(*V.at(f"d{u - 2}"))
                for b in range(BLOCKS):
                    k0 = max(b - width(g) + 1, 0)
                    dst = two_banks[u % 2][:, (2 * b + 2 - (b + 1 - k0)) * P:(2 * b + 2) * P]
                    mm = pe.matmul(dst, QT[hs, c, b * P:(b + 1) * P], KTT[hs, c, k0 * P:(b + 1) * P], start=True, stop=True)
                mm.then_inc(*S.inc(f"sc{u}"))
            scores(0)
            for u, (c, g, h) in enumerate(UNITS_AT):
                hs = slice(h * HD, h * HD + HD)
                if u + 1 < NU:
                    scores(u + 1)
                keys = [(b, w) for b in range(BLOCKS) for w in range(2 - width(g), 2) if b + w >= 1]
                pe.wait_ge(*A.at(f"ex{u}"))
                if u:
                    pe.wait_ge(*A.at(f"pt{u - 1}"))
                for b, w in keys:
                    mm = pe.transpose(two_banks[2][:, (2 * b + w) * P:(2 * b + w + 1) * P], PEX[:, (2 * b + w) * P:(2 * b + w + 1) * P], eye)
                mm.then_inc(*S.inc(f"tr{u}"))
                pe.wait_ge(*A.at(f"pt{u}"))
                if u >= 2:
                    pe.wait_ge(*A.at(f"u{u - 2}"))
                for b, w in keys:
                    first = w == 1 and (width(g) == 1 or b == 0)
                    mm = pe.matmul(bank[6][hs, b * P:(b + 1) * P], VT[:, c, b + w - 1, hs], PT[:, (2 * b + w) * P:(2 * b + w + 1) * P],
                                   start=first or w == 0, stop=w == 1)
                mm.then_inc(*S.inc(f"pv{u}"))
                if u >= 2:
                    pe.wait_ge(*A.at(f"m{u - 2}"))
                for b in range(BLOCKS):
                    mm = pe.matmul(bank[7][hs, b * P:(b + 1) * P], MX[:, u, b:b + 1].to_broadcast([P, HD]), eye, start=True, stop=True)
                mm.then_inc(*S.inc(f"mb{u}"))
                for b in range(BLOCKS):
                    mm = pe.matmul(two_banks[u % 2][hs, b * P:(b + 1) * P], DEN[:, u, b:b + 1].to_broadcast([P, HD]), eye, start=True, stop=True)
                mm.then_inc(*S.inc(f"db{u}"))

        def attention_scalar(act, st):
            A, V, S = st.act, st.dve, st.pe
            st.enter(act, "act")
            def weights(hp):
                mm = PARTS[hp][1]
                act.wait_ge(*V.at(f"sub{hp}"))
                act.activation(mm, mm, ACT.Exp, scale=HD ** -0.5).then_inc(*A.inc(f"e{hp}"))
            def high(hp):
                act.wait_ge(*V.at(f"y{hp}"))
                for g in range(GROUPS):
                    ins = act.activation(YBHI[:, 2 * g + hp, :], PARTS[hp][0][:, g, :], ACT.Copy)
                ins.then_inc(*A.inc(f"hi{hp}"))
            for u, (c, g, h) in enumerate(UNITS_AT):
                hs = slice(h * HD, h * HD + HD)
                act.wait_ge(*V.at(f"nm{u}"))
                if u:
                    act.wait_ge(*S.at(f"tr{u - 1}"))
                for b in range(BLOCKS):
                    cols = slice((2 * b + 2 - width(g)) * P, (2 * b + 2) * P)
                    ins = act.activation(PEX[:, cols], SMB[:, u % 2, cols], ACT.Exp, scale=HD ** -0.5, bias=NM[:, u, b:b + 1],
                                         accum_out=DEN[:, u, b:b + 1])
                ins.then_inc(*A.inc(f"ex{u}"))
                act.wait_ge(*S.at(f"tr{u}"))
                if u:
                    act.wait_ge(*S.at(f"pv{u - 1}"))
                four = lambda t: t.rearrange("p (b w n) -> p b w n", b=BLOCKS, w=2)[:, :, 2 - width(g):, :]
                if g == 0:
                    act.activation(PT[:, P:], two_banks[2][:, P:], ACT.Copy).then_inc(*A.inc(f"pt{u}"))
                else:
                    act.activation(four(PT[:, :]), four(two_banks[2]), ACT.Copy).then_inc(*A.inc(f"pt{u}"))
                act.wait_ge(*S.at(f"pv{u}"))
                act.activation(in_order(PARTS[c % 2][0][hs, g, :], g), ordered(bank[6][hs, :], g), ACT.Copy).then_inc(*A.inc(f"u{u}"))
                act.wait_ge(*S.at(f"mb{u}"))
                act.activation(in_order(PARTS[c % 2][1][hs, g, :], g), ordered(bank[7][hs, :], g), ACT.Copy).then_inc(*A.inc(f"m{u}"))
                if u == NU // 2:
                    weights(0)
                if u == NU // 2 + 3:
                    high(0)
            weights(1)
            high(1)

        def attention_vector(dve, st):
            A, V, S = st.act, st.dve, st.pe
            st.enter(dve, "dve")
            dve.memset(SMB[:, :, 0:P], NEG_INF).then_inc(*V.inc("neg"))
            dve.wait_ge(*V.at("neg"))
            mask = lambda n, w: FCC[:, FC["masks"] + n * P:FC["masks"] + (n + w) * P]
            four = lambda t: t.rearrange("p (b n) -> p b n", b=BLOCKS)
            all3 = lambda t: t.rearrange("p (o n) -> p o n", o=1).to_broadcast([P, GROUPS, T])
            def den_out(u):
                c, g, h = UNITS_AT[u]
                hs = slice(h * HD, h * HD + HD)
                dve.wait_ge(*S.at(f"db{u}"))
                dve.tensor_copy(in_order(PARTS[c % 2][2][hs, g, :], g), ordered(two_banks[u % 2][hs, 0:T], g)).then_inc(*V.inc(f"d{u}"))
            def combine(hp, part):
                uu, mm, dd = PARTS[hp]
                tt = lambda name, out, a, b, op: dve.tensor_tensor(out, a, b, op).then_inc(*V.inc(f"{name}{hp}"))
                after = lambda name: dve.wait_ge(*V.at(f"{name}{hp}"))
                if part == 0:
                    dve.wait_ge(*A.at(f"m{hp * 6 + 5}"))
                    dve.wait_ge(*V.at(f"d{hp * 6 + 5}"))
                    tt("max0", RS[:, 0, :], mm[:, 0, :], mm[:, 1, :], ALU.max)
                    after("max0")
                    tt("max", RS[:, 1, :], RS[:, 0, :], mm[:, 2, :], ALU.max)
                    after("max")
                    tt("sub", mm, mm, all3(RS[:, 1, :]), ALU.subtract)
                elif part == 1:
                    dve.wait_ge(*A.at(f"e{hp}"))
                    tt("de", dd, dd, mm, ALU.mult)
                    after("de")
                    tt("s0", RS[:, 0, :], dd[:, 0, :], dd[:, 1, :], ALU.add)
                    after("s0")
                    tt("s1", RS[:, 1, :], RS[:, 0, :], dd[:, 2, :], ALU.add)
                elif part == 2:
                    after("s1")
                    dve.reciprocal(RS[:, 0, :], RS[:, 1, :]).then_inc(*V.inc(f"ri{hp}"))
                    after("ri")
                    tt("al", mm, mm, all3(RS[:, 0, :]), ALU.mult)
                elif part == 3:
                    after("al")
                    tt("y", uu, uu, mm, ALU.mult)
                else:
                    dve.wait_ge(*A.at(f"hi{hp}"))
                    for g in range(GROUPS):
                        ins = dve.tensor_tensor(YBLO[:, 2 * g + hp, :], uu[:, g, :], YBHI[:, 2 * g + hp, :].bitcast(F32), ALU.subtract)
                    ins.then_inc(*V.inc(f"lo{hp}"))
            for u, (c, g, h) in enumerate(UNITS_AT):
                sm = SMB[:, u % 2, :]
                sc = two_banks[u % 2]
                dve.wait_ge(*S.at(f"sc{u}"))
                if u >= 2:
                    dve.wait_ge(*A.at(f"ex{u - 2}"))
                if g == 0:
                    dve.tensor_tensor(sm[:, P:2 * P], sc[:, P:2 * P], mask(1, 1), ALU.add)
                    dve.tensor_tensor(four(sm)[:, 1:, :], four(sc)[:, 1:, :], mask(0, 2).rearrange("p (o n) -> p o n", o=1)
                                      .to_broadcast([P, BLOCKS - 1, 2 * P]), ALU.add).then_inc(*V.inc(f"mk{u}"))
                else:
                    dve.tensor_tensor(four(sm)[:, :, P:], four(sc)[:, :, P:], mask(g, 1).rearrange("p (o n) -> p o n", o=1)
                                      .to_broadcast([P, BLOCKS, P]), ALU.add).then_inc(*V.inc(f"mk{u}"))
                dve.wait_ge(*V.at(f"mk{u}"))
                dve.tensor_reduce(MX[:, u, :], four(sm)[:, :, (2 - width(g)) * P:], AX, ALU.max).then_inc(*V.inc(f"mx{u}"))
                dve.wait_ge(*V.at(f"mx{u}"))
                dve.tensor_scalar(NM[:, u, :], MX[:, u, :], -HD ** -0.5, None, ALU.mult).then_inc(*V.inc(f"nm{u}"))
                if u:
                    den_out(u - 1)
                if 0 <= u - NU // 2 < len(COMBINE):
                    combine(0, u - NU // 2)
            den_out(NU - 1)
            for part in range(len(COMBINE)):
                combine(1, part)

        ma = Area(after_yb)
        MHI, MLO = ma("MHI", [P, KT, T], F32R), ma("MLO", [P, KT, T], F32R)
        GAB, PAB, MF = ma("GAB", [P, 2, T]), ma("PAB", [P, 2, T]), ma("MF", [P, T])
        xc_at = (arena - 4 * KT * TC) // 64 * 64
        XC = place("XC", [P, KT, TC], xc_at)
        SIN = place("SIN", [P, T], xc_at - 4 * T)
        assert max(ma.at, upper) <= xc_at - 4 * T

        def merge_tensor(pe, st):
            A, V = st.act, st.dve
            pe.wait_ge(*att.dve.at(f"d{NU - 1}"))
            ALLB = [(u, u) for u in range(AT_TILES)]
            with pe.Fori(0, KT) as n:
                for q in range(4):
                    pe.wait_ge(*(A.before(f"gate{q}", n) if q < 2 else V.before(f"mul{q - 2}", n)))
                    if q == 2:
                        pe.wait_ge(*att_in.dve.at(f"yl{KT - 1}"))
                    if q == 3:
                        pe.wait_ge(*att.dve.at("lo1"))
                    block_ready(pe, st.b0 + q, n, 4)
                    hi, lo = ((h_hi, h_lo), (h_hi, h_lo), (lambda t: YAHI[:, t, :], lambda t: YALO[:, t, :]),
                              (lambda t: YBHI[:, t, :], lambda t: YBLO[:, t, :]))[q]
                    product(pe, bank[q], (st.b0 + q) % 2, ALLB if q == 3 else ALLK, hi, lo, WHOLE).then_inc(k.blocks_used, 1)

        def merge_scalar(act, st):
            A, V = st.act, st.dve
            st.enter(act, "act")
            act.dma_start(XC[:, :, :], ctxT).then_inc(ctx_in, 16)
            act.dma_start(TRIG[:, :], trig[:, 0:SC["total"]]).then_inc(trig_in, 16)
            act.dma_start(SIN[:, :], trig[:, SC["total"]:]).then_inc(sin_in, 16)
            with act.Fori(0, KT) as n:
                for q in range(4):
                    block_out(act, st.b0 + q, n, 4)
                    round_block(act, st.b0 + q + 2, n, 4)
                    if q < 2:
                        act.wait_ge(*V.before(f"mul{q}", n))
                        act.activation(GAB[:, q, :], bank[q], ACT.Sigmoid, bias=col("b_gate", n + q * KT)).then_inc(*A.inc(f"gate{q}"))
                act.wait_ge(*V.at("sum", n))
                act.activation(MHI[:, n, :], MF[:, :], ACT.Copy).then_inc(*A.inc("hi"))

        def merge_vector(dve, st):
            A, V = st.act, st.dve
            st.enter(dve, "dve")
            with dve.Fori(0, KT) as n:
                for q in range(2):
                    block_out(dve, st.b0 + 2 + q, n, 4)
                    dve.wait_ge(*V.before("lo", n))
                    dve.wait_ge(*A.at(f"gate{q}", n))
                    dve.tensor_tensor(PAB[:, q, :], bank[2 + q], GAB[:, q, :], ALU.mult).then_inc(*V.inc(f"mul{q}"))
                dve.wait_ge(*V.at("mul1", n))
                dve.tensor_tensor(MF[:, :], PAB[:, 0, :], PAB[:, 1, :], ALU.add).then_inc(*V.inc("sum"))
                dve.wait_ge(*A.at("hi", n))
                dve.tensor_tensor(MLO[:, n, :], MF[:, :], MHI[:, n, :].bitcast(F32), ALU.subtract).then_inc(*V.inc("lo"))

        def out_tensor(pe, st):
            st.enter(pe, "pe")
            with pe.Fori(0, KT // 2) as i:
                for n in range(2):
                    pe.wait_ge(*st.dve.before(f"x{n}", i))
                    block_ready(pe, st.b0 + n, i, 2)
                    product(pe, bank[4 + n], (st.b0 + n) % 2, ALLK, lambda t: MHI[:, t, :], lambda t: MLO[:, t, :], WHOLE)\
                        .then_inc(k.blocks_used, 1)

        def out_scalar(act, st):
            with act.Fori(0, KT // 2) as i:
                for n in range(2):
                    round_block(act, st.b0 + n + 2, i, 2)

        def out_vector(dve, st):
            st.enter(dve, "dve")
            with dve.Fori(0, KT // 2) as i:
                for n in range(2):
                    block_out(dve, st.b0 + n, i, 2)
                    dve.tensor_tensor(X[:, i * 2 + n, :], bank[4 + n], X[:, i * 2 + n, :], ALU.add).then_inc(*st.dve.inc(f"x{n}"))

        class Layer:
            def __init__(self, l):
                self.l, self.last = l, l == LAYERS - 1
                self.width = T if self.last else TT
                self.parts = [(0, T)] if self.last else [(0, T), (T, TC)]
                l0 = l * MOD_TILES
                self.gain = Stage(k, 0, (), (), ("gain",))
                self.norm = Norm((SQ4B, HFB, STDB, RSTDB), *[
                    ((lambda t, src=src: src[:, t, :]), n, (lambda t, at=at, n=n: H2HI[:, t, at:at + n]),
                     (lambda t, at=at, n=n: H2LO[:, t, at:at + n]), (lambda t, c=c: MG[:, t, c:c + 1]),
                     (lambda t, c=c: MOD[:, l0 + t, c:c + 1])) for c, (src, at, n) in enumerate(((X, 0, T), (XC, T, TC)))])
                pe, act, dve = self.win_steps()
                self.win = Stage(k, len(WIN2), pe, act, dve)
                self.gate = Stage(k, 2, (), ("gate0", "gate1"), (), GATE2_BLOCKS // 2)
                self.taps = Stage(k, 0, (), (), ["first0", "first1", "bias0", "bias1"])
                self.tap = Stage(k, 0, (), (), ["tap0", "tap1"], CONV_K - 1)
                pe, act, dve = self.small_steps()
                self.small = Stage(k, SMALL2_BLOCKS, pe, act, dve)
                pe, act, dve = self.heads_steps()
                self.heads = Stage(k, 0, pe, act, dve, GQA_HEADS // GQA_KV)
                self.merge = Stage(k, 0, [f"tr{n}" for n in range(6)], [f"hi{n}" for n in range(8)],
                                   ["y0"] + [s for n in range(8) for s in [f"y{n + 1}"] * (n < 7) + [f"lo{n}"]])
                self.out = Stage(k, 2, (), (), ("x0", "x1") if self.last else ("x0", "c0", "x1", "c1"), KT // 2)

            def parts_of(self, t):
                return [(0, T, t % 2)] + ([(T, TC, 2 + t % 2)] if not self.last or WIN2[t] in ("mkv", "kr", "gk", "gv") else [])

            def tokens(self, t):
                return sum(n for _, n, _ in self.parts_of(t))

            NORMED = (("mq", (0, 1)), ("mkv", (2,)), ("gk", (4,)), ("gq0", (6,)), ("gq1", (7,)), ("gq2", (8,)))

            def win_plan(self):
                return {2: ["sum mq"], 3: ["sum mkv"], 5: ["sum gk"], 6: ["gv tokens", "swap gk"], 7: ["sum gq0"],
                        8: ["swap gq0", "sum gq1"], 9: ["swap gq1", "sum gq2"], 11: ["swap gq2"]}

            def win_steps(self):
                pe = [s for t in range(len(WIN2)) for s in self.win_plan().get(t, ())]
                act, dve = [], ["pads"]
                norm_of = {ts[-1]: name for name, ts in self.NORMED}
                for t, tile in enumerate(WIN2):
                    act += [f"copy{t}"] + ([f"sq{t}"] if tile not in ("kr", "gv", "ca0", "cg0", "ca1", "cg1") else [])
                    for s in self.win_plan().get(t, ()):
                        kind, name = s.split(" ")
                        if kind == "sum":
                            act += [f"sd {name}"]
                            dve += [f"ri {name}"]
                            if name == "mq":
                                dve += ["f mq0", "f mq1", "lo mq"]
                                act += ["hi mq"]
                            else:
                                dve += [f"f {name}"] + (["lo mkv"] if name == "mkv" else [])
                                act += ["hi mkv"] if name == "mkv" else []
                        elif kind == "swap":
                            dve += [f"{n} {name}" for n in ("cos", "sin", "rope")]
                            act += [f"ctx {name}"] if name == "gk" or not self.last else []
                        else:
                            dve += ["gv tokens"]
                    if tile == "kr":
                        dve += ["kr sin", "kr cos", "kr rope", "kr ctx"]
                    if tile in ("cg0", "cg1"):
                        dve += [tile]
                return pe, act, dve

            def small_steps(self):
                heads = range(MLA_HEADS)
                pe = ["mean", "q0", "q1", "var"] + [f"q{h}" for h in heads[2:]] + [f"kn{h}" for h in heads] + [f"v{b}" for b in range(KB)] + ["pw0", "pw1"]
                act = ["sq", "sd", "silu0", "silu1", "hi"] + [f"kn{h}" for h in heads] + [f"v{b}" for b in range(KB)] + ["pw0", "pw1"]
                dve = ["dev"] + [f"q{h}" for h in heads[:4]] + ["ri", "normed"] + [f"q{h}" for h in heads[4:]] + [f"kr{h}" for h in heads] + ["lo"]
                return pe, act, dve

            def units(self):
                return [(kind, a, qb) for kind in ("mla", "gqa") for a in range(2) for qb in range(BLOCKS if self.last else KB)]

            def heads_steps(self):
                n = len(self.units())
                pe, act, dve = ["sc0"], [], ["q", "mx0", "nm0"]
                for u in range(n):
                    if u:
                        dve += [f"ri{u - 1}"]
                    if u + 1 < n:
                        pe, dve = pe + [f"sc{u + 1}"], dve + [f"mx{u + 1}", f"nm{u + 1}"]
                    act += [f"ex{u}"]
                    if u:
                        pe += [f"pv{u - 1}"]
                    pe += [f"tr{u}"]
                    act += [f"pt{u}"]
                    dve += [f"pt{u}"]
                    if u:
                        dve += [f"o{u - 1}"]
                return pe + [f"pv{n - 1}"], act, dve + [f"ri{n - 1}", f"o{n - 1}"]

        sa = Area(0)
        H2HI, H2LO = sa("H2HI", [P, KT, TT], F32R), sa("H2LO", [P, KT, TT], F32R)
        after_h2 = sa.at
        KAG, VAG = sa("KAG", [P, TT]), sa("VAG", [P, KB, GQA_KV, HD])
        QAG = sa("QAG", [P, GQA_HEADS // GQA_KV, TT])
        gates_at = sa.at
        GATES = sa("GATES", [P, Y_TILES, TT])
        CW = HALO + T + HALO + TC + HALO
        SPAN = T + HALO + TC
        cin_at = sa.at
        CIN = sa("CIN", [P, 2, CW + 3])
        cacc_at = sa.at
        CACC = sa("CACC", [P, 2, SPAN + 1])
        ranks_at = sa.at
        CQHI, CQLO = sa("CQHI", [P, 2, TT], F32R), sa("CQLO", [P, 2, TT], F32R)
        CKHI, CKLO = sa("CKHI", [P, TT], F32R), sa("CKLO", [P, TT], F32R)
        KR = sa("KR", [P, TT])
        work_at = sa.at
        RW, SQ2, RN = sa("RW", [P, 4, TT]), sa("SQ2", [P, 2, TT]), sa("RN", [P, 2, TT])
        assert sa.at <= xc_at - 4 * T, (sa.at, xc_at)
        sn = Area(gates_at)
        SQ4B, HFB, STDB, RSTDB = sn("SQ4B", [P, 4, T]), sn("HFB", [P, 4, T]), sn("STDB", [P, 2, T]), sn("RSTDB", [P, 2, T])
        assert sn.at <= cin_at
        sh = Area(0)
        KAM, QAM = sh("KAM", [P, MLA_HEADS, TT]), sh("QAM", [P, MLA_HEADS, TT])
        VAM = sh("VAM", [P, KB, MLA_HEADS, HD])
        assert sh.at <= after_h2
        CHI2, CLO2 = place("CHI2", [P, 2, TT], work_at + 8 * TT, F32R), place("CLO2", [P, 2, TT], cin_at, F32R)
        YC = place("YC", [P, 2, TT], cacc_at)
        sw = Area(work_at)
        PX, PTS, QST = sw("PX", [P, 2, TT]), sw("PTS", [P, 2, TT]), sw("QST", [P, 3, TT])
        assert sw.at <= sa.at
        OT = place("OT", [P, KB, MLA_HEADS + GQA_HEADS, HD], ranks_at)
        assert ranks_at + 4 * KB * (MLA_HEADS + GQA_HEADS) * HD <= work_at
        YHI, YLO = place("YHI", [P, Y_TILES, TT], 0, F32R), place("YLO", [P, Y_TILES, TT], 4 * Y_TILES * TT, F32R)
        YF = place("YF", [P, 2, TT], work_at)

        def gain_vector(dve, L):
            st = L.gain
            st.enter(dve, "dve")
            for c in range(2):
                at = L.l * MOD_TILES + KT
                ins = dve.scalar_tensor_tensor(out=MG[:, :, c:c + 1], in0=MOD[:, at:at + KT, c:c + 1], scalar=1.0,
                                               in1=VEC[:, COL[f"norm{L.l}"]:COL[f"norm{L.l}"] + KT].rearrange("p (t o) -> p t o", o=1),
                                               op0=ALU.add, op1=ALU.mult)
            ins.then_inc(*st.dve.inc("gain"))
            dve.wait_ge(*st.dve.at("gain"))

        NORM_AT = {name: n for n, (name, _) in enumerate(Layer.NORMED)}
        SQ_SLOT = {0: 0, 1: 1, 2: 0, 4: 1, 6: 0, 7: 1, 8: 0}

        def win_tensor(pe, L):
            st = L.win
            A, V, S = st.act, st.dve, st.pe
            pe.wait_ge(*L.norm.st.dve.at(f"lo0_{KT - 1}"))
            for t in range(len(WIN2)):
                if t >= 2:
                    pe.wait_ge(*A.at(f"copy{t - 2}"))
                    if f"sq{t - 2}" in A.index:
                        pe.wait_ge(*A.at(f"sq{t - 2}"))
                block_ready(pe, st.b0 + t)
                for at, n, b in L.parts_of(t):
                    if at:
                        pe.wait_ge(*L.norm.st.dve.at(f"lo1_{KT - 1}"))
                    mm = product(pe, bank[b][:, 0:n], (st.b0 + t) % 2, ALLK, lambda u: H2HI[:, u, at:at + n],
                                 lambda u: H2LO[:, u, at:at + n], WHOLE)
                mm.then_inc(k.blocks_used, 1)
                for s in L.win_plan().get(t, ()):
                    kind, name = s.split(" ")
                    if kind == "sum":
                        i = NORM_AT[name]
                        tiles_of = Layer.NORMED[i][1]
                        if i:
                            pe.wait_ge(*A.at(f"sd {Layer.NORMED[i - 1][0]}"))
                        pe.wait_ge(*A.at(f"sq{tiles_of[-1]}"))
                        for at, n, b in L.parts_of(tiles_of[0]):
                            for m, tt in enumerate(tiles_of):
                                mm = pe.matmul(bank[4 + b // 2][:, 0:n], ones if name in ("mq", "mkv") else heads,
                                               SQ2[:, SQ_SLOT[tt], at:at + n], start=m == 0, stop=m == len(tiles_of) - 1)
                    elif kind == "swap":
                        tile = Layer.NORMED[NORM_AT[name]][1][0]
                        pe.wait_ge(*V.at(f"f {name}"))
                        pe.wait_ge(*V.at("gv tokens" if name == "gk" else f"sin {Layer.NORMED[NORM_AT[name] - 1][0]}"))
                        mm = pe.matmul(bank[6], TRIG[:, SC["swap"]:SC["swap"] + P], RW[:, tile % 4, 0:T], start=True, stop=True)
                    else:
                        pe.wait_ge(*A.at("copy5"))
                        for b in range(KB):
                            mm = pe.transpose(two_banks[3][:, b * P:(b + 1) * P], RW[:, 5 % 4, b * P:(b + 1) * P], eye)
                    mm.then_inc(*S.inc(s))

        RW_LAST = {0: ("dve", "lo mq"), 1: ("dve", "lo mq"), 2: ("dve", "lo mkv"), 3: ("dve", "kr ctx"), 4: ("act", "ctx gk"),
                   5: ("pe", "gv tokens"), 6: ("dve", "rope gq0"), 7: ("dve", "rope gq1"), 8: ("dve", "rope gq2")}

        def win_scalar(act, L):
            st = L.win
            A, V, S = st.act, st.dve, st.pe
            st.enter(act, "act")
            for t, tile in enumerate(WIN2):
                block_out(act, st.b0 + t)
                round_block(act, st.b0 + t + 2)
                if t >= 4:
                    eng, name = RW_LAST[t - 4]
                    act.wait_ge(*{"dve": V, "pe": S, "act": A}[eng].at(name))
                    if t - 4 in (6, 7, 8) and not L.last:
                        act.wait_ge(*A.at(f"ctx {WIN2[t - 4]}"))
                    if t - 4 == 4:
                        act.wait_ge(*V.at("rope gk"))
                for at, n, b in L.parts_of(t):
                    ins = act.activation(RW[:, t % 4, at:at + n], bank[b][:, 0:n], ACT.Sigmoid if tile in ("cg0", "cg1") else ACT.Copy)
                ins.then_inc(*A.inc(f"copy{t}"))
                if t in SQ_SLOT:
                    before = [u for u in range(t) if SQ_SLOT.get(u) == SQ_SLOT[t]]
                    if before:
                        name = [nm for nm, ts in Layer.NORMED if before[-1] in ts][0]
                        act.wait_ge(*S.at(f"sum {name}"))
                    for at, n, b in L.parts_of(t):
                        ins = act.activation(SQ2[:, SQ_SLOT[t], at:at + n], bank[b][:, 0:n], ACT.Square)
                    ins.then_inc(*A.inc(f"sq{t}"))
                for s in L.win_plan().get(t, ()):
                    kind, name = s.split(" ")
                    if kind == "sum":
                        i = NORM_AT[name]
                        t0 = Layer.NORMED[i][1][0]
                        act.wait_ge(*S.at(s))
                        if i >= 2:
                            prev = Layer.NORMED[i - 2][0]
                            act.wait_ge(*V.at(f"rope {prev}" if prev[0] == "g" else f"lo {prev}"))
                        size = {"mq": MLA_Q_RANK, "mkv": MLA_KV_RANK}.get(name, HD)
                        for at, n, b in L.parts_of(t0):
                            ins = act.activation(RN[:, i % 2, at:at + n], bank[4 + b // 2][:, 0:n], ACT.Sqrt, scale=1.0 / size, bias=EPS[:, 0:1])
                        ins.then_inc(*A.inc(f"sd {name}"))
                        w = L.tokens(t0)
                        if name == "mq":
                            act.wait_ge(*V.at("f mq1"))
                            act.activation(CQHI[:, :, 0:w], RW[:, 0:2, 0:w], ACT.Copy).then_inc(*A.inc("hi mq"))
                        if name == "mkv":
                            act.wait_ge(*V.at("f mkv"))
                            act.activation(CKHI[:, 0:w], RW[:, 2, 0:w], ACT.Copy).then_inc(*A.inc("hi mkv"))
                    elif kind == "swap" and (name == "gk" or not L.last):
                        tile_at = Layer.NORMED[NORM_AT[name]][1][0]
                        act.wait_ge(*V.at(f"f {name}"))
                        dst = KAG[:, T:] if name == "gk" else QAG[:, int(name[2]), T:]
                        act.activation(dst, RW[:, tile_at % 4, T:], ACT.Copy).then_inc(*A.inc(f"ctx {name}"))

        def win_vector(dve, L):
            st = L.win
            A, V, S = st.act, st.dve, st.pe
            l = L.l
            st.enter(dve, "dve")
            if L.l == 0:
                dve.wait_ge(trig_in, 16)
                dve.wait_ge(sin_in, 16)
            dve.memset(CIN[:, :, :], 0.0).then_inc(*V.inc("pads"))
            for t, tile in enumerate(WIN2):
                for s in L.win_plan().get(t, ()):
                    kind, name = s.split(" ")
                    if kind == "tokens" or s == "gv tokens":
                        dve.wait_ge(*S.at(s))
                        dve.tensor_copy(VAG[:, :, :, :].rearrange("p b g n -> p (b g n)"), two_banks[3][:, 0:TT]).then_inc(*V.inc(s))
                        continue
                    i = NORM_AT[name]
                    tiles_of = Layer.NORMED[i][1]
                    w = L.tokens(tiles_of[0])
                    rn = RN[:, i % 2, :]
                    if kind == "sum":
                        dve.wait_ge(*A.at(f"sd {name}"))
                        dve.reciprocal(rn[:, 0:w], rn[:, 0:w]).then_inc(*V.inc(f"ri {name}"))
                        dve.wait_ge(*V.at(f"ri {name}"))
                        for m, tt in enumerate(tiles_of):
                            rw = RW[:, tt % 4, 0:w]
                            gain = col(f"mla_q{l}", m) if name == "mq" else col(f"mla_kv{l}") if name == "mkv" else col(f"gqa_{name[1]}{l}")
                            dve.scalar_tensor_tensor(out=rw, in0=rw, scalar=gain, in1=rn[:, 0:w], op0=ALU.mult, op1=ALU.mult)\
                               .then_inc(*V.inc(f"f mq{m}" if name == "mq" else f"f {name}"))
                        if name in ("mq", "mkv"):
                            src, hi, lo = ((RW[:, 0:2, 0:w], CQHI[:, :, 0:w], CQLO[:, :, 0:w]) if name == "mq" else
                                           (RW[:, 2, 0:w], CKHI[:, 0:w], CKLO[:, 0:w]))
                            dve.wait_ge(*A.at(f"hi {name}"))
                            dve.tensor_tensor(lo, src, hi.bitcast(F32), ALU.subtract).then_inc(*V.inc(f"lo {name}"))
                    else:
                        rw = RW[:, tiles_of[0] % 4, 0:T]
                        dst = KAG[:, 0:T] if name == "gk" else QAG[:, int(name[2]), 0:T]
                        dve.wait_ge(*V.at(f"f {name}"))
                        dve.tensor_tensor(dst, rw, TRIG[:, SC["cos"]:SC["cos"] + T], ALU.mult).then_inc(*V.inc(f"cos {name}"))
                        dve.wait_ge(*S.at(s))
                        dve.tensor_tensor(rn[:, 0:T], bank[6], SIN[:, :], ALU.mult).then_inc(*V.inc(f"sin {name}"))
                        dve.wait_ge(*V.at(f"sin {name}"))
                        dve.tensor_tensor(dst, dst, rn[:, 0:T], ALU.add).then_inc(*V.inc(f"rope {name}"))
                if tile == "kr":
                    lo, up = slice(0, HD), slice(HD, P)
                    trig_of = lambda s: TRIG[s, SC["kr"]:SC["kr"] + T]
                    dve.wait_ge(*A.at(f"copy{t}"))
                    dve.tensor_tensor(KR[up, 0:T], RW[lo, t % 4, 0:T], trig_of(lo), ALU.mult).then_inc(*V.inc("kr sin"))
                    dve.tensor_tensor(RW[up, t % 4, 0:T], RW[up, t % 4, 0:T], trig_of(up), ALU.mult).then_inc(*V.inc("kr cos"))
                    dve.wait_ge(*V.at("kr cos"))
                    dve.tensor_tensor(KR[up, 0:T], KR[up, 0:T], RW[up, t % 4, 0:T], ALU.add).then_inc(*V.inc("kr rope"))
                    dve.tensor_copy(KR[up, T:], RW[up, t % 4, T:]).then_inc(*V.inc("kr ctx"))
                if tile in ("cg0", "cg1"):
                    dve.wait_ge(*A.at(f"copy{t}"))
                    dve.wait_ge(*V.at("pads"))
                    for at, n, _ in L.parts_of(t):
                        to = HALO + at + (HALO if at else 0)
                        ins = dve.tensor_tensor(CIN[:, int(tile[2]), to:to + n], RW[:, (t - 1) % 4, at:at + n], RW[:, t % 4, at:at + n], ALU.mult)
                    ins.then_inc(*V.inc(tile))

        def gate_tensor(pe, L):
            st = L.gate
            st.enter(pe, "pe")
            with pe.Fori(0, GATE2_BLOCKS // 2) as i:
                for n in range(2):
                    pe.wait_ge(*st.act.before(f"gate{n}", i))
                    block_ready(pe, st.b0 + n, i, 2)
                    for at, w in L.parts:
                        mm = product(pe, bank[n + (2 if at else 0)][:, 0:w], (st.b0 + n) % 2, ALLK, lambda u: H2HI[:, u, at:at + w],
                                     lambda u: H2LO[:, u, at:at + w], WHOLE)
                    mm.then_inc(k.blocks_used, 1)

        def gate_scalar(act, L):
            st = L.gate
            st.enter(act, "act")
            with act.Fori(0, GATE2_BLOCKS // 2) as i:
                for n in range(2):
                    block_out(act, st.b0 + n, i, 2)
                    round_block(act, st.b0 + n + 2, i, 2)
                    for at, w in L.parts:
                        ins = act.activation(GATES[:, i * 2 + n, at:at + w], bank[n + (2 if at else 0)][:, 0:w], ACT.Silu)
                    ins.then_inc(*st.act.inc(f"gate{n}"))

        def taps_vector(dve, L):
            l, V = L.l, L.taps.dve
            span = T if L.last else SPAN
            dve.wait_ge(*L.win.dve.at("cg1"))
            for i in range(2):
                dve.tensor_scalar(CACC[:, i, 0:span], CIN[:, i, 0:span], col(f"dw_w{l}", i * CONV_K), None, ALU.mult)\
                   .then_inc(*V.inc(f"first{i}"))
            for i in range(2):
                dve.wait_ge(*V.at(f"first{i}"))
                dve.tensor_scalar(CACC[:, i, 0:span], CACC[:, i, 0:span], col(f"dw_b{l}", i), None, ALU.add).then_inc(*V.inc(f"bias{i}"))
            V = L.tap.dve
            with dve.Fori(0, CONV_K - 1) as s:
                for i in range(2):
                    dve.wait_ge(*V.before(f"tap{i}", s))
                    dve.scalar_tensor_tensor(out=CACC[:, i, 0:span], in0=CIN[:, i, bass.ds(s + 1, span)],
                                             scalar=col(f"dw_w{l}", s + (i * CONV_K + 1)), in1=CACC[:, i, 0:span],
                                             op0=ALU.mult, op1=ALU.add).then_inc(*V.inc(f"tap{i}"))

        def conv_parts(L):
            return [(0, T, 0)] if L.last else [(0, T, 0), (T, TC, T + HALO)]

        def small_tensor(pe, L):
            st = L.small
            A, V, S = st.act, st.dve, st.pe
            st.enter(pe, "pe")
            done = -1
            def ready(idx):
                nonlocal done
                b = idx // UNITS
                if b != done:
                    block_ready(pe, st.b0 + b)
                    done = b
                return (st.b0 + b) % 2
            def used(mm, idx, name):
                mm.then_inc(*S.inc(name))
                if idx % UNITS == UNITS - 1 or idx == V0 + 2:
                    pe.wait_ge(*S.at(name))
                    pe.sem_inc(k.blocks_used)
            parts = [(at, w) for at, w in L.parts]
            cp = conv_parts(L)
            def conv_sum(name, src, b0):
                for m, (at, n, place_at) in enumerate(cp):
                    for i in range(2):
                        mm = pe.matmul(bank[b0 + m][:, 0:n], ones, src[:, i, (place_at if name == "mean" else at):][:, 0:n],
                                       start=i == 0, stop=i == 1)
                mm.then_inc(*S.inc(name))
            conv_sum("mean", CACC, 4)
            for h in range(MLA_HEADS):
                if h == 2:
                    pe.wait_ge(*A.at("sq"))
                    conv_sum("var", SQ2, 6)
                idx = UQ0 + 2 * h
                slot = ready(idx)
                if h >= 2:
                    pe.wait_ge(*V.at(f"q{h - 2}"))
                for at, w in parts:
                    mm = product(pe, bank[h % 2 + (2 if at else 0)][:, 0:w], slot, [(idx % UNITS + t, t) for t in range(2)],
                                 lambda t: CQHI[:, t, at:at + w], lambda t: CQLO[:, t, at:at + w], WHOLE)
                used(mm, idx + 1, f"q{h}")
            for h in range(MLA_HEADS):
                idx = KN0 + h
                slot = ready(idx)
                pe.wait_ge(*(A.at(f"kn{h - 2}") if h >= 2 else A.at("sd")))
                for at, w in ((0, T), (T, TC)):
                    mm = product(pe, bank[4 + h % 2 + (2 if at else 0)][:, 0:w], slot, [(idx % UNITS, 0)],
                                 lambda t: CKHI[:, at:at + w], lambda t: CKLO[:, at:at + w], WHOLE)
                used(mm, idx, f"kn{h}")
            slot = ready(V0)
            u0 = V0 % UNITS
            nv = MLA_HEADS * MLA_V
            for b in range(KB):
                pe.wait_ge(*(V.at(f"q{4 + b}") if b < 2 else A.at(f"v{b - 2}")))
                out = bank[b % 2][:, 0:nv]
                toks = slice(b * P, (b + 1) * P)
                pe.matmul(out, CKHI[:, toks], WHI[:, slot, u0 * P:u0 * P + nv], start=True, stop=False)
                pe.matmul(out, CKLO[:, toks], WHI[:, slot, u0 * P:u0 * P + nv], start=False, stop=False)
                mm = pe.matmul(out, CKHI[:, toks], WLO[:, slot, u0 * P:u0 * P + nv], start=False, stop=True)
                if b < KB - 1:
                    mm.then_inc(*S.inc(f"v{b}"))
                else:
                    used(mm, V0 + 2, f"v{b}")
            slot = ready(PW0)
            pe.wait_ge(*A.at(f"v{KB - 1}"))
            pe.wait_ge(*V.at("lo"))
            for i in range(2):
                for m, (at, n, _) in enumerate(cp):
                    mm = product(pe, bank[i + 2 * m][:, 0:n], slot, [(2 * i + t, t) for t in range(2)],
                                 lambda t: CHI2[:, t, at:at + n], lambda t: CLO2[:, t, at:at + n], WHOLE)
                mm.then_inc(*S.inc(f"pw{i}"))
            pe.wait_ge(*S.at("pw1"))
            pe.sem_inc(k.blocks_used)

        def small_scalar(act, L):
            st = L.small
            A, V, S = st.act, st.dve, st.pe
            l = L.l
            st.enter(act, "act")
            cp = conv_parts(L)
            act.wait_ge(*V.at("dev"))
            for at, n, place_at in cp:
                ins = act.activation(SQ2[:, :, at:at + n], CACC[:, :, place_at:place_at + n], ACT.Square)
            ins.then_inc(*A.inc("sq"))
            act.wait_ge(*S.at("var"))
            for m, (at, n, _) in enumerate(cp):
                ins = act.activation(RN[:, 0, at:at + n], bank[6 + m][:, 0:n], ACT.Sqrt, scale=1.0 / CONV_CH, bias=EPS[:, 0:1])
            ins.then_inc(*A.inc("sd"))
            round_block(act, st.b0 + 2)
            act.wait_ge(*V.at("normed"))
            for i in range(2):
                for at, n, place_at in cp:
                    ins = act.activation(RW[:, i, at:at + n], CACC[:, i, place_at:place_at + n], ACT.Silu,
                                         scale=col(f"cln_w{l}", i), bias=col(f"cln_b{l}", i))
                ins.then_inc(*A.inc(f"silu{i}"))
            act.wait_ge(*A.at("silu1"))
            act.activation(CHI2[:, :, 0:L.width], RW[:, 0:2, 0:L.width], ACT.Copy).then_inc(*A.inc("hi"))
            for h in range(MLA_HEADS):
                act.wait_ge(*S.at(f"kn{h}"))
                if h == KN0 + MLA_HEADS - 1 - KN0:
                    round_block(act, st.b0 + 3)
                for at, w, b in ((0, T, 4), (T, TC, 6)):
                    ins = act.activation(KAM[0:MLA_NOPE, h, at:at + w], bank[b + h % 2][0:MLA_NOPE, 0:w], ACT.Copy)
                ins.then_inc(*A.inc(f"kn{h}"))
            nv = MLA_HEADS * MLA_V
            for b in range(KB):
                act.wait_ge(*S.at(f"v{b}"))
                act.activation(VAM[:, b, :, :].rearrange("p h n -> p (h n)"), bank[b % 2][:, 0:nv], ACT.Copy).then_inc(*A.inc(f"v{b}"))
            round_block(act, st.b0 + 4)
            for i in range(2):
                act.wait_ge(*S.at(f"pw{i}"))
                for m, (at, n, _) in enumerate(cp):
                    ins = act.activation(YC[:, i, at:at + n], bank[i + 2 * m][:, 0:n], ACT.Identity, bias=col(f"pw_b{l}", i))
                ins.then_inc(*A.inc(f"pw{i}"))
            round_block(act, st.b0 + 5)

        def small_vector(dve, L):
            st = L.small
            A, V, S = st.act, st.dve, st.pe
            st.enter(dve, "dve")
            up = slice(MLA_NOPE, P)
            def query(h):
                dve.wait_ge(*S.at(f"q{h}"))
                for at, w in L.parts:
                    ins = dve.tensor_tensor(QAM[:, h, at:at + w], bank[h % 2 + (2 if at else 0)][:, 0:w],
                                            TRIG[:, SC["mla"] + at:SC["mla"] + at + w], ALU.mult)
                ins.then_inc(*V.inc(f"q{h}"))
            cp = conv_parts(L)
            two = lambda t: t.rearrange("p (o n) -> p o n", o=1).to_broadcast([P, 2, t.shape[1]])
            dve.wait_ge(*S.at("mean"))
            for m, (at, n, place_at) in enumerate(cp):
                c = CACC[:, :, place_at:place_at + n]
                ins = dve.scalar_tensor_tensor(out=c, in0=two(bank[4 + m][:, 0:n]), scalar=-1.0 / CONV_CH, in1=c, op0=ALU.mult, op1=ALU.add)
            ins.then_inc(*V.inc("dev"))
            for h in range(4):
                query(h)
            dve.wait_ge(*A.at("sd"))
            dve.reciprocal(RN[:, 0, 0:L.width], RN[:, 0, 0:L.width]).then_inc(*V.inc("ri"))
            dve.wait_ge(*V.at("ri"))
            for m, (at, n, place_at) in enumerate(cp):
                c = CACC[:, :, place_at:place_at + n]
                ins = dve.tensor_tensor(c, c, two(RN[:, 0, at:at + n]), ALU.mult)
            ins.then_inc(*V.inc("normed"))
            for h in range(4, MLA_HEADS):
                query(h)
            for h in range(MLA_HEADS):
                dve.tensor_copy(KAM[up, h, :], KR[up, :]).then_inc(*V.inc(f"kr{h}"))
            dve.wait_ge(*A.at("hi"))
            dve.tensor_tensor(CLO2[:, :, 0:L.width], RW[:, 0:2, 0:L.width], CHI2[:, :, 0:L.width].bitcast(F32), ALU.subtract)\
               .then_inc(*V.inc("lo"))

        def keys_of(qb):
            return range(KB) if qb < BLOCKS else range(BLOCKS, KB)

        def scale_of(kind):
            return (MLA_NOPE + MLA_ROPE if kind == "mla" else HD) ** -0.5

        def heads_tensor(pe, L):
            st = L.heads
            A, V, S = st.act, st.dve, st.pe
            us = L.units()
            st.enter(pe, "pe")
            with pe.Fori(0, st.times) as i:
                def scores(u):
                    kind, a, qb = us[u]
                    pe.wait_ge(*(V.at("q", i) if u < 2 else A.at(f"ex{u - 2}", i)))
                    pe.sem_inc(tensor_ready)
                    for at, w in ((0, T), (T, TC)):
                        if qb >= BLOCKS and not at:
                            continue
                        hs = slice(a * HD, a * HD + HD)
                        lhs, rhs = ((QST[:, a, qb * P:(qb + 1) * P], KAM[:, i * 2 + a, at:at + w]) if kind == "mla" else
                                    (QST[hs, 2, qb * P:(qb + 1) * P], KAG[hs, at:at + w]))
                        mm = pe.matmul(two_banks[u % 2][:, at:at + w], lhs, rhs, start=True, stop=True)
                    mm.then_inc(*S.inc(f"sc{u}"))
                def values(u):
                    kind, a, qb = us[u]
                    pe.wait_ge(*V.at(f"pt{u}", i))
                    pe.wait_ge(*A.at(f"pt{u}", i))
                    pe.sem_inc(tensor_ready)
                    ks = keys_of(qb)
                    for b in ks:
                        rhs = VAM[:, b, i * 2 + a, :] if kind == "mla" else VAG[:, b, a, :]
                        mm = pe.matmul(two_banks[2 + u % 2][:, TT:TT + HD], PTS[:, u % 2, b * P:(b + 1) * P], rhs,
                                       start=b == ks[0], stop=b == ks[-1])
                    mm.then_inc(*S.inc(f"pv{u}"))
                scores(0)
                for u, (kind, a, qb) in enumerate(us):
                    if u + 1 < len(us):
                        scores(u + 1)
                    if u:
                        values(u - 1)
                    pe.wait_ge(*A.at(f"ex{u}", i))
                    if u >= 2:
                        pe.wait_ge(*V.at(f"o{u - 2}", i))
                    pe.sem_inc(tensor_ready)
                    for b in keys_of(qb):
                        mm = pe.transpose(two_banks[2 + u % 2][:, b * P:(b + 1) * P], PX[:, u % 2, b * P:(b + 1) * P], eye)
                    mm.then_inc(*S.inc(f"tr{u}"))
                values(len(us) - 1)

        def heads_scalar(act, L):
            st = L.heads
            A, V, S = st.act, st.dve, st.pe
            us = L.units()
            st.enter(act, "act")
            with act.Fori(0, st.times) as i:
                for u, (kind, a, qb) in enumerate(us):
                    c0 = 0 if qb < BLOCKS else T
                    act.wait_ge(*V.at(f"nm{u}", i))
                    if u >= 2:
                        act.wait_ge(*S.at(f"tr{u - 2}", i))
                    act.activation(PX[:, u % 2, c0:], two_banks[u % 2][:, c0:TT], ACT.Exp, scale=scale_of(kind), bias=NM2[:, u:u + 1],
                                   accum_out=DEN2[:, u:u + 1]).then_inc(*A.inc(f"ex{u}"))
                    act.wait_ge(*S.at(f"tr{u}", i))
                    if u >= 2:
                        act.wait_ge(*S.at(f"pv{u - 2}", i))
                    if qb < BLOCKS:
                        act.activation(PTS[:, u % 2, 0:T], two_banks[2 + u % 2][:, 0:T], ACT.Copy).then_inc(*A.inc(f"pt{u}"))
                    else:
                        act.sem_inc(A.inc(f"pt{u}")[0])

        def heads_vector(dve, L):
            st = L.heads
            A, V, S = st.act, st.dve, st.pe
            us = L.units()
            st.enter(dve, "dve")
            with dve.Fori(0, st.times) as i:
                dve.wait_ge(*S.before(f"sc{len(us) - 1}", i))
                dve.tensor_copy(QST[:, 0:2, 0:L.width], QAM[:, bass.ds(i * 2, 2), 0:L.width])
                dve.tensor_copy(QST[:, 2, 0:L.width], QAG[:, i, 0:L.width]).then_inc(*V.inc("q"))
                def largest(u):
                    kind, a, qb = us[u]
                    dve.wait_ge(*S.at(f"sc{u}", i))
                    dve.tensor_reduce(MX2[:, u:u + 1], two_banks[u % 2][:, (0 if qb < BLOCKS else T):TT], AX, ALU.max).then_inc(*V.inc(f"mx{u}"))
                    dve.wait_ge(*V.at(f"mx{u}", i))
                    dve.tensor_scalar(NM2[:, u:u + 1], MX2[:, u:u + 1], -scale_of(kind), None, ALU.mult).then_inc(*V.inc(f"nm{u}"))
                def inverse(u):
                    dve.wait_ge(*A.at(f"ex{u}", i))
                    dve.reciprocal(DEN2[:, u:u + 1], DEN2[:, u:u + 1]).then_inc(*V.inc(f"ri{u}"))
                def result(u):
                    kind, a, qb = us[u]
                    head = a + i * 2 + (MLA_HEADS if kind == "gqa" else 0)
                    dve.wait_ge(*V.at(f"ri{u}", i))
                    dve.wait_ge(*S.at(f"pv{u}", i))
                    dve.tensor_scalar(OT[:, qb, head, :], two_banks[2 + u % 2][:, TT:TT + HD], DEN2[:, u:u + 1], None, ALU.mult)\
                       .then_inc(*V.inc(f"o{u}"))
                largest(0)
                for u in range(len(us)):
                    if u:
                        inverse(u - 1)
                    if u + 1 < len(us):
                        largest(u + 1)
                    dve.wait_ge(*S.at(f"tr{u}", i))
                    dve.tensor_copy(PTS[:, u % 2, T:], two_banks[2 + u % 2][:, T:TT]).then_inc(*V.inc(f"pt{u}"))
                    if u:
                        result(u - 1)
                inverse(len(us) - 1)
                result(len(us) - 1)

        def gated_tensor(pe, L):
            st = L.merge
            st.enter(pe, "pe")
            for n in range(6):
                if n >= 2:
                    pe.wait_ge(*st.dve.at(f"y{n - 2}"))
                for b in range(L.width // P):
                    mm = pe.transpose(two_banks[n % 2][:, b * P:(b + 1) * P], OT[:, b, 2 * n:2 * n + 2, :].rearrange("p h n -> p (h n)"), eye)
                mm.then_inc(*st.pe.inc(f"tr{n}"))

        def gated_scalar(act, L):
            st = L.merge
            st.enter(act, "act")
            for n in range(Y_TILES):
                act.wait_ge(*st.dve.at(f"y{n}"))
                act.activation(YHI[:, n, 0:L.width], YF[:, n % 2, 0:L.width], ACT.Copy).then_inc(*st.act.inc(f"hi{n}"))

        def gated_vector(dve, L):
            st = L.merge
            st.enter(dve, "dve")
            w = L.width
            def gated(n):
                if n < 6:
                    dve.wait_ge(*st.pe.at(f"tr{n}"))
                if n >= 2:
                    dve.wait_ge(*st.dve.at(f"lo{n - 2}"))
                dve.tensor_tensor(YF[:, n % 2, 0:w], two_banks[n % 2][:, 0:w] if n < 6 else YC[:, n - 6, 0:w], GATES[:, n, 0:w], ALU.mult)\
                   .then_inc(*st.dve.inc(f"y{n}"))
            gated(0)
            for n in range(Y_TILES):
                if n + 1 < Y_TILES:
                    gated(n + 1)
                dve.wait_ge(*st.act.at(f"hi{n}"))
                dve.tensor_tensor(YLO[:, n, 0:w], YF[:, n % 2, 0:w], YHI[:, n, 0:w].bitcast(F32), ALU.subtract).then_inc(*st.dve.inc(f"lo{n}"))

        def out2_tensor(pe, L):
            st = L.out
            st.enter(pe, "pe")
            with pe.Fori(0, KT // 2) as i:
                for n in range(2):
                    pe.wait_ge(*st.dve.before(f"x{n}" if L.last else f"c{n}", i))
                    block_ready(pe, st.b0 + n, i, 2)
                    for at, w in L.parts:
                        mm = product(pe, bank[4 + n + (2 if at else 0)][:, 0:w], (st.b0 + n) % 2, ALLK, lambda u: YHI[:, u, at:at + w],
                                     lambda u: YLO[:, u, at:at + w], WHOLE)
                    mm.then_inc(k.blocks_used, 1)

        def out2_scalar(act, L):
            st = L.out
            full = KT // 2 - (1 if L.last else 0)
            with act.Fori(0, full) as i:
                for n in range(2):
                    round_block(act, st.b0 + n + 2, i, 2)
            if L.last:
                round_block(act, st.b0 + KT)

        def out2_vector(dve, L):
            st = L.out
            st.enter(dve, "dve")
            with dve.Fori(0, KT // 2) as i:
                for n in range(2):
                    block_out(dve, st.b0 + n, i, 2)
                    for c, (at, w) in enumerate(L.parts):
                        x = (XC if c else X)[:, i * 2 + n, :]
                        dve.scalar_tensor_tensor(out=x, in0=bank[4 + n + 2 * c][:, 0:w],
                                                 scalar=MOD[:, i * 2 + (L.l * MOD_TILES + 2 * KT + n), c:c + 1], in1=x,
                                                 op0=ALU.mult, op1=ALU.add).then_inc(*st.dve.inc(f"{'xc'[c]}{n}"))

        OUT = place("OUT", [P, KT, T], 0)
        SQF, RF = place("SQF", [P, 4, T], after_h2), place("RF", [P, 2, T], after_h2 + 16 * T)

        def final_tensor(pe, st):
            st.enter(pe, "pe")
            for t in range(KT):
                pe.wait_ge(*st.act.at(f"sq{t}"))
                pe.matmul(bank[0], ones, SQF[:, t % 4, :], start=t == 0, stop=t == KT - 1).then_inc(*st.pe.inc(f"sum{t}"))

        def final_scalar(act, st):
            st.enter(act, "act")
            for t in range(KT):
                if t >= 4:
                    act.wait_ge(*st.pe.at(f"sum{t - 4}"))
                act.activation(SQF[:, t % 4, :], X[:, t, :], ACT.Square).then_inc(*st.act.inc(f"sq{t}"))
            act.wait_ge(*st.pe.at(f"sum{KT - 1}"))
            act.activation(RF[:, 0, :], bank[0], ACT.Sqrt, scale=1.0 / D, bias=EPS[:, 0:1]).then_inc(*st.act.inc("sd"))

        def final_vector(dve, st):
            st.enter(dve, "dve")
            dve.wait_ge(*st.act.at("sd"))
            dve.reciprocal(RF[:, 1, :], RF[:, 0, :]).then_inc(*st.dve.inc("ri"))
            dve.wait_ge(*st.dve.at("ri"))
            for t in range(KT):
                dve.scalar_tensor_tensor(out=OUT[:, t, :], in0=X[:, t, :], scalar=col("final_norm", t), in1=RF[:, 1, :],
                                         op0=ALU.mult, op1=ALU.mult).then_inc(*st.dve.inc(f"out{t}"))

        cond = Stage(k, 0, (), ("silu", "hi"), ("lo",))
        ffn1 = FFN("ffn1_norm")
        mix = plain_norm("mix_norm")
        lora_st = Stage(k, PRO_BLOCKS, (), [f"pb{c}" for c in range(LORA_BLOCKS + 1)] + ["tanh", "sig"] + [f"pb{c}" for c in range(LORA_BLOCKS + 1, PRO_BLOCKS)],
                        ("zero", "ka1", "d0", "o0", "d1", "o1", "d2", "o2"))
        pairs_st = Stage(k, LOOP_BLOCKS, rw_pe, rw_act, rw_dve, PAIRS // 2)
        att_in = Stage(k, ATT_BLOCKS, ain_pe, ain_act, ain_dve)
        att = Stage(k, 0, att_pe, att_act, att_dve)
        merge = Stage(k, 4, (), ("gate0", "gate1", "hi"), ("mul0", "mul1", "sum", "lo"), KT)
        way_out = Stage(k, 2, (), (), ("x0", "x1"), KT // 2)
        ffn2 = FFN("ffn2_norm")
        layers = []
        for l in range(LAYERS):
            layers.append(Layer(l))
        final = Stage(k, 0, [f"sum{t}" for t in range(KT)], [f"sq{t}" for t in range(KT)] + ["sd"], ["ri"] + [f"out{t}" for t in range(KT)])
        k.planned = k.blocks

        block = ctx.enter_context(nc.Block())

        @block.sync
        def _(sp):
            sp.dma_start(VEC[:, :], vec).then_inc(vec_in, 16)
            sp.dma_start(X[:, 0:4, :], xT[:, 0:4, :]).then_inc(x_in[0], 16)
            sp.dma_start(X[:, 4:8, :], xT[:, 4:8, :]).then_inc(x_in[1], 16)
            sp.dma_start(SQC[:, :], square).then_inc(const_in, 16)
            for s in range(2):
                sp.dma_start(RAW[:, s, :], wstream[s]).then_inc(raw_full[s], 16)
            sp.dma_start(FCC[:, :], first).then_inc(first_in, 16)
            sp.dma_start(LVL[:, :, :], levels.rearrange("p (l c) -> p l c", c=CHUNK)).then_inc(levels_in, 16)
            with sp.Fori(1, nblocks // 2) as i:
                for s in range(2):
                    sp.wait_ge(split, i * 2 + (s - 1))
                    sp.dma_start(RAW[:, s, :], wstream[i * 2 + s]).then_inc(raw_full[s], 16)
            for z in range(4):
                sp.wait_ge(*final.dve.at(f"out{2 * z + 1}"))
                sp.dma_start(outT[:, 2 * z:2 * z + 2, :], OUT[:, 2 * z:2 * z + 2, :]).then_inc(out_done, 16)
            sp.wait_ge(out_done, 4 * 16)

        @block.gpsimd
        def _(pool):
            pool.memset(EPS[:, 0:1], RMS_EPS).then_inc(filled, 1)
            pool.memset(EPS[:, 1:2], GN_EPS).then_inc(filled, 1)
            for s in range(2):
                pool.wait_ge(rounded, s + 1)
                pool.tensor_tensor(WLO[:, s, :], RAW[:, s, :], WHI[:, s, :].bitcast(F32), ALU.subtract).then_inc(split, 1)
            with pool.Fori(1, nblocks // 2) as i:
                for s in range(2):
                    pool.wait_ge(rounded, i * 2 + (s + 1))
                    pool.tensor_tensor(WLO[:, s, :], RAW[:, s, :], WHI[:, s, :].bitcast(F32), ALU.subtract)\
                        .then_inc(split, 1)

        @block.tensor
        def _(pe):
            pe.wait_ge(const_in, 16)
            pe.wait_ge(first_in, 16)
            ffn_tensor(pe, ffn1)
            norm_tensor(pe, mix)
            lora_tensor(pe, lora_st)
            rwkv_tensor(pe, pairs_st)
            attention_in_tensor(pe, att_in)
            attention_tensor(pe, att)
            merge_tensor(pe, merge)
            out_tensor(pe, way_out)
            ffn_tensor(pe, ffn2)
            pe.wait_ge(trig_in, 16)
            for L in layers:
                norm_tensor(pe, L.norm)
                win_tensor(pe, L)
                gate_tensor(pe, L)
                small_tensor(pe, L)
                heads_tensor(pe, L)
                gated_tensor(pe, L)
                out2_tensor(pe, L)
            final_tensor(pe, final)

        @block.scalar
        def _(act):
            act.wait_ge(vec_in, 16)
            act.wait_ge(filled, 2)
            c2 = VEC[:, COL["cond"]:COL["cond"] + 2 * KT].rearrange("p (t c) -> p t c", c=2)
            act.activation(CS[:, :, :], c2, ACT.Silu).then_inc(*cond.act.inc("silu"))
            act.wait_ge(*cond.act.at("silu"))
            act.activation(CHL[:, :, 0:2], CS[:, :, :], ACT.Copy).then_inc(*cond.act.inc("hi"))
            round_block(act, 0)
            round_block(act, 1)
            act.wait_ge(x_in[0], 16)
            act.wait_ge(x_in[1], 16)
            ffn_scalar(act, ffn1)
            norm_scalar(act, mix)
            lora_scalar(act, lora_st)
            rwkv_scalar(act, pairs_st)
            attention_in_scalar(act, att_in)
            attention_scalar(act, att)
            merge_scalar(act, merge)
            out_scalar(act, way_out)
            ffn_scalar(act, ffn2)
            act.wait_ge(ctx_in, 16)
            for L in layers:
                norm_scalar(act, L.norm)
                win_scalar(act, L)
                gate_scalar(act, L)
                small_scalar(act, L)
                heads_scalar(act, L)
                gated_scalar(act, L)
                out2_scalar(act, L)
            final_scalar(act, final)

        @block.vector
        def _(dve):
            dve.wait_ge(vec_in, 16)
            dve.wait_ge(x_in[0], 16)
            dve.wait_ge(x_in[1], 16)
            dve.wait_ge(*cond.act.at("hi"))
            dve.tensor_tensor(CHL[:, :, 2:4], CS[:, :, :], CHL[:, :, 0:2].bitcast(F32), ALU.subtract).then_inc(*cond.dve.inc("lo"))
            dve.wait_ge(first_in, 16)
            dve.wait_ge(levels_in, 16)
            ffn_vector(dve, ffn1)
            norm_vector(dve, mix)
            lora_vector(dve, lora_st)
            rwkv_vector(dve, pairs_st)
            attention_in_vector(dve, att_in)
            attention_vector(dve, att)
            merge_vector(dve, merge)
            out_vector(dve, way_out)
            ffn_vector(dve, ffn2)
            dve.wait_ge(ctx_in, 16)
            for L in layers:
                gain_vector(dve, L)
                norm_vector(dve, L.norm)
                win_vector(dve, L)
                taps_vector(dve, L)
                small_vector(dve, L)
                heads_vector(dve, L)
                gated_vector(dve, L)
                out2_vector(dve, L)
            final_vector(dve, final)

        return k




def tiles(w):
    kt, nt = -(-w.shape[0] // P), -(-w.shape[1] // P)
    full = np.zeros((kt * P, nt * P), w.dtype)
    full[:w.shape[0], :w.shape[1]] = w
    return full.reshape(kt, P, nt, P).transpose(0, 2, 1, 3)


def blocks_of(w):
    t = tiles(w)
    out = []
    for n in range(t.shape[1]):
        for m in range(0, t.shape[0], UNITS):
            b = np.zeros((UNITS, P, P), w.dtype)
            b[:min(UNITS, t.shape[0] - m)] = t[m:m + UNITS, n]
            out.append(b)
    return out


def columns_of(v):
    v = v.reshape(-1)
    full = np.zeros(-(-v.size // P) * P, v.dtype)
    full[:v.size] = v
    return full.reshape(-1, P).T


def moving_blocks(w):
    n = w.shape[1] // (2 * P)
    w = w.reshape(2, KT // 2, P, n, 2, P).transpose(3, 0, 1, 4, 2, 5)
    return list(w.reshape(2 * n, UNITS, P, P))


def stream(a):
    def ffn(n):
        w = a[f"ffn{n}_w_in"][0]
        gate, up, down = blocks_of(w[:, :D_FF]), blocks_of(w[:, D_FF:]), blocks_of(a[f"ffn{n}_w_out"][0])
        out = [b for pair in zip(gate, up) for b in pair]
        return out + down
    out = ffn(1)
    w = a["w_in"][0]
    cuts = np.cumsum([0, D, D, D, W_LORA + A_LORA, G_LORA, AT_WIDTH, AT_WIDTH, AT_WIDTH, D, D])
    r, kx, v, wa, g, aq, ak, av, ga, gb = (blocks_of(w[:, cuts[i]:cuts[i + 1]]) for i in range(10))
    out += wa + g
    mods = [moving_blocks(a["w_mod_2"][l]) for l in range(LAYERS)]
    per = 2 * MOD_TILES // PAIRS
    two = [[t for j in (n, n + 1) for t in (r[j], kx[j], v[j])] for n in range(0, PAIRS, 2)]
    two.append([t for c in range(2) for t in (aq[c], ak[c], av[c])])
    out += two[0]
    for n in range(PAIRS // 2):
        kinds = {"M": iter([t for m in mods for t in m[n * per:(n + 1) * per]]), "S": iter(two[n + 1])}
        out += [next(kinds[kind]) for kind in ROUND_ORDER]
    for c in range(2, AT_TILES):
        out += [aq[c], ak[c], av[c]]
    pa, pb = blocks_of(a["w_proj_rwkv"][0]), blocks_of(a["w_proj_attn"][0])
    for n in range(KT):
        out += [ga[n], gb[n], pa[n], pb[n]]
    out += blocks_of(a["w_out"][0])
    out += ffn(2)
    for l in range(LAYERS):
        out += second_layer(a, l)
    return out


GQA_ORDER = [h for j in range(GQA_HEADS // GQA_KV) for h in (j, GQA_HEADS // GQA_KV + j)]


def in_tiles(parts):
    out = []
    for m in range(0, len(parts), UNITS):
        b = np.zeros((UNITS, P, P), parts[0].dtype)
        for u, part in enumerate(parts[m:m + UNITS]):
            b[u, :part.shape[0], :part.shape[1]] = part
        out.append(b)
    return out


def second_layer(a, l):
    w = a["w_in_2"][l]
    cut = np.cumsum([0, MLA_Q_RANK, MLA_KV_RANK, MLA_ROPE, GQA_KV * HD, GQA_KV * HD, GQA_HEADS * HD, 2 * CONV_CH, D])
    mq, mkv, kr, gk, gv, gq, conv, gate = (w[:, cut[i]:cut[i + 1]] for i in range(8))
    partner = rope_tables(MLA_ROPE)[2]
    kr = np.concatenate([kr[:, partner]] * 2 + [kr] * 2, 1)
    def heads_in_order(m, axis):
        return np.concatenate([np.take(m, range(h * HD, (h + 1) * HD), axis) for h in GQA_ORDER], axis)
    g0, g1 = MLA_HEADS * MLA_V, MLA_HEADS * MLA_V + GQA_HEADS * HD
    gate = np.concatenate([gate[:, :g0], heads_in_order(gate[:, g0:g1], 1), gate[:, g1:]], 1)
    a0, a1, c0, c1 = (conv[:, i * P:(i + 1) * P] for i in range(4))
    out = []
    for m in (mq, mkv, kr, gk, gv, heads_in_order(gq, 1), a0, c0, a1, c1):
        out += blocks_of(m)
    uq = a["mla_w_uq_2"][l].reshape(MLA_Q_RANK, MLA_HEADS, MLA_NOPE + MLA_ROPE)
    uq = np.concatenate([uq, uq[:, :, MLA_NOPE:][:, :, partner]], 2)
    ukv = a["mla_w_ukv_2"][l].reshape(MLA_KV_RANK, MLA_HEADS, MLA_NOPE + MLA_V)
    small = [uq[t * P:(t + 1) * P, h] for h in range(MLA_HEADS) for t in range(2)]
    small += [ukv[:, h, :MLA_NOPE] for h in range(MLA_HEADS)]
    v = ukv[:, :, MLA_NOPE:].reshape(MLA_KV_RANK, MLA_HEADS * MLA_V)
    small += [v[:, i * P:(i + 1) * P] for i in range(3)]
    pw = a["conv_pw_w_2"][l]
    small += [np.zeros((P, P), pw.dtype)] * (PW0 - len(small))
    small += [pw[t * P:(t + 1) * P, n * P:(n + 1) * P] for n in range(2) for t in range(2)]
    out += blocks_of(gate) + in_tiles(small)
    wo = a["w_out_2"][l]
    wo = np.concatenate([wo[:g0], heads_in_order(wo[g0:g1], 0), wo[g1:]], 0)
    return out + blocks_of(wo)


def vectors(a):
    out = np.zeros((P, COL["total"]), np.float32)
    def put(name, v):
        c = columns_of(v)
        out[:, COL[name]:COL[name] + c.shape[1]] = c
    for n in ("ffn1_norm", "mix_norm", "ffn2_norm", "b_gate"):
        put(n, a[n])
    mu = a["rwkv_mu"][0]
    put("mu_lora", mu[3 * D:])
    put("mu_rkv", mu[:3 * D].reshape(3, PAIRS, P).transpose(1, 0, 2))
    for n in ("w0", "a0", "k_k", "k_a", "r_k", "ln_w", "ln_b"):
        put(n, a[f"rwkv_{n}"])
    put("q_norm", np.concatenate([a["attn_q_norm"][0]] * 2))
    put("k_norm", np.concatenate([a["attn_k_norm"][0]] * 2))
    put("final_norm", a["final_norm_w_2"])
    cond = np.stack([columns_of(a["c_2"]), columns_of(a["c_ctx_2"])], 2)
    out[:, COL["cond"]:COL["cond"] + 2 * KT] = cond.reshape(P, 2 * KT)
    for l in range(LAYERS):
        put(f"norm{l}", a["norm_w_2"][l])
        put(f"b_mod{l}", a["b_mod_2"][l])
        put(f"mla_q{l}", a["mla_q_norm_2"][l])
        put(f"mla_kv{l}", a["mla_kv_norm_2"][l])
        put(f"gqa_q{l}", np.concatenate([a["gqa_q_norm_2"][l]] * 2))
        put(f"gqa_k{l}", np.concatenate([a["gqa_k_norm_2"][l]] * 2))
        put(f"dw_w{l}", a["conv_dw_w_2"][l].reshape(CONV_K, 2, P).transpose(1, 0, 2))
        put(f"dw_b{l}", a["conv_dw_b_2"][l])
        put(f"cln_w{l}", a["conv_ln_w_2"][l])
        put(f"cln_b{l}", a["conv_ln_b_2"][l])
        put(f"pw_b{l}", a["conv_pw_b_2"][l])
    return out


def low_ranks(a):
    out = np.zeros((P, PAIRS + 2, 3, P), np.float32)
    out[:W_LORA, :PAIRS, 0] = a["rwkv_w2"][0].reshape(W_LORA, PAIRS, P)
    out[W_LORA:, :PAIRS, 0] = a["rwkv_a2"][0].reshape(A_LORA, PAIRS, P)
    g = a["rwkv_g2"][0].reshape(G_LORA, PAIRS, P)
    out[:, :PAIRS, 1] = g[:P]
    out[:G_LORA - P, :PAIRS, 2] = g[P:]
    return out.reshape(P, PAIRS + 2, 3 * P)


def channel_major(x):
    return np.ascontiguousarray(x.reshape(x.shape[0], KT, P).transpose(2, 1, 0))


def even(w):
    return np.concatenate([w, np.zeros_like(w[:len(w) % 2])])


def layout(a):
    square, first, levels, second = constant_arrays()
    return {
        "xT": channel_major(a["x"][0]), "ctxT": channel_major(a["ctx_2"][0]), "vec": vectors(a), "square": square,
        "first": first, "levels": levels, "trig": second, "lora": low_ranks(a),
        "wstream": even(np.stack([b.transpose(1, 0, 2).reshape(P, UNITS * P) for b in stream(a)])),
    }


def kernel(**inputs):
    import concourse.bacc as bacc
    from concourse.bass_utils import run_bass_kernel_spmd

    arrays = layout({name: np.asarray(v) for name, v in inputs.items()})
    nc = bacc.Bacc("TRN2", target_bir_lowering=False, num_devices=1)
    ins = [nc.dram_tensor(f"in_{name}", v.shape, mybir.dt.from_np(v.dtype), kind="ExternalInput").ap() for name, v in arrays.items()]
    out = nc.dram_tensor("out_T", (P, KT, T), F32, kind="ExternalOutput").ap()
    block_kernel(nc, *ins, out)
    r = run_bass_kernel_spmd(nc, [{f"in_{name}": v for name, v in arrays.items()}], core_ids=[0])
    return np.ascontiguousarray(r.results[0]["out_T"].transpose(2, 1, 0)).reshape(1, T, D)
```
